# Optimizing a Trainium2 kernel written in Bass

```python
import math
import jax, jax.numpy as jnp
from jax import lax
import numpy as np

D_MODEL = 1024
BATCH = 1
SEQ = 512
DEPTH = 2

N_MIXERS = 2
N_FOX = (DEPTH + 1) // 2
N_MLA = DEPTH // 2
FOX_HEADS = 16
FOX_HEAD_DIM = D_MODEL // FOX_HEADS
MLA_HEADS = 16
MLA_NOPE_DIM = D_MODEL // MLA_HEADS
MLA_ROPE_DIM = MLA_NOPE_DIM // 2
MLA_V_DIM = D_MODEL // MLA_HEADS
MLA_Q_RANK = D_MODEL // 4
MLA_KV_RANK = D_MODEL // 8
D_FF = 4 * D_MODEL
Q_BLOCK = 128
ROPE_THETA = 10000.0
NORM_EPS = 1e-6
N_MOD = 6

kernel_name = "hybrid_fox_mla_adaln_trunk"

def rms_norm(x, g):
    x32 = x.astype(jnp.float32)
    y = x32 * lax.rsqrt(jnp.mean(x32 * x32, axis=-1, keepdims=True) + NORM_EPS)
    return y.astype(x.dtype) * g

def causal_block_attention(logits_fn, v):
    S = v.shape[1]
    outs = []
    for qb in range(S // Q_BLOCK):
        q0, q1 = qb * Q_BLOCK, (qb + 1) * Q_BLOCK
        logits = logits_fn(q0, q1)
        allowed = jnp.arange(q1)[None, :] <= jnp.arange(q0, q1)[:, None]
        logits = jnp.where(allowed, logits, -jnp.inf)
        p = jax.nn.softmax(logits, axis=-1).astype(v.dtype)
        outs.append(jnp.einsum('bhqk,bkhd->bqhd', p, v[:, :q1]))
    return jnp.concatenate(outs, axis=1)

def rope_cos_sin(positions, dim):
    inv_freq = ROPE_THETA ** (-jnp.arange(0, dim, 2, dtype=jnp.float32) / dim)
    ang = positions.astype(jnp.float32)[..., None] * inv_freq
    return jnp.cos(ang), jnp.sin(ang)

def apply_rope(x, cos, sin):
    half = x.shape[-1] // 2
    x1, x2 = x[..., :half], x[..., half:]
    cos = cos.astype(x.dtype)
    sin = sin.astype(x.dtype)
    return jnp.concatenate([x1 * cos - x2 * sin, x2 * cos + x1 * sin], axis=-1)

def fox_mixer(h, w_in, b_f, w_out):
    B, S, _ = h.shape
    proj = h @ w_in
    q = proj[..., :D_MODEL].reshape(B, S, FOX_HEADS, FOX_HEAD_DIM)
    k = proj[..., D_MODEL:2 * D_MODEL].reshape(B, S, FOX_HEADS, FOX_HEAD_DIM)
    v = proj[..., 2 * D_MODEL:3 * D_MODEL].reshape(B, S, FOX_HEADS, FOX_HEAD_DIM)
    log_f = jax.nn.log_sigmoid((proj[..., 3 * D_MODEL:] + b_f).astype(jnp.float32))
    F = jnp.cumsum(log_f, axis=1).transpose(0, 2, 1)
    scale = FOX_HEAD_DIM ** -0.5

    def logits_fn(q0, q1):
        s = jnp.einsum('bqhd,bkhd->bhqk', q[:, q0:q1], k[:, :q1],
                       preferred_element_type=jnp.float32)
        return s * scale + (F[:, :, q0:q1, None] - F[:, :, None, :q1])

    o = causal_block_attention(logits_fn, v)
    return o.reshape(B, S, D_MODEL) @ w_out

def mla_mixer(h, cos, sin, w_dq, q_norm_g, w_uq, w_dkv, kv_norm_g, w_ukv, w_out):
    B, S, _ = h.shape
    cq = rms_norm(h @ w_dq, q_norm_g)
    q = (cq @ w_uq).reshape(B, S, MLA_HEADS, MLA_NOPE_DIM + MLA_ROPE_DIM)
    q_nope = q[..., :MLA_NOPE_DIM]
    q_rope = apply_rope(q[..., MLA_NOPE_DIM:], cos[:, :, None, :], sin[:, :, None, :])
    dkv = h @ w_dkv
    ckv = rms_norm(dkv[..., :MLA_KV_RANK], kv_norm_g)
    k_rope = apply_rope(dkv[..., MLA_KV_RANK:], cos, sin)
    kv = (ckv @ w_ukv).reshape(B, S, MLA_HEADS, MLA_NOPE_DIM + MLA_V_DIM)
    k_nope = kv[..., :MLA_NOPE_DIM]
    v = kv[..., MLA_NOPE_DIM:]
    scale = (MLA_NOPE_DIM + MLA_ROPE_DIM) ** -0.5

    def logits_fn(q0, q1):
        s = jnp.einsum('bqhd,bkhd->bhqk', q_nope[:, q0:q1], k_nope[:, :q1],
                       preferred_element_type=jnp.float32)
        s = s + jnp.einsum('bqhd,bkd->bhqk', q_rope[:, q0:q1], k_rope[:, :q1],
                           preferred_element_type=jnp.float32)
        return s * scale

    o = causal_block_attention(logits_fn, v)
    return o.reshape(B, S, MLA_HEADS * MLA_V_DIM) @ w_out

def sq_relu_mlp(h, w1, w2):
    a = jax.nn.relu(h @ w1)
    return (a * a) @ w2

def setup_inputs(seed: int = 0) -> dict:
    key = jax.random.key(seed)
    ks = iter(jax.random.split(key, 32))
    D = D_MODEL

    def nrm(shape, fan_in, mult=1.0):
        return jax.random.normal(next(ks), shape, jnp.float32) * (mult * fan_in ** -0.5)

    def gain(shape):
        return 1.0 + 0.02 * jax.random.normal(next(ks), shape, jnp.float32)

    x = jax.random.normal(next(ks), (BATCH, SEQ, D), jnp.float32)
    c = jax.random.normal(next(ks), (BATCH, D), jnp.float32)
    offs = jax.random.randint(next(ks), (BATCH, 1), 0, 4096, dtype=jnp.int32)
    positions = (jnp.arange(SEQ, dtype=jnp.int32)[None, :] + offs).astype(jnp.int32)
    return {
        "x": x,
        "c": c,
        "positions": positions,
        "ada_w": nrm((DEPTH, D, N_MOD * D), D),
        "ada_b": 0.02 * jax.random.normal(next(ks), (DEPTH, N_MOD * D), jnp.float32),
        "norm_mix_g": gain((DEPTH, D)),
        "norm_mlp_g": gain((DEPTH, D)),
        "fox_w_in": nrm((N_FOX, D, 3 * D + FOX_HEADS), D),
        "fox_b_f": jax.random.uniform(next(ks), (N_FOX, FOX_HEADS), jnp.float32, 2.0, 6.0),
        "fox_w_out": nrm((N_FOX, D, D), D),
        "mla_w_dq": nrm((N_MLA, D, MLA_Q_RANK), D),
        "mla_q_norm_g": gain((N_MLA, MLA_Q_RANK)),
        "mla_w_uq": nrm((N_MLA, MLA_Q_RANK, MLA_HEADS * (MLA_NOPE_DIM + MLA_ROPE_DIM)), MLA_Q_RANK),
        "mla_w_dkv": nrm((N_MLA, D, MLA_KV_RANK + MLA_ROPE_DIM), D),
        "mla_kv_norm_g": gain((N_MLA, MLA_KV_RANK)),
        "mla_w_ukv": nrm((N_MLA, MLA_KV_RANK, MLA_HEADS * (MLA_NOPE_DIM + MLA_V_DIM)), MLA_KV_RANK),
        "mla_w_out": nrm((N_MLA, MLA_HEADS * MLA_V_DIM, D), MLA_HEADS * MLA_V_DIM),
        "mlp_w1": nrm((DEPTH, D, D_FF), D),
        "mlp_w2": nrm((DEPTH, D_FF, D), D_FF),
        "final_norm_g": gain((D,)),
    }

def reference(x, c, positions, ada_w, ada_b, norm_mix_g, norm_mlp_g,
              fox_w_in, fox_b_f, fox_w_out,
              mla_w_dq, mla_q_norm_g, mla_w_uq, mla_w_dkv, mla_kv_norm_g, mla_w_ukv, mla_w_out,
              mlp_w1, mlp_w2, final_norm_g):
    cos, sin = rope_cos_sin(positions, MLA_ROPE_DIM)
    c_act = jax.nn.silu(c)
    for i in range(DEPTH):
        mod = (c_act @ ada_w[i] + ada_b[i])[:, None, :]
        sh_m, sc_m, g_m, sh_f, sc_f, g_f = jnp.split(mod, N_MOD, axis=-1)
        h = rms_norm(x, norm_mix_g[i]) * (1 + sc_m) + sh_m
        j = i // N_MIXERS
        if i % N_MIXERS == 0:
            y = fox_mixer(h, fox_w_in[j], fox_b_f[j], fox_w_out[j])
        else:
            y = mla_mixer(h, cos, sin, mla_w_dq[j], mla_q_norm_g[j], mla_w_uq[j],
                          mla_w_dkv[j], mla_kv_norm_g[j], mla_w_ukv[j], mla_w_out[j])
        x = x + g_m * y
        h = rms_norm(x, norm_mlp_g[i]) * (1 + sc_f) + sh_f
        x = x + g_f * sq_relu_mlp(h, mlp_w1[i], mlp_w2[i])
    return rms_norm(x, final_norm_g)


_drawn_inputs = setup_inputs


def setup_inputs(seed=0):
    import zlib

    import numpy as np

    out = dict(_drawn_inputs(seed))
    spreads = {}
    factors = {'norm_mix_g': 5.379,
     'norm_mlp_g': 2.74,
     'mla_q_norm_g': 8.0,
     'mla_kv_norm_g': 8.0,
     'final_norm_g': 2.887}
    for name, (base, spread) in spreads.items():
        noise = np.random.default_rng([zlib.crc32(name.encode()), seed]).standard_normal(out[name].shape)
        drawn = base * np.exp(spread * noise) if base else spread * noise
        out[name] = __import__('jax').numpy.asarray(drawn.astype(out[name].dtype))
    for name, factor in factors.items():
        out[name] = (out[name] * factor).astype(out[name].dtype)
    return out
```

```python
import math
from contextlib import ExitStack

import concourse.bass as bass
from concourse import mybir

F32 = mybir.dt.float32
F32R = mybir.dt.float32r
BF16 = mybir.dt.bfloat16
I32 = mybir.dt.int32
ALU = mybir.AluOpType
ACT = mybir.ActivationFunctionType
AXX = mybir.AxisListType.X

P = 128
T = 512
D = 1024
C = D // P
TB = T // P
HEADS = 16
HD = D // HEADS
ROPE = HD // 2
PAIRS = HEADS // 2
QR, KVR = D // 4, D // 8
DFF = 4 * D
GROUPS = DFF // (C * P)
UW = 256
UNIT = C * UW
HALF = UNIT // 2
ADA_UNITS = 2 * 6 * D // UW
ADA_START = 8
EPS = 1e-6
NEG = -1e30
INV_2PI = 1 / (2 * math.pi)
ROUND = 1.5 * 2.0 ** 23
TWO_PI_PARTS = (6.28125, 0.0019340515136718750, 1.2556659146e-06)
FOX_SCALE = HD ** -0.5
MLA_SCALE = (HD + ROPE) ** -0.5
MLA_K = HD + ROPE
F_AT = 96
PTS = 384
PTH = PTS * 3 + T

U_V = 0
U_QK = U_V + 4
U_FOUT = U_QK + PAIRS
U_MLP = (U_FOUT + 4, U_FOUT + 4 + 32 + 4 + PAIRS + 4)
U_DKV = U_MLP[0] + 32
U_DQ, U_MV, U_QROPE = U_DKV + 1, U_DKV + 2, U_DKV + 3
U_MQK = U_DKV + 4
U_MOUT = U_MQK + PAIRS
N_UNITS = U_MLP[1] + 32
MQK_W = 3 * P

D_V = 0
D_FOUT = 16
D_MLP = (D_FOUT + C, D_FOUT + C + 64 + 4 + 8 + 4 + C)
D_DKV = D_MLP[0] + 64
D_DQ, D_MV, D_QROPE = D_DKV + 2, D_DKV + 4, D_DKV + 12
D_MOUT = D_DKV + 16
RING = 4

TD_FOUT = 16
TD_MLP = (TD_FOUT + C, TD_FOUT + C + 32 + 16 + C)
TD_DKV = TD_MLP[0] + 32
TD_MOUT = TD_DKV + 16

ADA_ORDER = [(layer, w) for layer in range(2) for w in ("sc_m", "sh_m", "g_m", "sh_f", "sc_f", "g_f")]

CV_C = 0
CV_ADAB = CV_C + C
CV_GMIX = CV_ADAB + 2 * ADA_UNITS
CV_GMLP = CV_GMIX + 2 * C
CV_GFIN = CV_GMLP + 2 * C
CV_GQ = CV_GFIN + C
CV_GKV = CV_GQ + 2
CV_BF = CV_GKV + 1
CV_N = CV_BF + 1
CC_ID = 0
CC_MASK = CC_ID + P
CC_FREQ = CC_MASK + P
CC_EPS = CC_FREQ + 1
CC_SIGN = CC_EPS + 1
CC_N = CC_SIGN + 1


def trunk(nc, xt, pos, cvec, cconst, ada, w_v, w_qk, w_f, w_fout, w_dkv, w_dq, w_mv, w_qrope, w_mqk, w_mout, w_mlp, f_dram, yt):
    ctx = ExitStack()
    with ctx:
        def sb(name, shape, dt):
            return ctx.enter_context(nc.sbuf_tensor(name, shape, dt))

        def sem(name):
            return ctx.enter_context(nc.semaphore(name))

        x = sb("x", [P, C, T], F32)
        h_hi, h_lo = sb("h_hi", [P, C, T], F32R), sb("h_lo", [P, C, T], F32R)
        o_hi, o_lo = sb("o_hi", [P, C, T], F32R), sb("o_lo", [P, C, T], F32R)
        w_raw = sb("w_raw", [P, UNIT], F32)
        w_hi, w_lo = sb("w_hi", [P, 2, UNIT], F32R), sb("w_lo", [P, 2, UNIT], F32R)
        adab = sb("adab", [P, 4, T], F32)
        v_raw = sb("v_raw", [P, 8, T], F32)
        qa, qb, ka, kb = ([sb(f"{n}{s}", [P, T], F32R) for s in range(2)] for n in ("qa", "qb", "ka", "kb"))
        pe_ = sb("probs", [P, 4, T], F32)
        pt_hi = sb("pt_hi", [P, PTH + PTS * 5], F32R)
        pt_lo = sb("pt_lo", [P, PTH + PTS * 5], F32R)
        vs_hi, vs_lo = sb("vs_hi", [P, TB, P], F32R), sb("vs_lo", [P, TB, P], F32R)
        cv = sb("cv", [P, CV_N], F32)
        cc = sb("cc", [P, CC_N], F32)
        ones = sb("ones", [P, P], F32)
        id_b, mask_b = sb("id_b", [P, P], BF16), sb("mask_b", [P, P], BF16)
        cact = sb("cact", [P, C], F32)
        ctmp = sb("ctmp", [P, 3, C], F32)
        mod = sb("mod", [P, 2 * ADA_UNITS], F32)
        acol = sb("acol", [P, C], F32)
        adaacc = sb("adaacc", [P, 2, UW], F32)
        nmax, rsum, rinv = sb("nmax", [P, 2, 2], F32), sb("rsum", [P, 2, 2], F32), sb("rinv", [P, 2, 2], F32)
        f_rows = [kb[part][F_AT:F_AT + HEADS, :] for part in range(2)]
        wf_raw = sb("wf_raw", [P, C * HEADS], F32)
        wf_hi, wf_lo = sb("wf_hi", [P, C, HEADS], F32R), sb("wf_lo", [P, C, HEADS], F32R)

        ps = [ctx.enter_context(nc.psum_tensor(f"ps{i}", [P, T], F32)) for i in range(8)]
        S_BANK = [[ps[0], ps[1]], [ps[2], ps[3]]]
        T_BANK = [ps[4], ps[5]]
        PQ, PK = ps[6], ps[7]

        ident = cc[:, CC_ID:CC_ID + P]
        sc = v_raw
        prob = [[pe_[:, 2 * r + s, :] for s in range(2)] for r in range(2)]
        cos_t, sin_t = adab[:, 0, :], adab[:, 1, :]
        ada_slots = [t.rearrange("p a t -> p (a t)") for t in (adab[:, :, :], v_raw[:, 0:4, :], pe_[:, :, :])]
        v_tok = v_raw[:, :, :].rearrange("p a t -> p (a t)").rearrange("p (b n) -> p b n", b=TB)

        def mcols(layer, what):
            at = C * ADA_ORDER.index((layer, what))
            return mod[:, at:at + C]

        s_cin, s_xin, s_posin, s_fin = sem("const_in"), sem("x_in"), sem("pos_in"), sem("wf_in")
        s_ast = [sem(f"ada_start_in{i}") for i in range(3)]
        s_ain = [sem(f"ada_in{i}") for i in range(2)]
        s_win = [sem(f"w_in{i}") for i in range(2)]
        s_whi, s_wlo = sem("w_hi_done"), sem("w_lo_done")
        s_adastep, s_adamm, s_mod = sem("ada_step"), sem("ada_mm"), sem("mod_done")
        s_ones, s_bf, s_csil, s_cact = sem("ones_set"), sem("bf_consts"), sem("silu_act"), sem("silu_dve")
        s_tile = sem("tile_done")
        s_tact, s_tdve = sem("tile_read_act"), sem("tile_read_dve")
        s_xup, s_sq, s_acc = sem("x_updated"), sem("square_done"), sem("square_summed")
        s_ss, s_ln, s_rstd = sem("sumsq_mm"), sem("ln_done"), sem("rstd_done")
        s_acol, s_tm, s_hhi, s_hlo = sem("acol_done"), sem("xhat_done"), sem("h_hi_done"), sem("h_lo_done")
        s_relu, s_sqr, s_ahi, s_alo = sem("relu_done"), sem("relu_squared"), sem("a_hi_done"), sem("a_lo_done")
        s_wf, s_fmm, s_fa, s_fd, s_fr = sem("wf_split"), sem("f_mm"), sem("f_act"), sem("f_dve"), sem("f_rows")
        s_score, s_max, s_exp, s_rinv, s_norm = sem("scores"), sem("rowmax"), sem("exp"), sem("rinv"), sem("normed")
        s_tr, s_pthi, s_ptlo = sem("transposed"), sem("pt_hi_done"), sem("pt_lo_done")
        s_pq, s_pk, s_qhi, s_qlo, s_khi, s_klo = (sem(n) for n in ("q_mm", "k_mm", "q_hi_done", "q_lo_done", "k_hi_done", "k_lo_done"))
        s_qx, s_kx, s_fx = ([sem(f"{n}{s}") for s in range(2)] for n in ("q_rows_in", "k_rows_in", "f_rows_in"))
        s_vhi, s_vlo, s_pv, s_ohi, s_olo = sem("v_hi_done"), sem("v_lo_done"), sem("pv_mm"), sem("o_hi_done"), sem("o_lo_done")
        s_rope, s_rpa, s_kr, s_lat = sem("rope_dve"), sem("rope_act"), sem("krope_rows"), sem("latent_raw")
        s_trig, s_triga, s_qrd, s_qra = sem("trig_dve"), sem("trig_act"), sem("qrope_dve"), sem("qrope_act")
        s_out = [sem(f"y_out{i}") for i in range(C)]
        s_fdram = sem("f_stored")
        s_zero, s_passed = sem("zero_rows"), sem("pool_waits_passed")
        s_yn = sem("y_done")

        block = ctx.enter_context(nc.Block())

        def pt(s, buf, i, n):
            at = s * PTH + P * i
            return buf[:, at:at + PTS * n].rearrange("p (j c) -> p j c", c=PTS)[:, :, 0:P]


        def after(i, r):
            return (i, 1) if r == 0 else (i + 1, 0)

        @block.sync
        def _(sp):
            def load_w(u, src, n=UNIT, narrow=False):
                for hf in range(2):
                    split = 2 * u if narrow else 2 * u + hf - 1
                    if not (isinstance(u, int) and u == 0):
                        sp.wait_ge(s_whi, split)
                        sp.wait_ge(s_wlo, split)
                    a, b = hf * (n // 2), (hf + 1) * (n // 2)
                    sp.dma_start(w_raw[:, a:b], src[:, a:b]).then_inc(s_win[hf], 16)

            def load_ada(a):
                for hf in range(2):
                    sp.wait_ge(s_adastep, 8 * a + 4 * hf - 4)
                    a0, b0 = hf * HALF, (hf + 1) * HALF
                    sp.dma_start(ada_slots[0][:, a0:b0], ada[a, :, a0:b0]).then_inc(s_ain[hf], 16)

            def operand_rows(layer, i, r):
                gp = PAIRS * layer + 2 * i + r
                sp.wait_ge(s_score, 8 * gp)
                for s in range(2):
                    if layer == 0:
                        sp.dma_start(kb[s][HD:HD + 2, :].bitcast(F32), f_dram[bass.ds(4 * i + (2 * r + s), 1), :, :]).then_inc(s_fx[s], 16)
                    else:
                        at = ROPE * (2 * r + s)
                        for dst, src in ((qa, h_hi), (qb, h_lo)):
                            sp.dma_start(dst[s][HD:MLA_K, :].bitcast(F32), src[at:at + ROPE, bass.ds(2 + i, 1), :].bitcast(F32)).then_inc(s_qx[s], 16)
                if layer == 0:
                    for s in range(2):
                        sp.wait_ge(s_qhi, 2 * gp + s + 1)
                        sp.dma_start(qb[s][0:HD, :].bitcast(F32), qa[s][0:HD, :].bitcast(F32)).then_inc(s_qx[s], 16)
                    for s in range(2):
                        sp.wait_ge(s_khi, 2 * gp + s + 1)
                        sp.dma_start(ka[s][HD:P, :].bitcast(F32), ka[s][0:HD, :].bitcast(F32)).then_inc(s_kx[s], 16)

            sp.dma_start(cv[:], cvec).then_inc(s_cin, 16)
            sp.dma_start(cc[:], cconst).then_inc(s_cin, 16)
            sp.dma_start(ada_slots[0], ada[0, :, :]).then_inc(s_ast[0], 16)
            sp.dma_start(x[:, :, :], xt).then_inc(s_xin, 16)
            for a in range(1, ADA_START):
                if a >= 3:
                    sp.wait_ge(s_adastep, 8 * (a - 2))
                sp.dma_start(ada_slots[a % 3], ada[a, :, :]).then_inc(s_ast[a % 3], 16)
            sp.dma_start(wf_raw[:], w_f).then_inc(s_fin, 16)
            load_w(0, w_v[0])
            for n in range(4):
                load_w(U_V + n + 1, w_v[n + 1] if n < 3 else w_qk[0])
                load_ada(ADA_START + 2 * n)
                load_ada(ADA_START + 2 * n + 1)
            load_w(U_QK + 1, w_qk[1])
            for part in range(2):
                sp.wait_ge(s_fr, part + 1)
                sp.dma_start(f_dram[:, part, :], f_rows[part].bitcast(F32)).then_inc(s_fdram, 16)
            sp.wait_ge(s_fdram, 32)
            operand_rows(0, 0, 0)
            with sp.Fori(0, 3) as i:
                for r in range(2):
                    load_w(U_QK + 2 * i + r + 2, w_qk[2 * i + (r + 2)])
                    load_ada(ADA_START + 8 + 2 * i + r)
                    operand_rows(0, *after(i, r))
            load_w(U_FOUT, w_fout[0])
            load_ada(ADA_START + 14)
            operand_rows(0, 3, 1)
            load_ada(ADA_START + 15)
            for n in range(1, 4):
                load_w(U_FOUT + n, w_fout[n])
            load_w(U_MLP[0], w_mlp[0])

            def mlp_loads(layer, g, last):
                for n in range(8):
                    if not (last and n == 7):
                        load_w(U_MLP[layer] + 8 * g + n + 1, w_mlp[32 * layer + 8 * g + (n + 1)])
                    elif layer == 0:
                        load_w(U_DKV, w_dkv[0], C * 160)
                    if layer == 0 and n < 6:
                        load_ada(24 + 6 * g + n)
                    if layer == 0 and last and n == 5:
                        sp.wait_ge(s_adastep, 8 * ADA_UNITS)
                        sp.dma_start(adab[:, 2, :].bitcast(I32), pos.partition_broadcast(P)).then_inc(s_posin, 16)

            with sp.Fori(0, GROUPS - 1) as g:
                mlp_loads(0, g, False)
            mlp_loads(0, GROUPS - 1, True)
            load_w(U_DQ, w_dq[0], narrow=True)
            load_w(U_MV, w_mv[0], D)
            load_w(U_QROPE, w_qrope[0], 2 * T)
            load_w(U_MQK, w_mqk[0], MQK_W)
            load_w(U_MQK + 1, w_mqk[1], MQK_W)
            sp.wait_ge(s_qrd, TB)
            operand_rows(1, 0, 0)
            with sp.Fori(0, 3) as i:
                for r in range(2):
                    load_w(U_MQK + 2 * i + r + 2, w_mqk[2 * i + (r + 2)], MQK_W)
                    operand_rows(1, *after(i, r))
            operand_rows(1, 3, 1)
            for n in range(4):
                load_w(U_MOUT + n, w_mout[n], narrow=(n == 0))
            load_w(U_MLP[1], w_mlp[32])
            with sp.Fori(0, GROUPS - 1) as g:
                mlp_loads(1, g, False)
            mlp_loads(1, GROUPS - 1, True)
            for c in range(C):
                sp.wait_ge(s_yn, c + 1)
                sp.dma_start(yt[:, c, :], sc[:, c, :]).then_inc(s_out[c], 16)
            for c in range(C):
                sp.wait_ge(s_out[c], 16)


        @block.gpsimd
        def _(pool):
            nc.gpsimd.memset(ones[:], 1.0).then_inc(s_ones, 1)
            for s in range(2):
                pool.wait_ge(s_ones, 1)
                if s:
                    pool.wait_ge(s_zero, 1)
                nc.gpsimd.memset(qb[s][HD:HD + 2, :].bitcast(F32), 1.0).then_inc(s_zero, 1)

            def waits(*pairs):
                for sem, count in pairs:
                    pool.wait_ge(sem, count)
                pool.sem_inc(s_passed, 1)

            def pair_rows(layer, i, r, more, u, n):
                gp = PAIRS * layer + 2 * i + r

                def norm(st):
                    for s in range(2):
                        pr = prob[st % 2][s][:, 0:P * (st + 1)]
                        k = 2 * st + s
                        if st == 0 and s == 0:
                            before = (s_vlo, gp + 1)
                        elif st == 2 and s == 0 and more:
                            before = (s_wlo, 2 * u + 2)
                        else:
                            before = (s_norm, 8 * gp + k)
                        waits((s_rinv, 4 * gp + st + 1), before)
                        nc.gpsimd.tensor_scalar(pr, pr, rinv[:, st % 2, s:s + 1], 1.0, ALU.mult, ALU.mult).then_inc(s_norm, 1)

                waits((s_vhi, gp + 1), (s_norm, 8 * gp))
                nc.gpsimd.tensor_tensor(vs_lo[:], v_tok[:, :, bass.ds(P * (2 * i + r), P)], vs_hi[:].bitcast(F32), ALU.subtract).then_inc(s_vlo, 1)
                norm(0)
                norm(1)
                if more:
                    slot = r
                    for hf in range(2):
                        a, b = hf * (n // 2), (hf + 1) * (n // 2)
                        waits((s_whi, 2 * u + hf + 1), (s_wlo, 2 * u + 1) if hf else (s_norm, 8 * gp + 4))
                        nc.gpsimd.tensor_tensor(w_lo[:, slot, a:b], w_raw[:, a:b], w_hi[:, slot, a:b].bitcast(F32), ALU.subtract).then_inc(s_wlo, 1)
                norm(2)
                norm(3)

            pool.wait_ge(s_zero, 2)
            for layer, u0, n, then in ((0, U_QK, UNIT, U_FOUT), (1, U_MQK, MQK_W, U_MOUT)):
                with pool.Fori(0, 3) as i:
                    for r in range(2):
                        pair_rows(layer, i, r, True, u0 + 2 * i + r + 2, n)
                pair_rows(layer, 3, 0, True, then, UNIT)
                pair_rows(layer, 3, 1, False, None, None)

        @block.scalar
        def _(act):
            def split_hi(u, n=UNIT, used=None):
                if used is not None:
                    act.wait_ge(*used)
                for hf in range(2):
                    a, b = hf * (n // 2), (hf + 1) * (n // 2)
                    act.wait_ge(s_win[hf], 16 * u + 16)
                    nc.scalar.activation(w_hi[:, slot_of[0], a:b], w_raw[:, a:b], ACT.Copy).then_inc(s_whi, 1)
                slot_of[0] ^= 1

            slot_of = [0]

            def rstd(n, out, tmp, width, k):
                act.wait_ge(s_ss, k + 1)
                nc.scalar.activation(tmp, T_BANK[1][:], ACT.Ln, bias=cc[:, CC_EPS:CC_EPS + 1], scale=1.0 / width).then_inc(s_ln, 1)
                act.wait_ge(s_ln, k + 1)
                nc.scalar.activation(out, tmp, ACT.Exp, scale=-0.5).then_inc(s_rstd, 1)

            def squares(n, c):
                if c >= 2:
                    act.wait_ge(s_acc, 7 * n + max(1, c - 2))
                nc.scalar.activation(sc[:, 4 + c % 2, :], x[:, c, :], ACT.Square).then_inc(s_sq, 1)

            def h_chunks(n, layer, what):
                sh = mcols(layer, what)
                for c in range(C):
                    act.wait_ge(s_tm, C * n + c + 1)
                    nc.scalar.activation(h_hi[:, c, :], sc[:, 4 + c % 2, :], ACT.Identity, bias=sh[:, c:c + 1]).then_inc(s_hhi, 1)

            act.wait_ge(s_cin, 32)
            nc.scalar.activation(ctmp[:, 0, :], cv[:, CV_C:CV_C + C], ACT.Exp, scale=-1.0).then_inc(s_csil, 1)
            nc.scalar.activation(id_b[:], ident, ACT.Copy).then_inc(s_bf, 1)
            nc.scalar.activation(mask_b[:], cc[:, CC_MASK:CC_MASK + P], ACT.Copy).then_inc(s_bf, 1)
            act.wait_ge(s_xin, 16)
            for c in range(C):
                squares(0, c)
            act.wait_ge(s_fin, 16)
            nc.scalar.activation(wf_hi[:, :, :].rearrange("p c h -> p (c h)"), wf_raw[:], ACT.Copy).then_inc(s_wf, 1)
            split_hi(0)
            rstd(0, sc[:, 7, :], sc[:, 7, :], D, 0)
            h_chunks(0, 0, "sh_m")
            for n in range(4):
                split_hi(n + 1, used=(s_tile, D_V + 4 * n) if n else None)

            z, za, ze, zl = (pe_[F_AT:F_AT + HEADS, k, :] for k in range(4))
            act.wait_ge(s_fmm, 1)
            nc.scalar.activation(z, T_BANK[0][0:HEADS, :], ACT.Identity, bias=cv[0:HEADS, CV_BF:CV_BF + 1]).then_inc(s_fa, 1)
            act.wait_ge(s_fa, 1)
            nc.scalar.activation(za, z, ACT.Abs).then_inc(s_fa, 1)
            act.wait_ge(s_fa, 2)
            nc.scalar.activation(ze, za, ACT.Exp, scale=-1.0).then_inc(s_fa, 1)
            act.wait_ge(s_fa, 3)
            nc.scalar.activation(zl, ze, ACT.Ln, bias=ones[F_AT:F_AT + HEADS, 0:1]).then_inc(s_fa, 1)
            act.wait_ge(s_fd, 3)
            nc.scalar.activation(f_rows[0], za, ACT.Copy, scale=-1.0).then_inc(s_fr, 1)

            def q_hi(layer, gp, first=False):
                scale = FOX_SCALE if layer == 0 else MLA_SCALE
                act.wait_ge(s_pq, gp + 1)
                if not first:
                    act.wait_ge(s_score, 8 * gp)
                for s in range(2):
                    nc.scalar.activation(qa[s][0:HD, :], PQ[s * HD:(s + 1) * HD, :], ACT.Copy, scale=scale).then_inc(s_qhi, 1)

            def k_hi(layer, gp):
                act.wait_ge(s_pk, gp + 1)
                for s in range(2):
                    nc.scalar.activation(ka[s][0:HD, :], PK[s * HD:(s + 1) * HD, :], ACT.Copy).then_inc(s_khi, 1)

            def exps(gp, st):
                for s in range(2):
                    n = P * (st + 1)
                    act.wait_ge(s_max, 2 * (4 * gp + st) + s + 1)
                    if st >= 2:
                        act.wait_ge(s_tr, 2 * (4 * gp + st) + s - 3)
                    nc.scalar.activation(prob[st % 2][s][:, 0:n], S_BANK[st % 2][s][:, 0:n], ACT.Exp,
                                         bias=nmax[:, st % 2, s:s + 1], accum_out=rsum[:, st % 2, s:s + 1]).then_inc(s_exp, 1)

            def pt_his(gp, st):
                for s in range(2):
                    act.wait_ge(s_tr, 2 * (4 * gp + st) + s + 1)
                    nc.scalar.activation(pt(s, pt_hi, st, st + 1), T_BANK[s][:, 0:P * (st + 1)].rearrange("p (j c) -> p j c", c=P),
                                         ACT.Copy).then_inc(s_pthi, 1)

            def attn(layer, i, r, more, unit):
                gp = PAIRS * layer + 2 * i + r
                act.wait_ge(s_pv, 2 * gp)
                nc.scalar.activation(vs_hi[:], v_tok[:, :, bass.ds(P * (2 * i + r), P)], ACT.Copy).then_inc(s_vhi, 1)
                exps(gp, 0)
                exps(gp, 1)
                if more:
                    split_hi(*unit, used=(s_pk, gp + 1))
                pt_his(gp, 0)
                exps(gp, 2)
                pt_his(gp, 1)
                exps(gp, 3)
                if more:
                    q_hi(layer, gp + 1)
                pt_his(gp, 2)
                pt_his(gp, 3)
                if more:
                    k_hi(layer, gp + 1)
                for s in range(2):
                    act.wait_ge(s_pv, 2 * gp + s + 1)
                    rows = slice(s * HD, (s + 1) * HD)
                    nc.scalar.activation(o_hi[rows, bass.ds(2 * i + r, 1), :].rearrange("p a t -> p (a t)"), S_BANK[1][s][rows, :], ACT.Copy).then_inc(s_ohi, 1)

            def attn_layer(layer, u0, n, then):
                split_hi(u0 + 1, n, used=(s_tile, D_MOUT if layer else D_FOUT))
                q_hi(layer, PAIRS * layer, first=(layer == 0))
                k_hi(layer, PAIRS * layer)
                with act.Fori(0, 3) as i:
                    for r in range(2):
                        attn(layer, i, r, True, (u0 + 2 * i + r + 2, n))
                attn(layer, 3, 0, True, (then, UNIT))
                attn(layer, 3, 1, False, None)

            def out_proj(layer, u0, d, td):
                n = 2 * layer + 1
                for k in range(4):
                    split_hi(u0 + k + 1, used=(s_tile, d + 2 * k) if k else (s_pk, PAIRS * (layer + 1)))
                    for c in (2 * k, 2 * k + 1):
                        act.wait_ge(s_tdve, td + c + 1)
                        squares(n, c)
                rstd(n, sc[:, 7, :], sc[:, 7, :], D, n + 2 * (n > 2))
                h_chunks(n, layer, "sh_f")

            def mlp_group(layer, g, last, after_u):
                base = 32 * layer + 8 * g
                for k in range(8):
                    used = (s_tile, D_MLP[layer] + 16 * g + 2 * k)
                    if not (last and k == 7):
                        split_hi(U_MLP[layer] + 8 * g + k + 1, used=used)
                    elif after_u:
                        split_hi(*after_u, used=used)
                    if layer == 0 and last and k == 7:
                        act.wait_ge(s_trig, 8)
                        nc.scalar.activation(sin_t, adab[:, 2, :], ACT.Sin).then_inc(s_triga, 1)
                        act.wait_ge(s_trig, 12)
                        nc.scalar.activation(cos_t, adab[:, 3, :], ACT.Sin).then_inc(s_triga, 1)
                    for j in (2 * k, 2 * k + 1):
                        if k < 4:
                            act.wait_ge(s_tile, D_MLP[layer] + 16 * g + j + 1)
                            nc.scalar.activation(sc[:, j % 2, :], ps[j % RING][:], ACT.Relu).then_inc(s_tact, 1)
                            act.wait_ge(s_sqr, base + j + 1)
                            nc.scalar.activation(o_hi[:, j, :], sc[:, 2 + j % 2, :], ACT.Copy).then_inc(s_ahi, 1)
                        elif last:
                            c = j - 8
                            act.wait_ge(s_tdve, TD_MLP[layer] + 8 * g + c + 1)
                            squares(2 * layer + 2, c)

            def mlp(layer, after_u):
                with act.Fori(0, GROUPS - 1) as g:
                    mlp_group(layer, g, False, None)
                mlp_group(layer, GROUPS - 1, True, after_u)

            attn_layer(0, U_QK, UNIT, U_FOUT)
            out_proj(0, U_FOUT, D_FOUT, TD_FOUT)
            mlp(0, (U_DKV, C * 160))
            rstd(2, sc[:, 7, :], sc[:, 7, :], D, 2)
            h_chunks(2, 1, "sh_m")
            split_hi(U_DQ, used=(s_tile, D_DKV))
            ckv_raw, cq_raw, cq_n = prob[0][0], (prob[0][1], prob[1][0]), (prob[0][0], prob[1][1])
            act.wait_ge(s_tdve, TD_DKV + 1)
            nc.scalar.activation(sc[:, 4, :], ckv_raw, ACT.Square).then_inc(s_rpa, 1)
            act.wait_ge(s_kr, 3)
            nc.scalar.activation(qa[0][0:ROPE, :], sc[0:ROPE, 1, :], ACT.Copy).then_inc(s_rpa, 1)
            rstd(5, sc[:, 6, :], sc[:, 6, :], KVR, 3)
            split_hi(U_MV, D, used=(s_tile, D_DQ))
            act.wait_ge(s_rope, 1)
            nc.scalar.activation(o_hi[:, 7, :], sc[:, 5, :], ACT.Copy).then_inc(s_rpa, 1)
            act.wait_ge(s_kr, 4)
            for s in range(2):
                nc.scalar.activation(ka[s][HD:MLA_K, :], qa[0][0:ROPE, :].bitcast(F32), ACT.Copy).then_inc(s_rpa, 1)
                nc.scalar.activation(kb[s][HD:MLA_K, :], qa[1][0:ROPE, :].bitcast(F32), ACT.Copy).then_inc(s_rpa, 1)
            for k in range(2):
                act.wait_ge(s_tdve, TD_DKV + 3 + k)
                nc.scalar.activation(adab[:, 2 + k, :], cq_raw[k], ACT.Square).then_inc(s_rpa, 1)
            rstd(6, adab[:, 3, :], adab[:, 3, :], QR, 4)
            for k in range(2):
                act.wait_ge(s_rope, 4 + k)
                nc.scalar.activation(h_hi[:, k, :], cq_n[k], ACT.Copy).then_inc(s_rpa, 1)
            split_hi(U_QROPE, 2 * T, used=(s_tile, D_MV))
            split_hi(U_MQK, MQK_W, used=(s_tile, D_QROPE))
            for k in range(TB):
                act.wait_ge(s_qra, 3 * k + 3)
                nc.scalar.activation(h_hi[:, 2 + k, :], adab[:, 2, :], ACT.Copy, scale=MLA_SCALE).then_inc(s_rpa, 1)
            attn_layer(1, U_MQK, MQK_W, U_MOUT)
            out_proj(1, U_MOUT, D_MOUT, TD_MOUT)
            mlp(1, None)
            rstd(4, prob[0][0], prob[0][0], D, 6)

        @block.vector
        def _(dve):
            slot_of = [0]

            def split_lo(u, n=UNIT):
                for hf in range(2):
                    a, b = hf * (n // 2), (hf + 1) * (n // 2)
                    dve.wait_ge(s_whi, 2 * u + hf + 1)
                    nc.vector.tensor_tensor(w_lo[:, slot_of[0], a:b], w_raw[:, a:b], w_hi[:, slot_of[0], a:b].bitcast(F32),
                                            ALU.subtract).then_inc(s_wlo, 1)
                slot_of[0] ^= 1

            def ada_sum(a, par, k0=0, k1=C):
                start = isinstance(a, int) and a < ADA_START
                buf = ada_slots[a % 3 if start else 0]
                if k0 == 0 and not (isinstance(a, int) and a < 2):
                    dve.wait_ge(s_adamm, a - 1)
                for k in range(k0, k1):
                    if start:
                        dve.wait_ge(s_ast[a % 3], 16 * (a // 3 + 1))
                    elif k % 4 == 0:
                        dve.wait_ge(s_ain[k // 4], 16 * (a - ADA_START + 1))
                    w = buf[:, k * UW:(k + 1) * UW]
                    if k == 0:
                        nc.vector.tensor_scalar(adaacc[:, par, :], w, cact[:, 0:1], None, ALU.mult).then_inc(s_adastep, 1)
                    else:
                        dve.wait_ge(s_adastep, 8 * a + k)
                        nc.vector.scalar_tensor_tensor(out=adaacc[:, par, :], in0=w, scalar=cact[:, k:k + 1], in1=adaacc[:, par, :],
                                                       op0=ALU.mult, op1=ALU.add).then_inc(s_adastep, 1)

            def ada_add(a):
                dve.wait_ge(s_adamm, a + 1)
                nc.vector.tensor_tensor(mod[:, bass.ds(2 * a, 2)], ps[7][:, 0:2], cv[:, bass.ds(CV_ADAB + 2 * a, 2)], ALU.add).then_inc(s_mod, 1)

            def sum_square(n, c):
                if c == 0:
                    return
                dve.wait_ge(s_sq, C * n + c + 1)
                if c > 1:
                    dve.wait_ge(s_acc, 7 * n + c - 1)
                a = sc[:, 4, :] if c == 1 else sc[:, 6, :]
                nc.vector.tensor_tensor(sc[:, 6, :], a, sc[:, 4 + c % 2, :], ALU.add).then_inc(s_acc, 1)

            def gain_col(n, gain, layer, what, mods):
                dve.wait_ge(s_mod, mods)
                nc.vector.scalar_tensor_tensor(out=acol[:], in0=mcols(layer, what), scalar=1.0, in1=cv[:, gain:gain + C],
                                               op0=ALU.add, op1=ALU.mult).then_inc(s_acol, 1)

            def h_chunks(n, layer, what, rk):
                sh = mcols(layer, what)

                def lo(c):
                    dve.wait_ge(s_hhi, C * n + c + 1)
                    nc.vector.scalar_tensor_tensor(out=h_lo[:, c, :], in0=sc[:, 4 + c % 2, :], scalar=sh[:, c:c + 1],
                                                   in1=h_hi[:, c, :].bitcast(F32), op0=ALU.add, op1=ALU.subtract).then_inc(s_hlo, 1)

                dve.wait_ge(s_acol, n + 1)
                dve.wait_ge(s_rstd, rk + 1)
                for c in range(C):
                    if c >= 2:
                        dve.wait_ge(s_hlo, C * n + c - 1)
                    nc.vector.scalar_tensor_tensor(out=sc[:, 4 + c % 2, :], in0=x[:, c, :], scalar=acol[:, c:c + 1], in1=sc[:, 7, :],
                                                   op0=ALU.mult, op1=ALU.mult).then_inc(s_tm, 1)
                    if c >= 1:
                        lo(c - 1)
                lo(C - 1)

            dve.wait_ge(s_csil, 1)
            nc.vector.tensor_scalar(ctmp[:, 1, :], ctmp[:, 0, :], 1.0, None, ALU.add).then_inc(s_cact, 1)
            dve.wait_ge(s_cact, 1)
            nc.vector.reciprocal(ctmp[:, 2, :], ctmp[:, 1, :]).then_inc(s_cact, 1)
            dve.wait_ge(s_cact, 2)
            nc.vector.tensor_tensor(cact[:], ctmp[:, 2, :], cv[:, CV_C:CV_C + C], ALU.mult).then_inc(s_cact, 1)
            dve.wait_ge(s_cact, 3)
            for a in range(ADA_START):
                ada_sum(a, a % 2)
                if a >= 1:
                    ada_add(a - 1)
                if a == 2:
                    for c in range(C):
                        sum_square(0, c)
            ada_add(ADA_START - 1)
            gain_col(0, CV_GMIX, 0, "sc_m", ADA_START)
            dve.wait_ge(s_wf, 1)
            nc.vector.tensor_tensor(wf_lo[:, :, :].rearrange("p c h -> p (c h)"), wf_raw[:],
                                    wf_hi[:, :, :].rearrange("p c h -> p (c h)").bitcast(F32), ALU.subtract).then_inc(s_wf, 1)
            h_chunks(0, 0, "sh_m", 0)
            split_lo(0)

            for n in range(4):
                split_lo(n + 1)
                for tk in range(TB):
                    dve.wait_ge(s_tile, D_V + 4 * n + tk + 1)
                    nc.vector.tensor_copy(v_tok[:, tk, n * UW:(n + 1) * UW], ps[tk][:, 0:UW]).then_inc(s_tdve, 1)
                    a = ADA_START + 2 * n
                    if tk == 0:
                        ada_sum(a, 0)
                    if tk == 1:
                        ada_add(a)
                        ada_sum(a + 1, 1)
                    if tk == 2 and n < 3:
                        ada_add(a + 1)

            z, za, ze, zl = (pe_[F_AT:F_AT + HEADS, k, :] for k in range(4))
            dve.wait_ge(s_fa, 4)
            nc.vector.tensor_scalar(ze, z, 0.0, None, ALU.min).then_inc(s_fd, 1)
            dve.wait_ge(s_fd, 1)
            nc.vector.tensor_tensor(ze, ze, zl, ALU.subtract).then_inc(s_fd, 1)
            dve.wait_ge(s_fd, 2)
            nc.vector.tensor_tensor_scan(za, ze, ze, 0.0, ALU.add, ALU.bypass).then_inc(s_fd, 1)
            dve.wait_ge(s_fr, 1)
            nc.vector.scalar_tensor_tensor(out=f_rows[1], in0=za, scalar=-1.0, in1=f_rows[0].bitcast(F32),
                                           op0=ALU.mult, op1=ALU.subtract).then_inc(s_fr, 1)

            def q_lo(layer, gp):
                scale = FOX_SCALE if layer == 0 else MLA_SCALE
                for s in range(2):
                    dve.wait_ge(s_qhi, 2 * gp + s + 1)
                    out = qa[s][HD:P, :] if layer == 0 else qb[s][0:HD, :]
                    nc.vector.scalar_tensor_tensor(out=out, in0=PQ[s * HD:(s + 1) * HD, :], scalar=scale, in1=qa[s][0:HD, :].bitcast(F32),
                                                   op0=ALU.mult, op1=ALU.subtract).then_inc(s_qlo, 1)

            def k_lo(layer, gp):
                for s in range(2):
                    dve.wait_ge(s_khi, 2 * gp + s + 1)
                    nc.vector.tensor_tensor(kb[s][0:HD, :], PK[s * HD:(s + 1) * HD, :], ka[s][0:HD, :].bitcast(F32), ALU.subtract).then_inc(s_klo, 1)

            def maxes(gp, st):
                for s in range(2):
                    dve.wait_ge(s_score, 2 * (4 * gp + st) + s + 1)
                    nc.vector.tensor_reduce(nmax[:, st % 2, s:s + 1], S_BANK[st % 2][s][:, 0:P * (st + 1)], AXX, ALU.max,
                                            negate=True).then_inc(s_max, 1)

            def rinvs(gp, st):
                dve.wait_ge(s_exp, 2 * (4 * gp + st) + 2)
                nc.vector.reciprocal(rinv[:, st % 2, :], rsum[:, st % 2, :]).then_inc(s_rinv, 1)

            def pt_los(gp, st):
                for s in range(2):
                    dve.wait_ge(s_pthi, 2 * (4 * gp + st) + s + 1)
                    nc.vector.tensor_tensor(pt(s, pt_lo, st, st + 1), T_BANK[s][:, 0:P * (st + 1)].rearrange("p (j c) -> p j c", c=P),
                                            pt(s, pt_hi, st, st + 1).bitcast(F32), ALU.subtract).then_inc(s_ptlo, 1)

            def attn(layer, i, r, more, a):
                gp = PAIRS * layer + 2 * i + r
                maxes(gp, 0)
                maxes(gp, 1)
                rinvs(gp, 0)
                if a is not None:
                    ada_add(a - 1)
                rinvs(gp, 1)
                if a is not None:
                    ada_sum(a, r, 0, 4)
                maxes(gp, 2)
                maxes(gp, 3)
                pt_los(gp, 0)
                rinvs(gp, 2)
                pt_los(gp, 1)
                rinvs(gp, 3)
                if more:
                    q_lo(layer, gp + 1)
                pt_los(gp, 2)
                pt_los(gp, 3)
                if a is not None:
                    ada_sum(a, r, 4, 8)
                if more:
                    k_lo(layer, gp + 1)
                for s in range(2):
                    dve.wait_ge(s_ohi, 2 * gp + s + 1)
                    rows = slice(s * HD, (s + 1) * HD)
                    hi = o_hi[rows, bass.ds(2 * i + r, 1), :].rearrange("p a t -> p (a t)").bitcast(F32)
                    lo = o_lo[rows, bass.ds(2 * i + r, 1), :].rearrange("p a t -> p (a t)")
                    nc.vector.tensor_tensor(lo, S_BANK[1][s][rows, :], hi, ALU.subtract).then_inc(s_olo, 1)

            def attn_layer(layer, u0, n):
                split_lo(u0 + 1, n)
                q_lo(layer, PAIRS * layer)
                k_lo(layer, PAIRS * layer)
                a0 = ADA_START + 8 if layer == 0 else None
                with dve.Fori(0, 3) as i:
                    for r in range(2):
                        attn(layer, i, r, True, None if a0 is None else a0 + 2 * i + r)
                attn(layer, 3, 0, True, None if a0 is None else a0 + 6)
                attn(layer, 3, 1, False, None if a0 is None else a0 + 7)
                if layer == 0:
                    ada_add(a0 + 7)

            def gated_add(layer, what, j, c):
                g = mcols(layer, what)
                nc.vector.scalar_tensor_tensor(out=x[:, c, :], in0=ps[j % RING][:], scalar=g[:, c:c + 1], in1=x[:, c, :],
                                               op0=ALU.mult, op1=ALU.add).then_inc(s_tdve, 1)

            def out_proj(layer, u0, d):
                slot_of[0] = (u0 + 1) % 2
                n = 2 * layer + 1
                for k in range(4):
                    split_lo(u0 + k + 1)
                    for c in (2 * k, 2 * k + 1):
                        dve.wait_ge(s_tile, d + c + 1)
                        gated_add(layer, "g_m", c, c)
                        if c:
                            sum_square(n, c - 1)
                sum_square(n, C - 1)
                gain_col(n, CV_GMLP + C * layer, layer, "sc_f", 24 if layer == 0 else ADA_UNITS)
                h_chunks(n, layer, "sh_f", n + 2 * (n > 2))

            def mlp_group(layer, g, last, after_u):
                base = 32 * layer + 8 * g
                a = 24 + 6 * g
                for k in range(8):
                    if not (last and k == 7):
                        split_lo(U_MLP[layer] + 8 * g + k + 1)
                    elif after_u:
                        split_lo(*after_u)
                    if layer == 0 and 0 < k < 7:
                        ada_add(a + k - 1)
                    if layer == 0 and last and k == 7:
                        trig_tables()
                    for j in (2 * k, 2 * k + 1):
                        dve.wait_ge(s_tile, D_MLP[layer] + 16 * g + j + 1) if k >= 4 else dve.wait_ge(s_tact, base + j + 1)
                        if k < 4:
                            nc.vector.tensor_tensor(sc[:, 2 + j % 2, :], sc[:, j % 2, :], sc[:, j % 2, :], ALU.mult).then_inc(s_sqr, 1)
                            dve.wait_ge(s_ahi, base + j + 1)
                            nc.vector.tensor_tensor(o_lo[:, j, :], sc[:, 2 + j % 2, :], o_hi[:, j, :].bitcast(F32), ALU.subtract).then_inc(s_alo, 1)
                        else:
                            c = j - 8
                            gated_add(layer, "g_f", j, c)
                            if last and c:
                                sum_square(2 * layer + 2, c - 1)
                        if layer == 0 and k < 6 and j % 2 == 0:
                            ada_sum(a + k, k % 2)
                if last:
                    sum_square(2 * layer + 2, C - 1)

            def trig_tables():
                k, r = adab[:, 3, :], adab[:, 2, :]
                pi = 3.1415925
                dve.wait_ge(s_posin, 16)
                nc.vector.tensor_copy(k, adab[:, 2, :].bitcast(I32)).then_inc(s_trig, 1)
                dve.wait_ge(s_trig, 1)
                nc.vector.tensor_scalar(r, k, cc[:, CC_FREQ:CC_FREQ + 1], None, ALU.mult).then_inc(s_trig, 1)
                dve.wait_ge(s_trig, 2)
                nc.vector.tensor_scalar(k, r, INV_2PI, ROUND, ALU.mult, ALU.add).then_inc(s_trig, 1)
                dve.wait_ge(s_trig, 3)
                nc.vector.tensor_scalar(k, k, ROUND, None, ALU.subtract).then_inc(s_trig, 1)
                for n, part in enumerate(TWO_PI_PARTS):
                    dve.wait_ge(s_trig, 4 + n)
                    nc.vector.scalar_tensor_tensor(out=r, in0=k, scalar=-part, in1=r, op0=ALU.mult, op1=ALU.add).then_inc(s_trig, 1)
                dve.wait_ge(s_trig, 7)
                nc.vector.tensor_scalar(r, r, pi, -pi, ALU.min, ALU.max).then_inc(s_trig, 1)
                dve.wait_ge(s_trig, 8)
                nc.vector.tensor_scalar(k, r, 0.5 * math.pi, None, ALU.add).then_inc(s_trig, 1)
                dve.wait_ge(s_trig, 9)
                nc.vector.tensor_scalar(cos_t, k, math.pi, -2 * math.pi, ALU.is_gt, ALU.mult).then_inc(s_trig, 1)
                dve.wait_ge(s_trig, 10)
                nc.vector.tensor_tensor(k, k, cos_t, ALU.add).then_inc(s_trig, 1)
                dve.wait_ge(s_trig, 11)
                nc.vector.tensor_scalar(k, k, pi, -pi, ALU.min, ALU.max).then_inc(s_trig, 1)
                dve.wait_ge(s_triga, 1)
                nc.vector.tensor_scalar(sin_t, sin_t, cc[:, CC_SIGN:CC_SIGN + 1], None, ALU.mult).then_inc(s_trig, 1)

            def mlp(layer, after_u):
                with dve.Fori(0, GROUPS - 1) as g:
                    mlp_group(layer, g, False, None)
                mlp_group(layer, GROUPS - 1, True, after_u)

            attn_layer(0, U_QK, UNIT)
            out_proj(0, U_FOUT, D_FOUT)
            mlp(0, (U_DKV, C * 160))
            gain_col(2, CV_GMIX + C, 1, "sc_m", ADA_UNITS)
            h_chunks(2, 1, "sh_m", 2)
            split_lo(U_DQ)

            ckv_raw, cq_raw, cq_n = prob[0][0], (prob[0][1], prob[1][0]), (prob[0][0], prob[1][1])
            swap = [(m + ROPE // 2) % ROPE for m in range(ROPE)]
            krot, ksum = sc[0:ROPE, 0, :], sc[0:ROPE, 1, :]
            dve.wait_ge(s_tile, D_DKV + 1)
            nc.vector.tensor_copy(ckv_raw, ps[0][:]).then_inc(s_tdve, 1)
            dve.wait_ge(s_tile, D_DKV + 2)
            nc.vector.stream_shuffle(krot, ps[1][0:ROPE, :], swap).then_inc(s_kr, 1)
            dve.wait_ge(s_triga, 2)
            nc.vector.tensor_tensor(ksum, ps[1][0:ROPE, :], cos_t[0:ROPE, :], ALU.mult).then_inc(s_tdve, 1)
            dve.wait_ge(s_kr, 1)
            dve.wait_ge(s_trig, 13)
            nc.vector.tensor_tensor(krot, krot, sin_t[0:ROPE, :], ALU.mult).then_inc(s_kr, 1)
            dve.wait_ge(s_kr, 2)
            dve.wait_ge(s_tdve, TD_DKV + 2)
            nc.vector.tensor_tensor(ksum, ksum, krot, ALU.add).then_inc(s_kr, 1)
            dve.wait_ge(s_rstd, 4)
            nc.vector.scalar_tensor_tensor(out=sc[:, 5, :], in0=ckv_raw, scalar=cv[:, CV_GKV:CV_GKV + 1], in1=sc[:, 6, :],
                                           op0=ALU.mult, op1=ALU.mult).then_inc(s_rope, 1)
            dve.wait_ge(s_rpa, 2)
            nc.vector.tensor_tensor(qa[1][0:ROPE, :], ksum, qa[0][0:ROPE, :].bitcast(F32), ALU.subtract).then_inc(s_kr, 1)
            split_lo(U_MV, D)
            dve.wait_ge(s_rpa, 3)
            nc.vector.tensor_tensor(o_lo[:, 7, :], sc[:, 5, :], o_hi[:, 7, :].bitcast(F32), ALU.subtract).then_inc(s_rope, 1)
            for k in range(2):
                dve.wait_ge(s_tile, D_DQ + 1 + k)
                nc.vector.tensor_copy(cq_raw[k], ps[2 + k][:]).then_inc(s_tdve, 1)

            def v_tile(n):
                tk, half = n // 2, n % 2
                dve.wait_ge(s_tile, D_MV + n + 1)
                nc.vector.tensor_copy(v_tok[:, tk, half * T:(half + 1) * T], ps[n % RING][:]).then_inc(s_tdve, 1)

            v_tile(0)
            dve.wait_ge(s_rpa, 9)
            nc.vector.tensor_tensor(adab[:, 2, :], adab[:, 2, :], adab[:, 3, :], ALU.add).then_inc(s_rope, 1)
            for n in range(1, 5):
                v_tile(n)
            dve.wait_ge(s_rstd, 5)
            for k in range(2):
                nc.vector.scalar_tensor_tensor(out=cq_n[k], in0=cq_raw[k], scalar=cv[:, CV_GQ + k:CV_GQ + k + 1], in1=adab[:, 3, :],
                                               op0=ALU.mult, op1=ALU.mult).then_inc(s_rope, 1)
            for k in range(2):
                dve.wait_ge(s_rpa, 10 + k)
                nc.vector.tensor_tensor(h_lo[:, k, :], cq_n[k], h_hi[:, k, :].bitcast(F32), ALU.subtract).then_inc(s_rope, 1)
            for n in range(5, 8):
                v_tile(n)
            split_lo(U_QROPE, 2 * T)
            split_lo(U_MQK, MQK_W)
            for k in range(TB):
                a, b = adab[:, 2, :], adab[:, 3, :]
                dve.wait_ge(s_tile, D_QROPE + k + 1)
                nc.vector.stream_shuffle(b, ps[k][:], swap).then_inc(s_qra, 1)
                if k:
                    dve.wait_ge(s_qrd, k)
                nc.vector.tensor_tensor(a, ps[k][:], cos_t, ALU.mult).then_inc(s_tdve, 1)
                dve.wait_ge(s_qra, 3 * k + 1)
                nc.vector.tensor_tensor(b, b, sin_t, ALU.mult).then_inc(s_qra, 1)
                dve.wait_ge(s_tdve, TD_DKV + 13 + k)
                dve.wait_ge(s_qra, 3 * k + 2)
                nc.vector.tensor_tensor(a, a, b, ALU.add).then_inc(s_qra, 1)
                dve.wait_ge(s_rpa, 12 + k)
                nc.vector.scalar_tensor_tensor(out=h_lo[:, 2 + k, :], in0=a, scalar=MLA_SCALE, in1=h_hi[:, 2 + k, :].bitcast(F32),
                                               op0=ALU.mult, op1=ALU.subtract).then_inc(s_qrd, 1)

            attn_layer(1, U_MQK, MQK_W)
            out_proj(1, U_MOUT, D_MOUT)
            mlp(1, None)
            dve.wait_ge(s_rstd, 7)
            for c in range(C):
                nc.vector.scalar_tensor_tensor(out=sc[:, c, :], in0=x[:, c, :], scalar=cv[:, CV_GFIN + c:CV_GFIN + c + 1], in1=prob[0][0],
                                               op0=ALU.mult, op1=ALU.mult).then_inc(s_yn, 1)

        @block.tensor
        def _(pe):
            def product(out, lhs, rhs, start, stop):
                nc.tensor.matmul(out, lhs[0], rhs[0], start=start, stop=False)
                nc.tensor.matmul(out, lhs[1], rhs[0], start=False, stop=False)
                return nc.tensor.matmul(out, lhs[0], rhs[1], start=False, stop=stop)

            def w_view(slot, kc, n):
                return [w[:, slot, 0:kc * n].rearrange("p (k n) -> p k n", k=kc) for w in (w_hi, w_lo)]

            def w_ready(u):
                pe.wait_ge(s_wlo, 2 * u + 2)

            def bank_free(first, n, td):
                pe.wait_ge(s_tdve, td + n - 3)

            def ada_mm(a, par):
                pe.wait_ge(s_adastep, 8 * a + 8)
                if not (isinstance(a, int) and a == 0):
                    pe.wait_ge(s_mod, a)
                for j in range(2):
                    mm = nc.tensor.matmul(ps[7][:, j:j + 1], adaacc[:, par, j * P:(j + 1) * P], ones[:, 0:1], start=True, stop=True)
                mm.then_inc(s_adamm, 1)

            def sum_over_features(src):
                nc.tensor.matmul(T_BANK[1][:], ones[:], src, start=True, stop=True).then_inc(s_ss, 1)

            pe.wait_ge(s_ones, 1)
            for a in range(ADA_START):
                ada_mm(a, a % 2)
                if a == 3:
                    pe.wait_ge(s_acc, 7)
                    sum_over_features(sc[:, 6, :])

            for n in range(4):
                w = w_view(n % 2, C, UW)
                w_ready(U_V + n)
                for tk in range(TB):
                    d = 4 * n + tk
                    if d >= RING:
                        pe.wait_ge(s_tdve, d - RING + 1)
                    for k in range(C):
                        if d == 0:
                            pe.wait_ge(s_hlo, k + 1)
                        mm = product(ps[tk][:, 0:UW], [h[:, k, tk * P:(tk + 1) * P] for h in (h_hi, h_lo)],
                                     [v[:, k, :] for v in w], k == 0, k == C - 1)
                    mm.then_inc(s_tile, 1)
                    if tk == 1 or (tk == 2 and n < 3):
                        ada_mm(ADA_START + 2 * n + tk - 1, tk - 1)
            pe.wait_ge(s_wf, 2)
            for k in range(C):
                mm = product(T_BANK[0][0:HEADS, :], [w[:, k, :] for w in (wf_hi, wf_lo)], [h[:, k, :] for h in (h_hi, h_lo)],
                             k == 0, k == C - 1)
            mm.then_inc(s_fmm, 1)

            def q_part(layer, slot, k0, k1):
                if layer == 0:
                    w, n, at = w_view(slot, C, UW), C, 0
                else:
                    w, n, at = w_view(slot, 3, P), 2, 0
                for k in range(k0, min(k1, n)):
                    mm = product(PQ[:], [v[:, k, at:at + P] for v in w], [h[:, k, :] for h in (h_hi, h_lo)], k == 0, k == n - 1)
                    if k == n - 1:
                        mm.then_inc(s_pq, 1)

            def k_part(layer, slot, k0, k1):
                if layer == 0:
                    for k in range(k0, k1):
                        mm = product(PK[:], [v[:, k, P:2 * P] for v in w_view(slot, C, UW)], [h[:, k, :] for h in (h_hi, h_lo)],
                                     k == 0, k == C - 1)
                        if k == C - 1:
                            mm.then_inc(s_pk, 1)
                elif k0 == 0:
                    product(PK[:], [v[:, 2, :] for v in w_view(slot, 3, P)], [o[:, 7, :] for o in (o_hi, o_lo)],
                            True, True).then_inc(s_pk, 1)

            def scores(layer, gp, st):
                rows = (P, HD + 2) if layer == 0 else (MLA_K, MLA_K)
                n = P * (st + 1)
                for s in range(2):
                    out = S_BANK[st % 2][s]
                    if st == 0:
                        pe.wait_ge(s_qlo, 2 * gp + s + 1)
                        pe.wait_ge(s_klo, 2 * gp + s + 1)
                        if layer == 0:
                            pe.wait_ge(s_qx[s], 16 * gp + 16)
                            pe.wait_ge(s_kx[s], 16 * gp + 16)
                            pe.wait_ge(s_fx[s], 16 * gp + 16)
                        else:
                            pe.wait_ge(s_qx[s], 32 * gp + (32 - 16 * PAIRS))
                    if st == 1:
                        pe.wait_ge(s_olo, 2 * gp)
                    if st >= 2:
                        pe.wait_ge(s_exp, 2 * (4 * gp + st - 2) + s + 1)
                    q = [t[s][0:m, P * st:n] for t, m in zip((qa, qb), rows)]
                    k = [t[s][0:m, 0:n] for t, m in zip((ka, kb), rows)]
                    nc.tensor.matmul(out[:, 0:n], q[0], k[0], start=True, stop=False)
                    if layer == 0:
                        nc.tensor.matmul(out[:, 0:n], q[1], k[1], start=False, stop=False)
                    else:
                        nc.tensor.matmul(out[:, 0:n], q[1], k[0], start=False, stop=False)
                        nc.tensor.matmul(out[:, 0:n], q[0], k[1], start=False, stop=False)
                    nc.tensor.matmul(out[:, P * st:n], id_b[:], mask_b[:], start=False, stop=True).then_inc(s_score, 1)

            def transposes(gp, st):
                for s in range(2):
                    pe.wait_ge(s_norm, 2 * (4 * gp + st) + s + 1)
                    if st:
                        pe.wait_ge(s_ptlo, 2 * (4 * gp + st - 1) + s + 1)
                    for j in range(st + 1):
                        mm = nc.tensor.transpose(T_BANK[s][:, P * j:P * (j + 1)], prob[st % 2][s][:, P * j:P * (j + 1)], ident)
                    mm.then_inc(s_tr, 1)

            def attend(gp):
                pe.wait_ge(s_vlo, gp + 1)
                for s in range(2):
                    pe.wait_ge(s_ptlo, 2 * (4 * gp + 3) + s + 1)
                    for j in range(TB):
                        at = s * PTH + (PTS + P) * j
                        mm = product(S_BANK[1][s][:, P * j:T], [v[:, j, :] for v in (vs_hi, vs_lo)],
                                     [b[:, at:at + T - P * j] for b in (pt_hi, pt_lo)], j == 0, j == TB - 1)
                    mm.then_inc(s_pv, 1)

            def attn(layer, i, r, more, u, a):
                gp = PAIRS * layer + 2 * i + r
                slot = (r + 1) % 2
                if more:
                    w_ready(u)
                    pe.wait_ge(s_qlo, 2 * gp + 2)
                    q_part(layer, slot, 0, 4)
                scores(layer, gp, 0)
                if a is not None:
                    ada_mm(a - 1, (r + 1) % 2)
                scores(layer, gp, 1)
                if more:
                    q_part(layer, slot, 4, 8)
                scores(layer, gp, 2)
                scores(layer, gp, 3)
                transposes(gp, 0)
                if more:
                    if a is not None:
                        pe.wait_ge(s_mod, a)
                    pe.wait_ge(s_klo, 2 * gp + 2)
                    k_part(layer, slot, 0, 2)
                transposes(gp, 1)
                if more:
                    k_part(layer, slot, 2, 4)
                transposes(gp, 2)
                if more:
                    k_part(layer, slot, 4, 6)
                transposes(gp, 3)
                if more:
                    k_part(layer, slot, 6, 8)
                attend(gp)

            def attn_layer(layer, u0):
                w_ready(u0)
                q_part(layer, 0, 0, 8)
                if layer == 0:
                    pe.wait_ge(s_mod, ADA_START + 7)
                k_part(layer, 0, 0, 8)
                if layer == 0:
                    pe.wait_ge(s_tdve, TD_FOUT)
                    pe.wait_ge(s_zero, 2)
                else:
                    pe.wait_ge(s_tdve, TD_MOUT)
                    pe.wait_ge(s_rpa, 7)
                a0 = ADA_START + 8 if layer == 0 else None
                with pe.Fori(0, 3) as i:
                    for r in range(2):
                        attn(layer, i, r, True, u0 + 2 * i + r + 1, None if a0 is None else a0 + 2 * i + r)
                attn(layer, 3, 0, True, u0 + 7, None if a0 is None else a0 + 6)
                attn(layer, 3, 1, False, None, None if a0 is None else a0 + 7)
                if layer == 0:
                    ada_mm(a0 + 7, 1)

            def dense_tile(bank, w, at, rhs, ready=None):
                for k in range(C):
                    if ready is not None:
                        pe.wait_ge(ready[0], ready[1] + k)
                    mm = product(bank[:], [v[:, k, at:at + P] for v in w], [t[:, k, :] for t in rhs], k == 0, k == C - 1)
                mm.then_inc(s_tile, 1)

            def out_proj(layer, u0, td):
                for n in range(4):
                    w_ready(u0 + n)
                    for t in range(2):
                        c = 2 * n + t
                        if c < RING:
                            pe.wait_ge(s_olo, HEADS * (layer + 1))
                        else:
                            pe.wait_ge(s_tdve, td + c - 3)
                        dense_tile(ps[c % RING], w_view(n % 2, C, UW), t * P, (o_hi, o_lo))
                pe.wait_ge(s_acc, 7 * (2 * layer + 2))
                sum_over_features(sc[:, 6, :])

            def mlp_group(layer, g, first):
                base = 32 * layer + 8 * g
                norm = 2 * layer + 1
                for n in range(8):
                    w_ready(U_MLP[layer] + 8 * g + n)
                    if layer == 0 and 0 < n < 7:
                        ada_mm(24 + 6 * g + n - 1, (n - 1) % 2)
                    for t in range(2):
                        j = 2 * n + t
                        c = j - 8
                        if j < 4:
                            pe.wait_ge(s_tdve, TD_MLP[layer] + 8 * g + j - 3)
                        elif j < 12:
                            pe.wait_ge(s_tact, base + j - 3)
                        else:
                            pe.wait_ge(s_tdve, TD_MLP[layer] + 8 * g + c - 3)
                        if n < 4:
                            ready = (s_hlo, C * norm + 1) if first and j == 0 else None
                        else:
                            ready = (s_alo, base + 1) if c == 0 else None
                        dense_tile(ps[j % RING], w_view(n % 2, C, UW), t * P, (h_hi, h_lo) if n < 4 else (o_hi, o_lo), ready)

            def mlp(layer):
                mlp_group(layer, 0, True)
                with pe.Fori(1, GROUPS) as g:
                    mlp_group(layer, g, False)
                pe.wait_ge(s_acc, 7 * (2 * layer + 3))
                sum_over_features(sc[:, 6, :])

            attn_layer(0, U_QK)
            out_proj(0, U_FOUT, TD_FOUT)
            mlp(0)

            w = w_view(0, C, KVR + ROPE)
            w_ready(U_DKV)
            pe.wait_ge(s_tdve, TD_DKV - 3)
            dense_tile(ps[0], w, 0, (h_hi, h_lo), (s_hlo, 2 * C + 1))
            pe.wait_ge(s_tdve, TD_DKV - 2)
            for k in range(C):
                mm = product(ps[1][0:ROPE, :], [v[:, k, KVR:KVR + ROPE] for v in w], [t[:, k, :] for t in (h_hi, h_lo)],
                             k == 0, k == C - 1)
            mm.then_inc(s_tile, 1)
            w_ready(U_DQ)
            for t in range(2):
                pe.wait_ge(s_tdve, TD_DKV - 1 + t)
                dense_tile(ps[2 + t], w_view(1, C, UW), t * P, (h_hi, h_lo))
                if t == 0:
                    pe.wait_ge(s_rpa, 1)
                    sum_over_features(sc[:, 4, :])
            w_ready(U_MV)
            pe.wait_ge(s_rope, 2)
            for n in range(2 * TB):
                tk, half = n // 2, n % 2
                pe.wait_ge(s_tdve, TD_DKV + n + 1)
                product(ps[n % RING][:], [o[:, 7, tk * P:(tk + 1) * P] for o in (o_hi, o_lo)],
                        [v[:, 0, half * T:(half + 1) * T] for v in w_view(0, 1, D)], True, True).then_inc(s_tile, 1)
                if n == 3:
                    pe.wait_ge(s_rope, 3)
                    sum_over_features(adab[:, 2, :])
            w_ready(U_QROPE)
            pe.wait_ge(s_rope, 7)
            for t in range(TB):
                pe.wait_ge(s_tdve, TD_DKV + t + 9)
                for k in range(2):
                    mm = product(ps[t][:], [v[:, k, t * P:(t + 1) * P] for v in w_view(1, 2, T)], [h[:, k, :] for h in (h_hi, h_lo)],
                                 k == 0, k == 1)
                mm.then_inc(s_tile, 1)

            attn_layer(1, U_MQK)
            out_proj(1, U_MOUT, TD_MOUT)
            mlp(1)


def columns(v):
    import numpy as np
    return np.ascontiguousarray(np.asarray(v).reshape(-1, P).T)


def units(w, n):
    import numpy as np
    k, m = w.shape
    return np.ascontiguousarray(w.reshape(k // P, P, m // n, n).transpose(2, 1, 0, 3)).reshape(m // n, P, -1)


def kernel(**inputs):
    import numpy as np
    import concourse.bacc as bacc
    from concourse.bass_utils import run_bass_kernel_spmd as run

    a = {k: np.asarray(v) for k, v in inputs.items()}
    cat = np.concatenate

    which = ("sh_m", "sc_m", "g_m", "sh_f", "sc_f", "g_f")
    spans = [(layer, which.index(w) * D) for layer, w in ADA_ORDER]
    ada = cat([units(a["ada_w"][layer][:, at:at + D], UW) for layer, at in spans])
    ada_b = cat([a["ada_b"][layer][at:at + D] for layer, at in spans])
    bf = np.zeros(P, np.float32)
    bf[:HEADS] = a["fox_b_f"][0]
    cvec = cat([columns(v) for v in (
        a["c"][0], ada_b, a["norm_mix_g"][0], a["norm_mix_g"][1], a["norm_mlp_g"][0], a["norm_mlp_g"][1],
        a["final_norm_g"], a["mla_q_norm_g"][0], a["mla_kv_norm_g"][0], bf)], axis=1)

    row = np.arange(P)
    cconst = np.zeros((P, CC_N), np.float32)
    cconst[:, CC_ID:CC_ID + P] = np.eye(P)
    cconst[:, CC_MASK:CC_MASK + P] = np.where(row[None, :] > row[:, None], NEG, 0.0)
    cconst[:, CC_FREQ] = 10000.0 ** (-(2 * (row % (ROPE // 2))).astype(np.float64) / ROPE)
    cconst[:, CC_EPS] = EPS
    cconst[:, CC_SIGN] = np.where(row % ROPE < ROPE // 2, -1.0, 1.0)

    w_in = a["fox_w_in"][0]
    q, k, v, f = (w_in[:, n * D:(n + 1) * D] for n in range(4))
    w_qk = np.concatenate([units(q, P).reshape(PAIRS, P, C, P), units(k, P).reshape(PAIRS, P, C, P)], axis=3).reshape(PAIRS, P, UNIT)
    uq = a["mla_w_uq"][0].reshape(QR, HEADS, HD + ROPE)
    ukv = a["mla_w_ukv"][0].reshape(KVR, HEADS, 2 * HD)
    uq_nope, uq_rope = uq[:, :, :HD].reshape(QR, D), uq[:, :, HD:].reshape(QR, HEADS * ROPE)
    uk, uv = ukv[:, :, :HD].reshape(KVR, D), ukv[:, :, HD:].reshape(KVR, D)
    w_mlp = []
    for layer in range(2):
        w1, w2 = a["mlp_w1"][layer], a["mlp_w2"][layer]
        for g in range(GROUPS):
            w_mlp += [units(w1[:, g * D:(g + 1) * D], UW), units(w2[g * D:(g + 1) * D], UW)]
    feeds = dict(
        xt=np.ascontiguousarray(a["x"][0].reshape(T, C, P).transpose(2, 1, 0)),
        pos=a["positions"].reshape(T),
        cvec=cvec, cconst=cconst, ada=ada,
        w_v=units(v, UW), w_qk=w_qk, w_f=units(f, HEADS)[0],
        w_fout=units(a["fox_w_out"][0], UW),
        w_dkv=units(a["mla_w_dkv"][0], KVR + ROPE), w_dq=units(a["mla_w_dq"][0], UW),
        w_mv=units(uv, D), w_qrope=units(uq_rope, T),
        w_mqk=cat([units(uq_nope, P), units(uk, P)], axis=2),
        w_mout=units(a["mla_w_out"][0], UW), w_mlp=cat(w_mlp))

    nc = bacc.Bacc("TRN2", target_bir_lowering=False, num_devices=1)
    args, arrays = {}, {}
    for name, arr in feeds.items():
        arr = np.ascontiguousarray(arr)
        arrays[name + "_dram"] = arr
        args[name] = nc.dram_tensor(name + "_dram", arr.shape, mybir.dt.from_np(arr.dtype), kind="ExternalInput").ap()
    args["yt"] = nc.dram_tensor("yt_dram", (P, C, T), F32, kind="ExternalOutput").ap()
    args["f_dram"] = nc.dram_tensor("f_rows_dram", (HEADS, 2, T), F32, kind="Internal").ap()
    trunk(nc, **args)
    r = run(nc, [arrays], core_ids=[0])
    y = r.results[0]["yt_dram"]
    return np.ascontiguousarray(y.transpose(2, 1, 0)).reshape(1, T, D)
```

```python
import math
from contextlib import ExitStack

import concourse.bass as bass
from concourse import mybir

F32 = mybir.dt.float32
F32R = mybir.dt.float32r
BF16 = mybir.dt.bfloat16
I32 = mybir.dt.int32
ALU = mybir.AluOpType
ACT = mybir.ActivationFunctionType
AXX = mybir.AxisListType.X

P = 128
T = 512
D = 1024
C = D // P
TB = T // P
HEADS = 16
HD = D // HEADS
ROPE = HD // 2
PAIRS = HEADS // 2
QR, KVR = D // 4, D // 8
DFF = 4 * D
GROUPS = DFF // (C * P)
UW = 256
UNIT = C * UW
HALF = UNIT // 2
ADA_UNITS = 2 * 6 * D // UW
ADA_START = 8
EPS = 1e-6
NEG = -1e30
INV_2PI = 1 / (2 * math.pi)
ROUND = 1.5 * 2.0 ** 23
TWO_PI_PARTS = (6.28125, 0.0019340515136718750, 1.2556659146e-06)
FOX_SCALE = HD ** -0.5
MLA_SCALE = (HD + ROPE) ** -0.5
MLA_K = HD + ROPE
F_AT = 96
PTS = 384
PTH = PTS * 3 + T

U_V = 0
U_QK = U_V + 4
U_FOUT = U_QK + PAIRS
U_MLP = (U_FOUT + 4, U_FOUT + 4 + 32 + 4 + PAIRS + 4)
U_DKV = U_MLP[0] + 32
U_DQ, U_MV, U_QROPE = U_DKV + 1, U_DKV + 2, U_DKV + 3
U_MQK = U_DKV + 4
U_MOUT = U_MQK + PAIRS
N_UNITS = U_MLP[1] + 32
MQK_W = 3 * P

D_V = 0
D_FOUT = 16
D_MLP = (D_FOUT + C, D_FOUT + C + 64 + 4 + 8 + 4 + C)
D_DKV = D_MLP[0] + 64
D_DQ, D_MV, D_QROPE = D_DKV + 2, D_DKV + 4, D_DKV + 12
D_MOUT = D_DKV + 16
RING = 4

TD_FOUT = 16
TD_MLP = (TD_FOUT + C, TD_FOUT + C + 32 + 16 + C)
TD_DKV = TD_MLP[0] + 32
TD_MOUT = TD_DKV + 16

ADA_ORDER = [(layer, w) for layer in range(2) for w in ("sc_m", "sh_m", "g_m", "sh_f", "sc_f", "g_f")]

ADA_EARLY = 16
ADA_GP = (1, 4, 8, 10, 12, 14)
ADA_STEPS = (8, 7)
ADA_SLOT = (0, 1, 2, 3, 4, 5, 6, 0, 3, 4, 5, 6, 0, 3, 4, 5)


def ada_own(a):
    own = int(a in ADA_GP)
    return own, sum((b in ADA_GP) == bool(own) for b in range(a))


CV_C = 0
CV_ADAB = CV_C + C
CV_GMIX = CV_ADAB + 2 * ADA_UNITS
CV_GMLP = CV_GMIX + 2 * C
CV_GFIN = CV_GMLP + 2 * C
CV_GQ = CV_GFIN + C
CV_GKV = CV_GQ + 2
CV_BF = CV_GKV + 1
CV_N = CV_BF + 1
CC_ID = 0
CC_MASK = CC_ID + P
CC_FREQ = CC_MASK + P
CC_EPS = CC_FREQ + 1
CC_SIGN = CC_EPS + 1
CC_N = CC_SIGN + 1


def trunk(nc, xt, pos, cvec, cconst, ada, w_v, w_qk, w_f, w_fout, w_dkv, w_dq, w_mv, w_qrope, w_mqk, w_mout, w_mlp, f_dram, yt):
    ctx = ExitStack()
    with ctx:
        def sb(name, shape, dt):
            return ctx.enter_context(nc.sbuf_tensor(name, shape, dt))

        def sem(name):
            return ctx.enter_context(nc.semaphore(name))

        x = sb("x", [P, C, T], F32)
        h_hi, h_lo = sb("h_hi", [P, C, T], F32R), sb("h_lo", [P, C, T], F32R)
        o_at = nc.sbuf_base
        o_hi, o_lo = sb("o_hi", [P, C, T], F32R), sb("o_lo", [P, C, T], F32R)
        ada_space = nc.alloc_sbuf_tensor_at("ada_space", [P, 4, UNIT], F32, offset=o_at)
        w_raw = sb("w_raw", [P, UNIT], F32)
        w_hi, w_lo = sb("w_hi", [P, 2, UNIT], F32R), sb("w_lo", [P, 2, UNIT], F32R)
        adab = sb("adab", [P, 4, T], F32)
        v_raw = sb("v_raw", [P, 8, T], F32)
        qa, qb, ka, kb = ([sb(f"{n}{s}", [P, T], F32R) for s in range(2)] for n in ("qa", "qb", "ka", "kb"))
        pe_ = sb("probs", [P, 4, T], F32)
        pt_hi = sb("pt_hi", [P, PTH + PTS * 5], F32R)
        pt_lo = sb("pt_lo", [P, PTH + PTS * 5], F32R)
        vs_hi, vs_lo = sb("vs_hi", [P, TB, P], F32R), sb("vs_lo", [P, TB, P], F32R)
        cv = sb("cv", [P, CV_N], F32)
        cc = sb("cc", [P, CC_N], F32)
        ones = sb("ones", [P, P], F32)
        id_b, mask_b = sb("id_b", [P, P], BF16), sb("mask_b", [P, P], BF16)
        cact = sb("cact", [P, C], F32)
        ctmp = sb("ctmp", [P, 3, C], F32)
        mod = sb("mod", [P, 2 * ADA_UNITS], F32)
        acol = sb("acol", [P, C], F32)
        adaacc = sb("adaacc", [P, 4, UW], F32)
        warm = sb("warm", [P, 1], F32)
        nmax, rsum, rinv = sb("nmax", [P, 2, 2], F32), sb("rsum", [P, 2, 2], F32), sb("rinv", [P, 2, 2], F32)
        f_rows = [kb[part][F_AT:F_AT + HEADS, :] for part in range(2)]
        wf_raw = sb("wf_raw", [P, C * HEADS], F32)
        wf_hi, wf_lo = (t[:, 0:C * HEADS].rearrange("p (c h) -> p c h", c=C) for t in (pt_hi, pt_lo))

        ps = [ctx.enter_context(nc.psum_tensor(f"ps{i}", [P, T], F32)) for i in range(8)]
        S_BANK = [[ps[0], ps[1]], [ps[2], ps[3]]]
        T_BANK = [ps[4], ps[5]]
        PQ, PK = ps[6], ps[7]

        ident = cc[:, CC_ID:CC_ID + P]
        sc = v_raw
        prob = [[pe_[:, 2 * r + s, :] for s in range(2)] for r in range(2)]
        cos_t, sin_t = adab[:, 0, :], adab[:, 1, :]
        ada_slots = [t.rearrange("p a t -> p (a t)") for t in (
            adab[:, :, :], v_raw[:, 0:4, :], pe_[:, :, :],
            *(ada_space[:, n:n + 1, :] for n in range(4)))]
        v_tok = v_raw[:, :, :].rearrange("p a t -> p (a t)").rearrange("p (b n) -> p b n", b=TB)

        def mcols(layer, what):
            at = C * ADA_ORDER.index((layer, what))
            return mod[:, at:at + C]

        s_cin, s_xin, s_posin, s_fin = sem("const_in"), sem("x_in"), sem("pos_in"), sem("wf_in")
        s_ast = [sem(f"ada_start_in{i}") for i in range(7)]
        s_ain = [sem(f"ada_in{i}") for i in range(2)]
        s_win = [sem(f"w_in{i}") for i in range(2)]
        s_whi, s_wlo = sem("w_hi_done"), sem("w_lo_done")
        s_astep = [sem("ada_step_vector"), sem("ada_step_gpsimd")]
        s_adamm, s_mod, s_warm = sem("ada_mm"), sem("mod_done"), sem("table_warm")
        s_ones, s_bf, s_csil, s_cact = sem("ones_set"), sem("bf_consts"), sem("silu_act"), sem("silu_dve")
        s_tile = sem("tile_done")
        s_tact, s_tdve = sem("tile_read_act"), sem("tile_read_dve")
        s_xup, s_sq, s_acc = sem("x_updated"), sem("square_done"), sem("square_summed")
        s_ss, s_ln, s_rstd = sem("sumsq_mm"), sem("ln_done"), sem("rstd_done")
        s_acol, s_tm, s_hhi, s_hlo = sem("acol_done"), sem("xhat_done"), sem("h_hi_done"), sem("h_lo_done")
        s_relu, s_sqr, s_ahi, s_alo = sem("relu_done"), sem("relu_squared"), sem("a_hi_done"), sem("a_lo_done")
        s_wf, s_fmm, s_fa, s_fd, s_fr = sem("wf_split"), sem("f_mm"), sem("f_act"), sem("f_dve"), sem("f_rows")
        s_score, s_max, s_exp, s_rinv, s_norm = sem("scores"), sem("rowmax"), sem("exp"), sem("rinv"), sem("normed")
        s_tr, s_pthi, s_ptlo = sem("transposed"), sem("pt_hi_done"), sem("pt_lo_done")
        s_pq, s_pk, s_qhi, s_qlo, s_khi, s_klo = (sem(n) for n in ("q_mm", "k_mm", "q_hi_done", "q_lo_done", "k_hi_done", "k_lo_done"))
        s_qx, s_kx, s_fx = ([sem(f"{n}{s}") for s in range(2)] for n in ("q_rows_in", "k_rows_in", "f_rows_in"))
        s_vhi, s_vlo, s_pv, s_ohi, s_olo = sem("v_hi_done"), sem("v_lo_done"), sem("pv_mm"), sem("o_hi_done"), sem("o_lo_done")
        s_rope, s_rpa, s_kr, s_lat = sem("rope_dve"), sem("rope_act"), sem("krope_rows"), sem("latent_raw")
        s_trig, s_triga, s_qrd, s_qra = sem("trig_dve"), sem("trig_act"), sem("qrope_dve"), sem("qrope_act")
        s_out = [sem(f"y_out{i}") for i in range(C)]
        s_fdram = sem("f_stored")
        s_zero, s_passed = sem("zero_rows"), sem("pool_waits_passed")
        s_yn = sem("y_done")

        block = ctx.enter_context(nc.Block())

        def pt(s, buf, i, n):
            at = s * PTH + P * i
            return buf[:, at:at + PTS * n].rearrange("p (j c) -> p j c", c=PTS)[:, :, 0:P]


        def after(i, r):
            return (i, 1) if r == 0 else (i + 1, 0)

        @block.sync
        def _(sp):
            def load_w(u, src, n=UNIT, narrow=False):
                for hf in range(2):
                    split = 2 * u if narrow else 2 * u + hf - 1
                    if not (isinstance(u, int) and u == 0):
                        sp.wait_ge(s_whi, split)
                        sp.wait_ge(s_wlo, split)
                    a, b = hf * (n // 2), (hf + 1) * (n // 2)
                    sp.dma_start(w_raw[:, a:b], src[:, a:b]).then_inc(s_win[hf], 16)

            def load_ada_early(a):
                slot = ADA_SLOT[a]
                before = [b for b in range(a) if ADA_SLOT[b] == slot]
                if before:
                    own, idx = ada_own(before[-1])
                    sp.wait_ge(s_astep[own], ADA_STEPS[own] * (idx + 1))
                sp.dma_start(ada_slots[slot], ada[a, :, :]).then_inc(s_ast[slot], 16)

            def load_ada(a, own, idx):
                for hf in range(2):
                    sp.wait_ge(s_astep[own], ADA_STEPS[own] * (idx - 1) + (4, 3)[own] * (hf + 1) + own * hf)
                    a0, b0 = hf * HALF, (hf + 1) * HALF
                    sp.dma_start(ada_slots[0][:, a0:b0], ada[a, :, a0:b0]).then_inc(s_ain[hf], 16)

            def operand_rows(layer, i, r):
                gp = PAIRS * layer + 2 * i + r
                sp.wait_ge(s_score, 8 * gp)
                for s in range(2):
                    if layer == 0:
                        sp.dma_start(kb[s][HD:HD + 2, :].bitcast(F32), f_dram[bass.ds(4 * i + (2 * r + s), 1), :, :]).then_inc(s_fx[s], 16)
                    else:
                        at = ROPE * (2 * r + s)
                        for dst, src in ((qa, h_hi), (qb, h_lo)):
                            sp.dma_start(dst[s][HD:MLA_K, :].bitcast(F32), src[at:at + ROPE, bass.ds(2 + i, 1), :].bitcast(F32)).then_inc(s_qx[s], 16)
                if layer == 0:
                    for s in range(2):
                        sp.wait_ge(s_qhi, 2 * gp + s + 1)
                        sp.dma_start(qb[s][0:HD, :].bitcast(F32), qa[s][0:HD, :].bitcast(F32)).then_inc(s_qx[s], 16)
                    for s in range(2):
                        sp.wait_ge(s_khi, 2 * gp + s + 1)
                        sp.dma_start(ka[s][HD:P, :].bitcast(F32), ka[s][0:HD, :].bitcast(F32)).then_inc(s_kx[s], 16)

            sp.dma_start(cv[:], cvec).then_inc(s_cin, 16)
            sp.dma_start(cc[:], cconst).then_inc(s_cin, 16)
            for a in range(ADA_START):
                if a == 4:
                    sp.dma_start(x[:, :, :], xt).then_inc(s_xin, 16)
                load_ada_early(a)
            sp.dma_start(wf_raw[:], w_f).then_inc(s_fin, 16)
            load_w(0, w_v[0])
            for n in range(4):
                load_w(U_V + n + 1, w_v[n + 1] if n < 3 else w_qk[0])
                load_ada_early(ADA_START + 2 * n)
                load_ada_early(ADA_START + 2 * n + 1)
            load_w(U_QK + 1, w_qk[1])
            for part in range(2):
                sp.wait_ge(s_fr, part + 1)
                sp.dma_start(f_dram[:, part, :], f_rows[part].bitcast(F32)).then_inc(s_fdram, 16)
            sp.wait_ge(s_fdram, 32)
            operand_rows(0, 0, 0)
            with sp.Fori(0, 3) as i:
                for r in range(2):
                    load_w(U_QK + 2 * i + r + 2, w_qk[2 * i + (r + 2)])
                    load_ada(ADA_EARLY + 2 * i + r, 0, 10 + 2 * i + r)
                    operand_rows(0, *after(i, r))
            load_w(U_FOUT, w_fout[0])
            load_ada(22, 0, 16)
            operand_rows(0, 3, 1)
            load_ada(23, 0, 17)
            for n in range(1, 4):
                load_w(U_FOUT + n, w_fout[n])
            load_w(U_MLP[0], w_mlp[0])
            sp.wait_ge(s_astep[0], 8 * 18)

            def mlp_loads(layer, g, last):
                for n in range(8):
                    if not (last and n == 7):
                        load_w(U_MLP[layer] + 8 * g + n + 1, w_mlp[32 * layer + 8 * g + (n + 1)])
                    elif layer == 0:
                        load_w(U_DKV, w_dkv[0], C * 160)
                    if layer == 0 and n < 6:
                        load_ada(24 + 6 * g + n, 1, 6 + 6 * g + n)
                    if layer == 0 and last and n == 5:
                        sp.wait_ge(s_astep[1], 7 * (6 + 24))
                        sp.dma_start(adab[:, 2, :].bitcast(I32), pos.partition_broadcast(P)).then_inc(s_posin, 16)

            with sp.Fori(0, GROUPS - 1) as g:
                mlp_loads(0, g, False)
            mlp_loads(0, GROUPS - 1, True)
            load_w(U_DQ, w_dq[0], narrow=True)
            load_w(U_MV, w_mv[0], D)
            load_w(U_QROPE, w_qrope[0], 2 * T)
            load_w(U_MQK, w_mqk[0], MQK_W)
            load_w(U_MQK + 1, w_mqk[1], MQK_W)
            sp.wait_ge(s_qrd, TB)
            operand_rows(1, 0, 0)
            with sp.Fori(0, 3) as i:
                for r in range(2):
                    load_w(U_MQK + 2 * i + r + 2, w_mqk[2 * i + (r + 2)], MQK_W)
                    operand_rows(1, *after(i, r))
            operand_rows(1, 3, 1)
            for n in range(4):
                load_w(U_MOUT + n, w_mout[n], narrow=(n == 0))
            load_w(U_MLP[1], w_mlp[32])
            with sp.Fori(0, GROUPS - 1) as g:
                mlp_loads(1, g, False)
            mlp_loads(1, GROUPS - 1, True)
            for c in range(C):
                sp.wait_ge(s_yn, c + 1)
                sp.dma_start(yt[:, c, :], sc[:, c, :]).then_inc(s_out[c], 16)
            for c in range(C):
                sp.wait_ge(s_out[c], 16)


        @block.gpsimd
        def _(pool):
            nc.gpsimd.memset(ones[:], 1.0).then_inc(s_ones, 1)
            for s in range(2):
                pool.wait_ge(s_ones, 1)
                if s:
                    pool.wait_ge(s_zero, 1)
                nc.gpsimd.memset(qb[s][HD:HD + 2, :].bitcast(F32), 1.0).then_inc(s_zero, 1)

            def waits(*pairs):
                for sem, count in pairs:
                    pool.wait_ge(sem, count)
                pool.sem_inc(s_passed, 1)

            def ada_sum(a, idx, par, buf, arrived):
                acc = adaacc[:, 2 + par, :]
                step = 7 * idx
                if not (isinstance(idx, int) and idx < 2):
                    waits((s_adamm, a - 1))
                for hf in range(2):
                    waits(arrived(hf), (s_astep[1], step))
                    w = buf[:, hf * HALF:(hf + 1) * HALF]
                    wk = w.rearrange("p (k n) -> p k n", k=C // 2)
                    c = cact[:, hf * C // 2:(hf + 1) * C // 2].unsqueeze(2).to_broadcast([P, C // 2, UW])
                    nc.gpsimd.tensor_tensor(wk, wk, c, ALU.mult).then_inc(s_astep[1], 1)
                    waits((s_astep[1], step + 1))
                    nc.gpsimd.tensor_tensor(w[:, 0:HALF // 2], w[:, 0:HALF // 2], w[:, HALF // 2:HALF], ALU.add).then_inc(s_astep[1], 1)
                    waits((s_astep[1], step + 2))
                    out = w[:, 0:UW] if hf else acc
                    nc.gpsimd.tensor_tensor(out, w[:, 0:UW], w[:, UW:2 * UW], ALU.add).then_inc(s_astep[1], 1)
                    step = step + 3
                waits((s_astep[1], step))
                nc.gpsimd.tensor_tensor(acc, acc, w[:, 0:UW], ALU.add).then_inc(s_astep[1], 1)

            def pair_rows(layer, i, r, more, u, n):
                gp = PAIRS * layer + 2 * i + r

                def norm(st):
                    for s in range(2):
                        pr = prob[st % 2][s][:, 0:P * (st + 1)]
                        k = 2 * st + s
                        if st == 0 and s == 0:
                            before = (s_vlo, gp + 1)
                        elif st == 2 and s == 0 and more:
                            before = (s_wlo, 2 * u + 2)
                        else:
                            before = (s_norm, 8 * gp + k)
                        waits((s_rinv, 4 * gp + st + 1), before)
                        nc.gpsimd.tensor_scalar(pr, pr, rinv[:, st % 2, s:s + 1], 1.0, ALU.mult, ALU.mult).then_inc(s_norm, 1)

                waits((s_vhi, gp + 1), (s_norm, 8 * gp))
                nc.gpsimd.tensor_tensor(vs_lo[:], v_tok[:, :, bass.ds(P * (2 * i + r), P)], vs_hi[:].bitcast(F32), ALU.subtract).then_inc(s_vlo, 1)
                norm(0)
                norm(1)
                if more:
                    slot = r
                    for hf in range(2):
                        a, b = hf * (n // 2), (hf + 1) * (n // 2)
                        waits((s_whi, 2 * u + hf + 1), (s_wlo, 2 * u + 1) if hf else (s_norm, 8 * gp + 4))
                        nc.gpsimd.tensor_tensor(w_lo[:, slot, a:b], w_raw[:, a:b], w_hi[:, slot, a:b].bitcast(F32), ALU.subtract).then_inc(s_wlo, 1)
                norm(2)
                norm(3)

            pool.wait_ge(s_zero, 2)
            pool.wait_ge(s_cact, 3)
            for a in ADA_GP:
                idx, slot = ada_own(a)[1], ADA_SLOT[a]
                uses = 16 * sum(ADA_SLOT[b] == slot for b in range(a + 1))
                ada_sum(a, idx, idx % 2, ada_slots[slot], lambda hf: (s_ast[slot], uses))
            for layer, u0, n, then in ((0, U_QK, UNIT, U_FOUT), (1, U_MQK, MQK_W, U_MOUT)):
                waits((s_astep[1], 7 * (6 + 24 * layer)))
                with pool.Fori(0, 3) as i:
                    for r in range(2):
                        pair_rows(layer, i, r, True, u0 + 2 * i + r + 2, n)
                pair_rows(layer, 3, 0, True, then, UNIT)
                pair_rows(layer, 3, 1, False, None, None)
                if layer == 0:
                    waits((s_norm, 8 * PAIRS))
                    with pool.Fori(0, GROUPS) as g:
                        for k in range(6):
                            a = 24 + 6 * g + k
                            ada_sum(a, 6 + 6 * g + k, k % 2, ada_slots[0], lambda hf: (s_ain[hf], 16 * (a - ADA_EARLY + 1)))

        @block.scalar
        def _(act):
            def split_hi(u, n=UNIT, used=None):
                if used is not None:
                    act.wait_ge(*used)
                for hf in range(2):
                    a, b = hf * (n // 2), (hf + 1) * (n // 2)
                    act.wait_ge(s_win[hf], 16 * u + 16)
                    nc.scalar.activation(w_hi[:, slot_of[0], a:b], w_raw[:, a:b], ACT.Copy).then_inc(s_whi, 1)
                slot_of[0] ^= 1

            slot_of = [0]

            def rstd(out, width, k):
                if k:
                    act.wait_ge(s_warm, k)
                nc.scalar.activation(warm[:], ones[:, 0:1], ACT.Ln).then_inc(s_warm, 1)
                act.wait_ge(s_ss, k + 1)
                nc.scalar.activation(out, T_BANK[1][:], ACT.Ln, bias=cc[:, CC_EPS:CC_EPS + 1], scale=1.0 / width).then_inc(s_ln, 1)
                act.wait_ge(s_ln, k + 1)
                nc.scalar.activation(out, out, ACT.Exp, scale=-0.5).then_inc(s_rstd, 1)

            def squares(n, c):
                if c >= 2:
                    act.wait_ge(s_acc, 7 * n + max(1, c - 2))
                nc.scalar.activation(sc[:, 4 + c % 2, :], x[:, c, :], ACT.Square).then_inc(s_sq, 1)

            def h_chunks(n, layer, what):
                sh = mcols(layer, what)
                for c in range(C):
                    act.wait_ge(s_tm, C * n + c + 1)
                    nc.scalar.activation(h_hi[:, c, :], sc[:, 4 + c % 2, :], ACT.Identity, bias=sh[:, c:c + 1]).then_inc(s_hhi, 1)

            act.wait_ge(s_cin, 32)
            nc.scalar.activation(ctmp[:, 0, :], cv[:, CV_C:CV_C + C], ACT.Exp, scale=-1.0).then_inc(s_csil, 1)
            nc.scalar.activation(id_b[:], ident, ACT.Copy).then_inc(s_bf, 1)
            nc.scalar.activation(mask_b[:], cc[:, CC_MASK:CC_MASK + P], ACT.Copy).then_inc(s_bf, 1)
            act.wait_ge(s_xin, 16)
            for c in range(C):
                squares(0, c)
            act.wait_ge(s_fin, 16)
            nc.scalar.activation(wf_hi[:, :, :].rearrange("p c h -> p (c h)"), wf_raw[:], ACT.Copy).then_inc(s_wf, 1)
            split_hi(0)
            rstd(sc[:, 7, :], D, 0)
            h_chunks(0, 0, "sh_m")
            for n in range(4):
                split_hi(n + 1, used=(s_tile, D_V + 4 * n) if n else None)

            z, za, ze, zl = (pe_[F_AT:F_AT + HEADS, k, :] for k in range(4))
            act.wait_ge(s_fmm, 1)
            nc.scalar.activation(z, T_BANK[0][0:HEADS, :], ACT.Identity, bias=cv[0:HEADS, CV_BF:CV_BF + 1]).then_inc(s_fa, 1)
            act.wait_ge(s_fa, 1)
            nc.scalar.activation(za, z, ACT.Abs).then_inc(s_fa, 1)
            act.wait_ge(s_fa, 2)
            nc.scalar.activation(ze, za, ACT.Exp, scale=-1.0).then_inc(s_fa, 1)
            act.wait_ge(s_fa, 3)
            nc.scalar.activation(zl, ze, ACT.Ln, bias=ones[F_AT:F_AT + HEADS, 0:1]).then_inc(s_fa, 1)
            act.wait_ge(s_fd, 3)
            nc.scalar.activation(f_rows[0], za, ACT.Copy, scale=-1.0).then_inc(s_fr, 1)

            def q_hi(layer, gp, first=False):
                scale = FOX_SCALE if layer == 0 else MLA_SCALE
                act.wait_ge(s_pq, gp + 1)
                if not first:
                    act.wait_ge(s_score, 8 * gp)
                for s in range(2):
                    nc.scalar.activation(qa[s][0:HD, :], PQ[s * HD:(s + 1) * HD, :], ACT.Copy, scale=scale).then_inc(s_qhi, 1)

            def k_hi(layer, gp):
                act.wait_ge(s_pk, gp + 1)
                for s in range(2):
                    nc.scalar.activation(ka[s][0:HD, :], PK[s * HD:(s + 1) * HD, :], ACT.Copy).then_inc(s_khi, 1)

            def exps(gp, st):
                for s in range(2):
                    n = P * (st + 1)
                    act.wait_ge(s_max, 2 * (4 * gp + st) + s + 1)
                    if st >= 2:
                        act.wait_ge(s_tr, 2 * (4 * gp + st) + s - 3)
                    nc.scalar.activation(prob[st % 2][s][:, 0:n], S_BANK[st % 2][s][:, 0:n], ACT.Exp,
                                         bias=nmax[:, st % 2, s:s + 1], accum_out=rsum[:, st % 2, s:s + 1]).then_inc(s_exp, 1)

            def pt_his(gp, st):
                for s in range(2):
                    act.wait_ge(s_tr, 2 * (4 * gp + st) + s + 1)
                    nc.scalar.activation(pt(s, pt_hi, st, st + 1), T_BANK[s][:, 0:P * (st + 1)].rearrange("p (j c) -> p j c", c=P),
                                         ACT.Copy).then_inc(s_pthi, 1)

            def attn(layer, i, r, more, unit):
                gp = PAIRS * layer + 2 * i + r
                act.wait_ge(s_pv, 2 * gp)
                nc.scalar.activation(vs_hi[:], v_tok[:, :, bass.ds(P * (2 * i + r), P)], ACT.Copy).then_inc(s_vhi, 1)
                exps(gp, 0)
                exps(gp, 1)
                if more:
                    split_hi(*unit, used=(s_pk, gp + 1))
                pt_his(gp, 0)
                exps(gp, 2)
                pt_his(gp, 1)
                exps(gp, 3)
                if more:
                    q_hi(layer, gp + 1)
                pt_his(gp, 2)
                pt_his(gp, 3)
                if more:
                    k_hi(layer, gp + 1)
                for s in range(2):
                    act.wait_ge(s_pv, 2 * gp + s + 1)
                    rows = slice(s * HD, (s + 1) * HD)
                    nc.scalar.activation(o_hi[rows, bass.ds(2 * i + r, 1), :].rearrange("p a t -> p (a t)"), S_BANK[1][s][rows, :], ACT.Copy).then_inc(s_ohi, 1)

            def attn_layer(layer, u0, n, then):
                split_hi(u0 + 1, n, used=(s_tile, D_MOUT if layer else D_FOUT))
                q_hi(layer, PAIRS * layer, first=(layer == 0))
                k_hi(layer, PAIRS * layer)
                with act.Fori(0, 3) as i:
                    for r in range(2):
                        attn(layer, i, r, True, (u0 + 2 * i + r + 2, n))
                attn(layer, 3, 0, True, (then, UNIT))
                attn(layer, 3, 1, False, None)

            def out_proj(layer, u0, d, td):
                n = 2 * layer + 1
                for k in range(4):
                    split_hi(u0 + k + 1, used=(s_tile, d + 2 * k) if k else (s_pk, PAIRS * (layer + 1)))
                    for c in (2 * k, 2 * k + 1):
                        act.wait_ge(s_tdve, td + c + 1)
                        squares(n, c)
                rstd(sc[:, 7, :], D, n + 2 * (n > 2))
                h_chunks(n, layer, "sh_f")

            def mlp_group(layer, g, last, after_u):
                base = 32 * layer + 8 * g
                for k in range(8):
                    used = (s_tile, D_MLP[layer] + 16 * g + 2 * k)
                    if not (last and k == 7):
                        split_hi(U_MLP[layer] + 8 * g + k + 1, used=used)
                    elif after_u:
                        split_hi(*after_u, used=used)
                    if layer == 0 and last and k == 7:
                        act.wait_ge(s_trig, 8)
                        nc.scalar.activation(sin_t, adab[:, 2, :], ACT.Sin).then_inc(s_triga, 1)
                        act.wait_ge(s_trig, 12)
                        nc.scalar.activation(cos_t, adab[:, 3, :], ACT.Sin).then_inc(s_triga, 1)
                    for j in (2 * k, 2 * k + 1):
                        if k < 4:
                            act.wait_ge(s_tile, D_MLP[layer] + 16 * g + j + 1)
                            nc.scalar.activation(sc[:, j % 2, :], ps[j % RING][:], ACT.Relu).then_inc(s_tact, 1)
                            act.wait_ge(s_sqr, base + j + 1)
                            nc.scalar.activation(o_hi[:, j, :], sc[:, 2 + j % 2, :], ACT.Copy).then_inc(s_ahi, 1)
                        elif last:
                            c = j - 8
                            act.wait_ge(s_tdve, TD_MLP[layer] + 8 * g + c + 1)
                            squares(2 * layer + 2, c)

            def mlp(layer, after_u):
                with act.Fori(0, GROUPS - 1) as g:
                    mlp_group(layer, g, False, None)
                mlp_group(layer, GROUPS - 1, True, after_u)

            attn_layer(0, U_QK, UNIT, U_FOUT)
            out_proj(0, U_FOUT, D_FOUT, TD_FOUT)
            mlp(0, (U_DKV, C * 160))
            rstd(sc[:, 7, :], D, 2)
            h_chunks(2, 1, "sh_m")
            split_hi(U_DQ, used=(s_tile, D_DKV))
            ckv_raw, cq_raw, cq_n = prob[0][0], (prob[0][1], prob[1][0]), (prob[0][0], prob[1][1])
            act.wait_ge(s_tdve, TD_DKV + 1)
            nc.scalar.activation(sc[:, 4, :], ckv_raw, ACT.Square).then_inc(s_rpa, 1)
            act.wait_ge(s_kr, 3)
            nc.scalar.activation(qa[0][0:ROPE, :], sc[0:ROPE, 1, :], ACT.Copy).then_inc(s_rpa, 1)
            rstd(sc[:, 6, :], KVR, 3)
            split_hi(U_MV, D, used=(s_tile, D_DQ))
            act.wait_ge(s_rope, 1)
            nc.scalar.activation(o_hi[:, 7, :], sc[:, 5, :], ACT.Copy).then_inc(s_rpa, 1)
            act.wait_ge(s_kr, 4)
            for s in range(2):
                nc.scalar.activation(ka[s][HD:MLA_K, :], qa[0][0:ROPE, :].bitcast(F32), ACT.Copy).then_inc(s_rpa, 1)
                nc.scalar.activation(kb[s][HD:MLA_K, :], qa[1][0:ROPE, :].bitcast(F32), ACT.Copy).then_inc(s_rpa, 1)
            for k in range(2):
                act.wait_ge(s_tdve, TD_DKV + 3 + k)
                nc.scalar.activation(adab[:, 2 + k, :], cq_raw[k], ACT.Square).then_inc(s_rpa, 1)
            rstd(adab[:, 3, :], QR, 4)
            for k in range(2):
                act.wait_ge(s_rope, 4 + k)
                nc.scalar.activation(h_hi[:, k, :], cq_n[k], ACT.Copy).then_inc(s_rpa, 1)
            split_hi(U_QROPE, 2 * T, used=(s_tile, D_MV))
            split_hi(U_MQK, MQK_W, used=(s_tile, D_QROPE))
            for k in range(TB):
                act.wait_ge(s_qra, 3 * k + 3)
                nc.scalar.activation(h_hi[:, 2 + k, :], adab[:, 2, :], ACT.Copy, scale=MLA_SCALE).then_inc(s_rpa, 1)
            attn_layer(1, U_MQK, MQK_W, U_MOUT)
            out_proj(1, U_MOUT, D_MOUT, TD_MOUT)
            mlp(1, None)
            rstd(prob[0][0], D, 6)

        @block.vector
        def _(dve):
            slot_of = [0]

            def split_lo(u, n=UNIT):
                for hf in range(2):
                    a, b = hf * (n // 2), (hf + 1) * (n // 2)
                    dve.wait_ge(s_whi, 2 * u + hf + 1)
                    nc.vector.tensor_tensor(w_lo[:, slot_of[0], a:b], w_raw[:, a:b], w_hi[:, slot_of[0], a:b].bitcast(F32),
                                            ALU.subtract).then_inc(s_wlo, 1)
                slot_of[0] ^= 1

            def ada_sum(a, idx, par, k0=0, k1=C):
                early = isinstance(a, int) and a < ADA_EARLY
                slot = ADA_SLOT[a] if early else 0
                if k0 == 0 and not (isinstance(idx, int) and idx < 2):
                    dve.wait_ge(s_adamm, a - 1)
                for k in range(k0, k1):
                    if early and k == 0:
                        dve.wait_ge(s_ast[slot], 16 * sum(ADA_SLOT[b] == slot for b in range(a + 1)))
                    elif not early and k % 4 == 0:
                        dve.wait_ge(s_ain[k // 4], 16 * (a - ADA_EARLY + 1))
                    w = ada_slots[slot][:, k * UW:(k + 1) * UW]
                    acc = adaacc[:, par, :]
                    if k == 0:
                        nc.vector.tensor_scalar(acc, w, cact[:, 0:1], None, ALU.mult).then_inc(s_astep[0], 1)
                    else:
                        dve.wait_ge(s_astep[0], 8 * idx + k)
                        nc.vector.scalar_tensor_tensor(out=acc, in0=w, scalar=cact[:, k:k + 1], in1=acc,
                                                       op0=ALU.mult, op1=ALU.add).then_inc(s_astep[0], 1)

            def ada_early(a):
                idx = ada_own(a)[1]
                ada_sum(a, idx, idx % 2)

            def ada_add(a, n=1):
                dve.wait_ge(s_adamm, a + n)
                nc.vector.tensor_tensor(mod[:, bass.ds(2 * a, 2 * n)], ps[7][:, 0:2 * n], cv[:, bass.ds(CV_ADAB + 2 * a, 2 * n)],
                                        ALU.add).then_inc(s_mod, n)

            def sum_square(n, c):
                if c == 0:
                    return
                dve.wait_ge(s_sq, C * n + c + 1)
                if c > 1:
                    dve.wait_ge(s_acc, 7 * n + c - 1)
                a = sc[:, 4, :] if c == 1 else sc[:, 6, :]
                nc.vector.tensor_tensor(sc[:, 6, :], a, sc[:, 4 + c % 2, :], ALU.add).then_inc(s_acc, 1)

            def gain_col(n, gain, layer, what, mods):
                dve.wait_ge(s_mod, mods)
                nc.vector.scalar_tensor_tensor(out=acol[:], in0=mcols(layer, what), scalar=1.0, in1=cv[:, gain:gain + C],
                                               op0=ALU.add, op1=ALU.mult).then_inc(s_acol, 1)

            def h_chunks(n, layer, what, rk):
                sh = mcols(layer, what)

                def lo(c):
                    dve.wait_ge(s_hhi, C * n + c + 1)
                    nc.vector.scalar_tensor_tensor(out=h_lo[:, c, :], in0=sc[:, 4 + c % 2, :], scalar=sh[:, c:c + 1],
                                                   in1=h_hi[:, c, :].bitcast(F32), op0=ALU.add, op1=ALU.subtract).then_inc(s_hlo, 1)

                dve.wait_ge(s_rstd, rk + 1)
                dve.wait_ge(s_acol, n + 1)
                for c in range(C):
                    if c >= 2:
                        dve.wait_ge(s_hlo, C * n + c - 1)
                    nc.vector.scalar_tensor_tensor(out=sc[:, 4 + c % 2, :], in0=x[:, c, :], scalar=acol[:, c:c + 1], in1=sc[:, 7, :],
                                                   op0=ALU.mult, op1=ALU.mult).then_inc(s_tm, 1)
                    if c >= 1:
                        lo(c - 1)
                lo(C - 1)

            dve.wait_ge(s_csil, 1)
            nc.vector.tensor_scalar(ctmp[:, 1, :], ctmp[:, 0, :], 1.0, None, ALU.add).then_inc(s_cact, 1)
            dve.wait_ge(s_cact, 1)
            nc.vector.reciprocal(ctmp[:, 2, :], ctmp[:, 1, :]).then_inc(s_cact, 1)
            dve.wait_ge(s_cact, 2)
            nc.vector.tensor_tensor(cact[:], ctmp[:, 2, :], cv[:, CV_C:CV_C + C], ALU.mult).then_inc(s_cact, 1)
            dve.wait_ge(s_cact, 3)
            for a in (0, 2, 3):
                ada_early(a)
            for c in range(C):
                sum_square(0, c)
            ada_early(5)
            ada_add(0, 4)
            gain_col(0, CV_GMIX, 0, "sc_m", 4)
            ada_early(6)
            ada_early(7)
            dve.wait_ge(s_wf, 1)
            nc.vector.tensor_tensor(wf_lo[:, :, :].rearrange("p c h -> p (c h)"), wf_raw[:],
                                    wf_hi[:, :, :].rearrange("p c h -> p (c h)").bitcast(F32), ALU.subtract).then_inc(s_wf, 1)
            ada_add(4, 4)
            split_lo(0)
            h_chunks(0, 0, "sh_m", 0)

            for n in range(4):
                split_lo(n + 1)
                for tk in range(TB):
                    dve.wait_ge(s_tile, D_V + 4 * n + tk + 1)
                    nc.vector.tensor_copy(v_tok[:, tk, n * UW:(n + 1) * UW], ps[tk][:, 0:UW]).then_inc(s_tdve, 1)
                    a = ADA_START + 2 * n
                    if tk == 0:
                        ada_early(a + 1)
                    if tk == 3:
                        ada_add(a, 2 if n < 3 else 1)

            z, za, ze, zl = (pe_[F_AT:F_AT + HEADS, k, :] for k in range(4))
            dve.wait_ge(s_fa, 4)
            nc.vector.tensor_scalar(ze, z, 0.0, None, ALU.min).then_inc(s_fd, 1)
            dve.wait_ge(s_fd, 1)
            nc.vector.tensor_tensor(ze, ze, zl, ALU.subtract).then_inc(s_fd, 1)
            dve.wait_ge(s_fd, 2)
            nc.vector.tensor_tensor_scan(za, ze, ze, 0.0, ALU.add, ALU.bypass).then_inc(s_fd, 1)
            dve.wait_ge(s_fr, 1)
            nc.vector.scalar_tensor_tensor(out=f_rows[1], in0=za, scalar=-1.0, in1=f_rows[0].bitcast(F32),
                                           op0=ALU.mult, op1=ALU.subtract).then_inc(s_fr, 1)

            def q_lo(layer, gp):
                scale = FOX_SCALE if layer == 0 else MLA_SCALE
                for s in range(2):
                    dve.wait_ge(s_qhi, 2 * gp + s + 1)
                    out = qa[s][HD:P, :] if layer == 0 else qb[s][0:HD, :]
                    nc.vector.scalar_tensor_tensor(out=out, in0=PQ[s * HD:(s + 1) * HD, :], scalar=scale, in1=qa[s][0:HD, :].bitcast(F32),
                                                   op0=ALU.mult, op1=ALU.subtract).then_inc(s_qlo, 1)

            def k_lo(layer, gp):
                for s in range(2):
                    dve.wait_ge(s_khi, 2 * gp + s + 1)
                    nc.vector.tensor_tensor(kb[s][0:HD, :], PK[s * HD:(s + 1) * HD, :], ka[s][0:HD, :].bitcast(F32), ALU.subtract).then_inc(s_klo, 1)

            def maxes(gp, st):
                for s in range(2):
                    dve.wait_ge(s_score, 2 * (4 * gp + st) + s + 1)
                    nc.vector.tensor_reduce(nmax[:, st % 2, s:s + 1], S_BANK[st % 2][s][:, 0:P * (st + 1)], AXX, ALU.max,
                                            negate=True).then_inc(s_max, 1)

            def rinvs(gp, st):
                dve.wait_ge(s_exp, 2 * (4 * gp + st) + 2)
                nc.vector.reciprocal(rinv[:, st % 2, :], rsum[:, st % 2, :]).then_inc(s_rinv, 1)

            def pt_los(gp, st):
                for s in range(2):
                    dve.wait_ge(s_pthi, 2 * (4 * gp + st) + s + 1)
                    nc.vector.tensor_tensor(pt(s, pt_lo, st, st + 1), T_BANK[s][:, 0:P * (st + 1)].rearrange("p (j c) -> p j c", c=P),
                                            pt(s, pt_hi, st, st + 1).bitcast(F32), ALU.subtract).then_inc(s_ptlo, 1)

            def attn(layer, i, r, more, a):
                gp = PAIRS * layer + 2 * i + r
                maxes(gp, 0)
                maxes(gp, 1)
                rinvs(gp, 0)
                if a is not None:
                    ada_add(a - 1)
                rinvs(gp, 1)
                if a is not None:
                    ada_sum(a, a - 6, r, 0, 4)
                maxes(gp, 2)
                maxes(gp, 3)
                pt_los(gp, 0)
                rinvs(gp, 2)
                pt_los(gp, 1)
                rinvs(gp, 3)
                if more:
                    q_lo(layer, gp + 1)
                pt_los(gp, 2)
                pt_los(gp, 3)
                if a is not None:
                    ada_sum(a, a - 6, r, 4, 8)
                if more:
                    k_lo(layer, gp + 1)
                for s in range(2):
                    dve.wait_ge(s_ohi, 2 * gp + s + 1)
                    rows = slice(s * HD, (s + 1) * HD)
                    hi = o_hi[rows, bass.ds(2 * i + r, 1), :].rearrange("p a t -> p (a t)").bitcast(F32)
                    lo = o_lo[rows, bass.ds(2 * i + r, 1), :].rearrange("p a t -> p (a t)")
                    nc.vector.tensor_tensor(lo, S_BANK[1][s][rows, :], hi, ALU.subtract).then_inc(s_olo, 1)

            def attn_layer(layer, u0, n):
                split_lo(u0 + 1, n)
                q_lo(layer, PAIRS * layer)
                k_lo(layer, PAIRS * layer)
                a0 = ADA_START + 8 if layer == 0 else None
                with dve.Fori(0, 3) as i:
                    for r in range(2):
                        attn(layer, i, r, True, None if a0 is None else a0 + 2 * i + r)
                attn(layer, 3, 0, True, None if a0 is None else a0 + 6)
                attn(layer, 3, 1, False, None if a0 is None else a0 + 7)
                if layer == 0:
                    ada_add(a0 + 7)

            def gated_add(layer, what, j, c):
                g = mcols(layer, what)
                nc.vector.scalar_tensor_tensor(out=x[:, c, :], in0=ps[j % RING][:], scalar=g[:, c:c + 1], in1=x[:, c, :],
                                               op0=ALU.mult, op1=ALU.add).then_inc(s_tdve, 1)

            def out_proj(layer, u0, d):
                slot_of[0] = (u0 + 1) % 2
                n = 2 * layer + 1
                for k in range(4):
                    split_lo(u0 + k + 1)
                    for c in (2 * k, 2 * k + 1):
                        dve.wait_ge(s_tile, d + c + 1)
                        gated_add(layer, "g_m", c, c)
                        if c:
                            sum_square(n, c - 1)
                sum_square(n, C - 1)
                gain_col(n, CV_GMLP + C * layer, layer, "sc_f", 24 if layer == 0 else ADA_UNITS)
                h_chunks(n, layer, "sh_f", n + 2 * (n > 2))

            def mlp_group(layer, g, last, after_u):
                base = 32 * layer + 8 * g
                a = 24 + 6 * g
                for k in range(8):
                    if not (last and k == 7):
                        split_lo(U_MLP[layer] + 8 * g + k + 1)
                    elif after_u:
                        split_lo(*after_u)
                    if layer == 0 and last and k == 7:
                        trig_tables()
                    for j in (2 * k, 2 * k + 1):
                        dve.wait_ge(s_tile, D_MLP[layer] + 16 * g + j + 1) if k >= 4 else dve.wait_ge(s_tact, base + j + 1)
                        if k < 4:
                            nc.vector.tensor_tensor(sc[:, 2 + j % 2, :], sc[:, j % 2, :], sc[:, j % 2, :], ALU.mult).then_inc(s_sqr, 1)
                            dve.wait_ge(s_ahi, base + j + 1)
                            nc.vector.tensor_tensor(o_lo[:, j, :], sc[:, 2 + j % 2, :], o_hi[:, j, :].bitcast(F32), ALU.subtract).then_inc(s_alo, 1)
                        else:
                            c = j - 8
                            gated_add(layer, "g_f", j, c)
                            if last and c:
                                sum_square(2 * layer + 2, c - 1)
                        if layer == 0 and 0 < k < 7 and j % 2 == 0:
                            ada_add(a + k - 1)
                if last:
                    sum_square(2 * layer + 2, C - 1)

            def trig_tables():
                k, r = adab[:, 3, :], adab[:, 2, :]
                pi = 3.1415925
                dve.wait_ge(s_posin, 16)
                nc.vector.tensor_copy(k, adab[:, 2, :].bitcast(I32)).then_inc(s_trig, 1)
                dve.wait_ge(s_trig, 1)
                nc.vector.tensor_scalar(r, k, cc[:, CC_FREQ:CC_FREQ + 1], None, ALU.mult).then_inc(s_trig, 1)
                dve.wait_ge(s_trig, 2)
                nc.vector.tensor_scalar(k, r, INV_2PI, ROUND, ALU.mult, ALU.add).then_inc(s_trig, 1)
                dve.wait_ge(s_trig, 3)
                nc.vector.tensor_scalar(k, k, ROUND, None, ALU.subtract).then_inc(s_trig, 1)
                for n, part in enumerate(TWO_PI_PARTS):
                    dve.wait_ge(s_trig, 4 + n)
                    nc.vector.scalar_tensor_tensor(out=r, in0=k, scalar=-part, in1=r, op0=ALU.mult, op1=ALU.add).then_inc(s_trig, 1)
                dve.wait_ge(s_trig, 7)
                nc.vector.tensor_scalar(r, r, pi, -pi, ALU.min, ALU.max).then_inc(s_trig, 1)
                dve.wait_ge(s_trig, 8)
                nc.vector.tensor_scalar(k, r, 0.5 * math.pi, None, ALU.add).then_inc(s_trig, 1)
                dve.wait_ge(s_trig, 9)
                nc.vector.tensor_scalar(cos_t, k, math.pi, -2 * math.pi, ALU.is_gt, ALU.mult).then_inc(s_trig, 1)
                dve.wait_ge(s_trig, 10)
                nc.vector.tensor_tensor(k, k, cos_t, ALU.add).then_inc(s_trig, 1)
                dve.wait_ge(s_trig, 11)
                nc.vector.tensor_scalar(k, k, pi, -pi, ALU.min, ALU.max).then_inc(s_trig, 1)
                dve.wait_ge(s_triga, 1)
                nc.vector.tensor_scalar(sin_t, sin_t, cc[:, CC_SIGN:CC_SIGN + 1], None, ALU.mult).then_inc(s_trig, 1)

            def mlp(layer, after_u):
                with dve.Fori(0, GROUPS - 1) as g:
                    mlp_group(layer, g, False, None)
                mlp_group(layer, GROUPS - 1, True, after_u)

            attn_layer(0, U_QK, UNIT)
            out_proj(0, U_FOUT, D_FOUT)
            mlp(0, (U_DKV, C * 160))
            gain_col(2, CV_GMIX + C, 1, "sc_m", ADA_UNITS)
            h_chunks(2, 1, "sh_m", 2)
            split_lo(U_DQ)

            ckv_raw, cq_raw, cq_n = prob[0][0], (prob[0][1], prob[1][0]), (prob[0][0], prob[1][1])
            swap = [(m + ROPE // 2) % ROPE for m in range(ROPE)]
            krot, ksum = sc[0:ROPE, 0, :], sc[0:ROPE, 1, :]
            dve.wait_ge(s_tile, D_DKV + 1)
            nc.vector.tensor_copy(ckv_raw, ps[0][:]).then_inc(s_tdve, 1)
            dve.wait_ge(s_tile, D_DKV + 2)
            nc.vector.stream_shuffle(krot, ps[1][0:ROPE, :], swap).then_inc(s_kr, 1)
            dve.wait_ge(s_triga, 2)
            nc.vector.tensor_tensor(ksum, ps[1][0:ROPE, :], cos_t[0:ROPE, :], ALU.mult).then_inc(s_tdve, 1)
            dve.wait_ge(s_kr, 1)
            dve.wait_ge(s_trig, 13)
            nc.vector.tensor_tensor(krot, krot, sin_t[0:ROPE, :], ALU.mult).then_inc(s_kr, 1)
            dve.wait_ge(s_kr, 2)
            dve.wait_ge(s_tdve, TD_DKV + 2)
            nc.vector.tensor_tensor(ksum, ksum, krot, ALU.add).then_inc(s_kr, 1)
            dve.wait_ge(s_rstd, 4)
            nc.vector.scalar_tensor_tensor(out=sc[:, 5, :], in0=ckv_raw, scalar=cv[:, CV_GKV:CV_GKV + 1], in1=sc[:, 6, :],
                                           op0=ALU.mult, op1=ALU.mult).then_inc(s_rope, 1)
            dve.wait_ge(s_rpa, 2)
            nc.vector.tensor_tensor(qa[1][0:ROPE, :], ksum, qa[0][0:ROPE, :].bitcast(F32), ALU.subtract).then_inc(s_kr, 1)
            split_lo(U_MV, D)
            dve.wait_ge(s_rpa, 3)
            nc.vector.tensor_tensor(o_lo[:, 7, :], sc[:, 5, :], o_hi[:, 7, :].bitcast(F32), ALU.subtract).then_inc(s_rope, 1)
            for k in range(2):
                dve.wait_ge(s_tile, D_DQ + 1 + k)
                nc.vector.tensor_copy(cq_raw[k], ps[2 + k][:]).then_inc(s_tdve, 1)

            def v_tile(n):
                tk, half = n // 2, n % 2
                dve.wait_ge(s_tile, D_MV + n + 1)
                nc.vector.tensor_copy(v_tok[:, tk, half * T:(half + 1) * T], ps[n % RING][:]).then_inc(s_tdve, 1)

            v_tile(0)
            dve.wait_ge(s_rpa, 9)
            nc.vector.tensor_tensor(adab[:, 2, :], adab[:, 2, :], adab[:, 3, :], ALU.add).then_inc(s_rope, 1)
            for n in range(1, 5):
                v_tile(n)
            dve.wait_ge(s_rstd, 5)
            for k in range(2):
                nc.vector.scalar_tensor_tensor(out=cq_n[k], in0=cq_raw[k], scalar=cv[:, CV_GQ + k:CV_GQ + k + 1], in1=adab[:, 3, :],
                                               op0=ALU.mult, op1=ALU.mult).then_inc(s_rope, 1)
            for k in range(2):
                dve.wait_ge(s_rpa, 10 + k)
                nc.vector.tensor_tensor(h_lo[:, k, :], cq_n[k], h_hi[:, k, :].bitcast(F32), ALU.subtract).then_inc(s_rope, 1)
            for n in range(5, 8):
                v_tile(n)
            split_lo(U_QROPE, 2 * T)
            split_lo(U_MQK, MQK_W)
            for k in range(TB):
                a, b = adab[:, 2, :], adab[:, 3, :]
                dve.wait_ge(s_tile, D_QROPE + k + 1)
                nc.vector.stream_shuffle(b, ps[k][:], swap).then_inc(s_qra, 1)
                if k:
                    dve.wait_ge(s_qrd, k)
                nc.vector.tensor_tensor(a, ps[k][:], cos_t, ALU.mult).then_inc(s_tdve, 1)
                dve.wait_ge(s_qra, 3 * k + 1)
                nc.vector.tensor_tensor(b, b, sin_t, ALU.mult).then_inc(s_qra, 1)
                dve.wait_ge(s_tdve, TD_DKV + 13 + k)
                dve.wait_ge(s_qra, 3 * k + 2)
                nc.vector.tensor_tensor(a, a, b, ALU.add).then_inc(s_qra, 1)
                dve.wait_ge(s_rpa, 12 + k)
                nc.vector.scalar_tensor_tensor(out=h_lo[:, 2 + k, :], in0=a, scalar=MLA_SCALE, in1=h_hi[:, 2 + k, :].bitcast(F32),
                                               op0=ALU.mult, op1=ALU.subtract).then_inc(s_qrd, 1)

            attn_layer(1, U_MQK, MQK_W)
            out_proj(1, U_MOUT, D_MOUT)
            mlp(1, None)
            dve.wait_ge(s_rstd, 7)
            for c in range(C):
                nc.vector.scalar_tensor_tensor(out=sc[:, c, :], in0=x[:, c, :], scalar=cv[:, CV_GFIN + c:CV_GFIN + c + 1], in1=prob[0][0],
                                               op0=ALU.mult, op1=ALU.mult).then_inc(s_yn, 1)

        @block.tensor
        def _(pe):
            def product(out, lhs, rhs, start, stop):
                nc.tensor.matmul(out, lhs[0], rhs[0], start=start, stop=False)
                nc.tensor.matmul(out, lhs[1], rhs[0], start=False, stop=False)
                return nc.tensor.matmul(out, lhs[0], rhs[1], start=False, stop=stop)

            def w_view(slot, kc, n):
                return [w[:, slot, 0:kc * n].rearrange("p (k n) -> p k n", k=kc) for w in (w_hi, w_lo)]

            def w_ready(u):
                pe.wait_ge(s_wlo, 2 * u + 2)

            def bank_free(first, n, td):
                pe.wait_ge(s_tdve, td + n - 3)

            def ada_mm(a, own, idx, par, col=0):
                pe.wait_ge(s_astep[own], ADA_STEPS[own] * (idx + 1))
                if col == 0 and not (isinstance(a, int) and a == 0):
                    pe.wait_ge(s_mod, a)
                for j in range(2):
                    mm = nc.tensor.matmul(ps[7][:, col + j:col + j + 1], adaacc[:, 2 * own + par, j * P:(j + 1) * P], ones[:, 0:1],
                                          start=True, stop=True)
                mm.then_inc(s_adamm, 1)

            def ada_early(a, col):
                own, idx = ada_own(a)
                ada_mm(a, own, idx, idx % 2, col)

            def sum_over_features(src):
                nc.tensor.matmul(T_BANK[1][:], ones[:], src, start=True, stop=True).then_inc(s_ss, 1)

            pe.wait_ge(s_ones, 1)
            for a in range(ADA_START):
                ada_early(a, 2 * (a % 4))
                if a == 3:
                    pe.wait_ge(s_acc, 7)
                    sum_over_features(sc[:, 6, :])

            for n in range(4):
                w = w_view(n % 2, C, UW)
                w_ready(U_V + n)

                def part(tk, k):
                    return product(ps[tk][:, 0:UW], [h[:, k, tk * P:(tk + 1) * P] for h in (h_hi, h_lo)],
                                   [v[:, k, :] for v in w], k == 0, k == C - 1)

                if n == 0:
                    for k in range(C):
                        pe.wait_ge(s_hlo, k + 1)
                        for tk in range(TB):
                            mm = part(tk, k)
                            if k == C - 1:
                                mm.then_inc(s_tile, 1)
                for tk in range(TB):
                    if n:
                        pe.wait_ge(s_tdve, 4 * n + tk - RING + 1)
                        for k in range(C):
                            mm = part(tk, k)
                        mm.then_inc(s_tile, 1)
                    if tk == 2:
                        ada_early(ADA_START + 2 * n, 0)
                        if n < 3:
                            ada_early(ADA_START + 2 * n + 1, 2)
            pe.wait_ge(s_wf, 2)
            for k in range(C):
                mm = product(T_BANK[0][0:HEADS, :], [w[:, k, :] for w in (wf_hi, wf_lo)], [h[:, k, :] for h in (h_hi, h_lo)],
                             k == 0, k == C - 1)
            mm.then_inc(s_fmm, 1)

            def q_part(layer, slot, k0, k1):
                if layer == 0:
                    w, n, at = w_view(slot, C, UW), C, 0
                else:
                    w, n, at = w_view(slot, 3, P), 2, 0
                for k in range(k0, min(k1, n)):
                    mm = product(PQ[:], [v[:, k, at:at + P] for v in w], [h[:, k, :] for h in (h_hi, h_lo)], k == 0, k == n - 1)
                    if k == n - 1:
                        mm.then_inc(s_pq, 1)

            def k_part(layer, slot, k0, k1):
                if layer == 0:
                    for k in range(k0, k1):
                        mm = product(PK[:], [v[:, k, P:2 * P] for v in w_view(slot, C, UW)], [h[:, k, :] for h in (h_hi, h_lo)],
                                     k == 0, k == C - 1)
                        if k == C - 1:
                            mm.then_inc(s_pk, 1)
                elif k0 == 0:
                    product(PK[:], [v[:, 2, :] for v in w_view(slot, 3, P)], [o[:, 7, :] for o in (o_hi, o_lo)],
                            True, True).then_inc(s_pk, 1)

            def scores(layer, gp, st):
                rows = (P, HD + 2) if layer == 0 else (MLA_K, MLA_K)
                n = P * (st + 1)
                for s in range(2):
                    out = S_BANK[st % 2][s]
                    if st == 0:
                        pe.wait_ge(s_qlo, 2 * gp + s + 1)
                        pe.wait_ge(s_klo, 2 * gp + s + 1)
                        if layer == 0:
                            pe.wait_ge(s_qx[s], 16 * gp + 16)
                            pe.wait_ge(s_kx[s], 16 * gp + 16)
                            pe.wait_ge(s_fx[s], 16 * gp + 16)
                        else:
                            pe.wait_ge(s_qx[s], 32 * gp + (32 - 16 * PAIRS))
                    if st == 1:
                        pe.wait_ge(s_olo, 2 * gp)
                    if st >= 2:
                        pe.wait_ge(s_exp, 2 * (4 * gp + st - 2) + s + 1)
                    q = [t[s][0:m, P * st:n] for t, m in zip((qa, qb), rows)]
                    k = [t[s][0:m, 0:n] for t, m in zip((ka, kb), rows)]
                    nc.tensor.matmul(out[:, 0:n], q[0], k[0], start=True, stop=False)
                    if layer == 0:
                        nc.tensor.matmul(out[:, 0:n], q[1], k[1], start=False, stop=False)
                    else:
                        nc.tensor.matmul(out[:, 0:n], q[1], k[0], start=False, stop=False)
                        nc.tensor.matmul(out[:, 0:n], q[0], k[1], start=False, stop=False)
                    nc.tensor.matmul(out[:, P * st:n], id_b[:], mask_b[:], start=False, stop=True).then_inc(s_score, 1)

            def transposes(gp, st):
                for s in range(2):
                    pe.wait_ge(s_norm, 2 * (4 * gp + st) + s + 1)
                    if st:
                        pe.wait_ge(s_ptlo, 2 * (4 * gp + st - 1) + s + 1)
                    for j in range(st + 1):
                        mm = nc.tensor.transpose(T_BANK[s][:, P * j:P * (j + 1)], prob[st % 2][s][:, P * j:P * (j + 1)], ident)
                    mm.then_inc(s_tr, 1)

            def attend(gp):
                pe.wait_ge(s_vlo, gp + 1)
                for s in range(2):
                    pe.wait_ge(s_ptlo, 2 * (4 * gp + 3) + s + 1)
                    for j in range(TB):
                        at = s * PTH + (PTS + P) * j
                        mm = product(S_BANK[1][s][:, P * j:T], [v[:, j, :] for v in (vs_hi, vs_lo)],
                                     [b[:, at:at + T - P * j] for b in (pt_hi, pt_lo)], j == 0, j == TB - 1)
                    mm.then_inc(s_pv, 1)

            def attn(layer, i, r, more, u, a):
                gp = PAIRS * layer + 2 * i + r
                slot = (r + 1) % 2
                if more:
                    w_ready(u)
                    pe.wait_ge(s_qlo, 2 * gp + 2)
                    q_part(layer, slot, 0, 4)
                scores(layer, gp, 0)
                if a is not None:
                    ada_mm(a - 1, 0, a - 7, (r + 1) % 2)
                scores(layer, gp, 1)
                if more:
                    q_part(layer, slot, 4, 8)
                scores(layer, gp, 2)
                scores(layer, gp, 3)
                transposes(gp, 0)
                if more:
                    if a is not None:
                        pe.wait_ge(s_mod, a)
                    pe.wait_ge(s_klo, 2 * gp + 2)
                    k_part(layer, slot, 0, 2)
                transposes(gp, 1)
                if more:
                    k_part(layer, slot, 2, 4)
                transposes(gp, 2)
                if more:
                    k_part(layer, slot, 4, 6)
                transposes(gp, 3)
                if more:
                    k_part(layer, slot, 6, 8)
                attend(gp)

            def attn_layer(layer, u0):
                w_ready(u0)
                q_part(layer, 0, 0, 8)
                if layer == 0:
                    pe.wait_ge(s_mod, ADA_START + 7)
                k_part(layer, 0, 0, 8)
                if layer == 0:
                    pe.wait_ge(s_tdve, TD_FOUT)
                    pe.wait_ge(s_zero, 2)
                else:
                    pe.wait_ge(s_tdve, TD_MOUT)
                    pe.wait_ge(s_rpa, 7)
                a0 = ADA_START + 8 if layer == 0 else None
                with pe.Fori(0, 3) as i:
                    for r in range(2):
                        attn(layer, i, r, True, u0 + 2 * i + r + 1, None if a0 is None else a0 + 2 * i + r)
                attn(layer, 3, 0, True, u0 + 7, None if a0 is None else a0 + 6)
                attn(layer, 3, 1, False, None, None if a0 is None else a0 + 7)
                if layer == 0:
                    ada_mm(a0 + 7, 0, 17, 1)

            def dense_tile(bank, w, at, rhs):
                for k in range(C):
                    mm = product(bank[:], [v[:, k, at:at + P] for v in w], [t[:, k, :] for t in rhs], k == 0, k == C - 1)
                mm.then_inc(s_tile, 1)

            def dense_pair(banks, w, rhs, ready, widths=(P, P)):
                for k in range(C):
                    if ready(k) is not None:
                        pe.wait_ge(*ready(k))
                    for t, m in enumerate(widths):
                        mm = product(banks[t][0:m, :], [v[:, k, t * P:t * P + m] for v in w], [b[:, k, :] for b in rhs], k == 0, k == C - 1)
                        if k == C - 1:
                            mm.then_inc(s_tile, 1)

            def out_proj(layer, u0, td):
                for n in range(4):
                    w_ready(u0 + n)
                    if n == 0:
                        olo = HEADS * (layer + 1)
                        dense_pair(ps[0:2], w_view(0, C, UW), (o_hi, o_lo),
                                   lambda k: (s_olo, olo - 2) if k == 0 else (s_olo, olo) if k == C - 1 else None)
                        continue
                    for t in range(2):
                        c = 2 * n + t
                        if c >= RING:
                            pe.wait_ge(s_tdve, td + c - 3)
                        dense_tile(ps[c % RING], w_view(n % 2, C, UW), t * P, (o_hi, o_lo))
                pe.wait_ge(s_acc, 7 * (2 * layer + 2))
                sum_over_features(sc[:, 6, :])

            def mlp_group(layer, g, first):
                base = 32 * layer + 8 * g
                norm = 2 * layer + 1

                def bank_free(j):
                    if j < 4:
                        pe.wait_ge(s_tdve, TD_MLP[layer] + 8 * g + j - 3)
                    elif j < 12:
                        pe.wait_ge(s_tact, base + j - 3)
                    else:
                        pe.wait_ge(s_tdve, TD_MLP[layer] + 8 * g + j - 11)

                for n in range(8):
                    w_ready(U_MLP[layer] + 8 * g + n)
                    rhs = (h_hi, h_lo) if n < 4 else (o_hi, o_lo)
                    if (n == 0 and first) or n == 4:
                        sem_, count = (s_hlo, C * norm + 1) if n == 0 else (s_alo, base + 1)
                        bank_free(2 * n)
                        bank_free(2 * n + 1)
                        dense_pair(ps[0:2], w_view(0, C, UW), rhs, lambda k: (sem_, count + k))
                    for t in range(2):
                        j = 2 * n + t
                        if not ((n == 0 and first) or n == 4):
                            bank_free(j)
                            dense_tile(ps[j % RING], w_view(n % 2, C, UW), t * P, rhs)
                        if layer == 0 and 0 < n < 7 and t == 0:
                            ada_mm(24 + 6 * g + n - 1, 1, 5 + 6 * g + n, (n + 1) % 2)

            def mlp(layer):
                mlp_group(layer, 0, True)
                with pe.Fori(1, GROUPS) as g:
                    mlp_group(layer, g, False)
                pe.wait_ge(s_acc, 7 * (2 * layer + 3))
                sum_over_features(sc[:, 6, :])

            attn_layer(0, U_QK)
            out_proj(0, U_FOUT, TD_FOUT)
            mlp(0)

            w = w_view(0, C, KVR + ROPE)
            w_ready(U_DKV)
            pe.wait_ge(s_tdve, TD_DKV - 2)
            dense_pair(ps[0:2], w, (h_hi, h_lo), lambda k: (s_hlo, 2 * C + 1 + k), (KVR, ROPE))
            w_ready(U_DQ)
            for t in range(2):
                pe.wait_ge(s_tdve, TD_DKV - 1 + t)
                dense_tile(ps[2 + t], w_view(1, C, UW), t * P, (h_hi, h_lo))
                if t == 0:
                    pe.wait_ge(s_rpa, 1)
                    sum_over_features(sc[:, 4, :])
            w_ready(U_MV)
            pe.wait_ge(s_rope, 2)
            for n in range(2 * TB):
                tk, half = n // 2, n % 2
                pe.wait_ge(s_tdve, TD_DKV + n + 1)
                product(ps[n % RING][:], [o[:, 7, tk * P:(tk + 1) * P] for o in (o_hi, o_lo)],
                        [v[:, 0, half * T:(half + 1) * T] for v in w_view(0, 1, D)], True, True).then_inc(s_tile, 1)
                if n == 3:
                    pe.wait_ge(s_rope, 3)
                    sum_over_features(adab[:, 2, :])
            w_ready(U_QROPE)
            pe.wait_ge(s_rope, 7)
            for t in range(TB):
                pe.wait_ge(s_tdve, TD_DKV + t + 9)
                for k in range(2):
                    mm = product(ps[t][:], [v[:, k, t * P:(t + 1) * P] for v in w_view(1, 2, T)], [h[:, k, :] for h in (h_hi, h_lo)],
                                 k == 0, k == 1)
                mm.then_inc(s_tile, 1)

            attn_layer(1, U_MQK)
            out_proj(1, U_MOUT, TD_MOUT)
            mlp(1)


def columns(v):
    import numpy as np
    return np.ascontiguousarray(np.asarray(v).reshape(-1, P).T)


def units(w, n):
    import numpy as np
    k, m = w.shape
    return np.ascontiguousarray(w.reshape(k // P, P, m // n, n).transpose(2, 1, 0, 3)).reshape(m // n, P, -1)


def kernel(**inputs):
    import numpy as np
    import concourse.bacc as bacc
    from concourse.bass_utils import run_bass_kernel_spmd as run

    a = {k: np.asarray(v) for k, v in inputs.items()}
    cat = np.concatenate

    which = ("sh_m", "sc_m", "g_m", "sh_f", "sc_f", "g_f")
    spans = [(layer, which.index(w) * D) for layer, w in ADA_ORDER]
    ada = cat([units(a["ada_w"][layer][:, at:at + D], UW) for layer, at in spans])
    ada_b = cat([a["ada_b"][layer][at:at + D] for layer, at in spans])
    bf = np.zeros(P, np.float32)
    bf[:HEADS] = a["fox_b_f"][0]
    cvec = cat([columns(v) for v in (
        a["c"][0], ada_b, a["norm_mix_g"][0], a["norm_mix_g"][1], a["norm_mlp_g"][0], a["norm_mlp_g"][1],
        a["final_norm_g"], a["mla_q_norm_g"][0], a["mla_kv_norm_g"][0], bf)], axis=1)

    row = np.arange(P)
    cconst = np.zeros((P, CC_N), np.float32)
    cconst[:, CC_ID:CC_ID + P] = np.eye(P)
    cconst[:, CC_MASK:CC_MASK + P] = np.where(row[None, :] > row[:, None], NEG, 0.0)
    cconst[:, CC_FREQ] = 10000.0 ** (-(2 * (row % (ROPE // 2))).astype(np.float64) / ROPE)
    cconst[:, CC_EPS] = EPS
    cconst[:, CC_SIGN] = np.where(row % ROPE < ROPE // 2, -1.0, 1.0)

    w_in = a["fox_w_in"][0]
    q, k, v, f = (w_in[:, n * D:(n + 1) * D] for n in range(4))
    w_qk = np.concatenate([units(q, P).reshape(PAIRS, P, C, P), units(k, P).reshape(PAIRS, P, C, P)], axis=3).reshape(PAIRS, P, UNIT)
    uq = a["mla_w_uq"][0].reshape(QR, HEADS, HD + ROPE)
    ukv = a["mla_w_ukv"][0].reshape(KVR, HEADS, 2 * HD)
    uq_nope, uq_rope = uq[:, :, :HD].reshape(QR, D), uq[:, :, HD:].reshape(QR, HEADS * ROPE)
    uk, uv = ukv[:, :, :HD].reshape(KVR, D), ukv[:, :, HD:].reshape(KVR, D)
    w_mlp = []
    for layer in range(2):
        w1, w2 = a["mlp_w1"][layer], a["mlp_w2"][layer]
        for g in range(GROUPS):
            w_mlp += [units(w1[:, g * D:(g + 1) * D], UW), units(w2[g * D:(g + 1) * D], UW)]
    feeds = dict(
        xt=np.ascontiguousarray(a["x"][0].reshape(T, C, P).transpose(2, 1, 0)),
        pos=a["positions"].reshape(T),
        cvec=cvec, cconst=cconst, ada=ada,
        w_v=units(v, UW), w_qk=w_qk, w_f=units(f, HEADS)[0],
        w_fout=units(a["fox_w_out"][0], UW),
        w_dkv=units(a["mla_w_dkv"][0], KVR + ROPE), w_dq=units(a["mla_w_dq"][0], UW),
        w_mv=units(uv, D), w_qrope=units(uq_rope, T),
        w_mqk=cat([units(uq_nope, P), units(uk, P)], axis=2),
        w_mout=units(a["mla_w_out"][0], UW), w_mlp=cat(w_mlp))

    nc = bacc.Bacc("TRN2", target_bir_lowering=False, num_devices=1)
    args, arrays = {}, {}
    for name, arr in feeds.items():
        arr = np.ascontiguousarray(arr)
        arrays[name + "_dram"] = arr
        args[name] = nc.dram_tensor(name + "_dram", arr.shape, mybir.dt.from_np(arr.dtype), kind="ExternalInput").ap()
    args["yt"] = nc.dram_tensor("yt_dram", (P, C, T), F32, kind="ExternalOutput").ap()
    args["f_dram"] = nc.dram_tensor("f_rows_dram", (HEADS, 2, T), F32, kind="Internal").ap()
    trunk(nc, **args)
    r = run(nc, [arrays], core_ids=[0])
    y = r.results[0]["yt_dram"]
    return np.ascontiguousarray(y.transpose(2, 1, 0)).reshape(1, T, D)
```

```python
import math
from contextlib import ExitStack

import concourse.bass as bass
from concourse import mybir

F32 = mybir.dt.float32
F32R = mybir.dt.float32r
BF16 = mybir.dt.bfloat16
I32 = mybir.dt.int32
ALU = mybir.AluOpType
ACT = mybir.ActivationFunctionType
AXX = mybir.AxisListType.X

P = 128
T = 512
D = 1024
C = D // P
TB = T // P
HEADS = 16
HD = D // HEADS
ROPE = HD // 2
PAIRS = HEADS // 2
QR, KVR = D // 4, D // 8
DFF = 4 * D
GROUPS = DFF // (C * P)
UW = 256
UNIT = C * UW
HALF = UNIT // 2
ADA_UNITS = 2 * 6 * D // UW
ADA_START = 8
EPS = 1e-6
NEG = -1e30
INV_2PI = 1 / (2 * math.pi)
ROUND = 1.5 * 2.0 ** 23
TWO_PI_PARTS = (6.28125, 0.0019340515136718750, 1.2556659146e-06)
FOX_SCALE = HD ** -0.5
MLA_SCALE = (HD + ROPE) ** -0.5
MLA_K = HD + ROPE
F_AT = 96
PTS = 384
PTH = PTS * 3 + T

U_V = 0
U_QK = U_V + 4
U_FOUT = U_QK + PAIRS
U_MLP = (U_FOUT + 4, U_FOUT + 4 + 32 + 4 + PAIRS + 4)
U_DKV = U_MLP[0] + 32
U_DQ, U_MV, U_QROPE = U_DKV + 1, U_DKV + 2, U_DKV + 3
U_MQK = U_DKV + 4
U_MOUT = U_MQK + PAIRS
MQK_W = 3 * P

D_V = 0
D_FOUT = 16
D_MLP = (D_FOUT + C, D_FOUT + C + 64 + 4 + 8 + 4 + C)
D_DKV = D_MLP[0] + 64
D_DQ, D_MV, D_QROPE = D_DKV + 2, D_DKV + 4, D_DKV + 12
D_MOUT = D_DKV + 16
RING = 4

TD_FOUT = 16
TD_MLP = (TD_FOUT + C, TD_FOUT + C + 32 + 16 + C)
TD_DKV = TD_MLP[0] + 32
TD_MOUT = TD_DKV + 16

ADA_ORDER = [(layer, w) for layer in range(2) for w in ("sc_m", "sh_m", "g_m", "sh_f", "sc_f", "g_f")]

ADA_EARLY = 16
ADA_GP = (1, 4, 8, 10, 12, 14)
ADA_STEPS = (8, 7)
ADA_SLOT = (0, 1, 2, 3, 4, 5, 6, 0, 3, 4, 5, 6, 0, 3, 4, 5)


ADA_PE = (2, 6)
ADA_MM = (0, 2, 1, 3, 6, 4, 5, 7, *range(8, ADA_EARLY))


def ada_own(a):
    def owner(b):
        return 1 if b in ADA_GP else 2 if b in ADA_PE else 0
    return owner(a), sum(owner(b) == owner(a) for b in range(a))


def ada_acc_free(a):
    own, idx = ada_own(a)
    if idx < 2:
        return None
    return ADA_MM.index(next(b for b in range(a) if ada_own(b) == (own, idx - 2))) + 1


CV_C = 0
CV_ADAB = CV_C + C
CV_GMIX = CV_ADAB + 2 * ADA_UNITS
CV_GMLP = CV_GMIX + 2 * C
CV_GFIN = CV_GMLP + 2 * C
CV_GQ = CV_GFIN + C
CV_GKV = CV_GQ + 2
CV_BF = CV_GKV + 1
CV_N = CV_BF + 1
CC_ID = 0
CC_MASK = CC_ID + P
CC_FREQ = CC_MASK + P
CC_EPS = CC_FREQ + 1
CC_SIGN = CC_EPS + 1
CC_N = CC_SIGN + 1


def trunk(nc, xt, pos, cvec, cconst, ada, w_v, w_qk, w_f, w_fout, w_dkv, w_dq, w_mv, w_qrope, w_mqk, w_mout, w_mlp, f_dram, yt):
    ctx = ExitStack()
    with ctx:
        def sb(name, shape, dt):
            return ctx.enter_context(nc.sbuf_tensor(name, shape, dt))

        def sem(name):
            return ctx.enter_context(nc.semaphore(name))

        x = sb("x", [P, C, T], F32)
        h_hi, h_lo = sb("h_hi", [P, C, T], F32R), sb("h_lo", [P, C, T], F32R)
        o_at = nc.sbuf_base
        o_hi, o_lo = sb("o_hi", [P, C, T], F32R), sb("o_lo", [P, C, T], F32R)
        ada_space = nc.alloc_sbuf_tensor_at("ada_space", [P, 4, UNIT], F32, offset=o_at)
        w_raw = sb("w_raw", [P, UNIT], F32)
        w_hi, w_lo = sb("w_hi", [P, 2, UNIT], F32R), sb("w_lo", [P, 2, UNIT], F32R)
        adab = sb("adab", [P, 4, T], F32)
        v_raw = sb("v_raw", [P, 8, T], F32)
        qa, qb, ka, kb = ([sb(f"{n}{s}", [P, T], F32R) for s in range(2)] for n in ("qa", "qb", "ka", "kb"))
        probs = sb("probs", [P, 4, T], F32)
        pt_hi = sb("pt_hi", [P, PTH + PTS * 5], F32R)
        pt_lo = sb("pt_lo", [P, PTH + PTS * 5], F32R)
        vs_hi, vs_lo = sb("vs_hi", [P, TB, P], F32R), sb("vs_lo", [P, TB, P], F32R)
        cv = sb("cv", [P, CV_N], F32)
        cc = sb("cc", [P, CC_N], F32)
        ones = sb("ones", [P, P], F32)
        id_b, mask_b = sb("id_b", [P, P], BF16), sb("mask_b", [P, P], BF16)
        cact = sb("cact", [P, C], F32)
        ctmp = sb("ctmp", [P, 3, C], F32)
        mod = sb("mod", [P, 2 * ADA_UNITS], F32)
        acol = sb("acol", [P, C], F32)
        adaacc = sb("adaacc", [P, 4, UW], F32)
        warm = sb("warm", [P, 1], F32)
        nmax, rsum, rinv = sb("nmax", [P, 2, 2], F32), sb("rsum", [P, 2, 2], F32), sb("rinv", [P, 2, 2], F32)
        f_rows = [kb[part][F_AT:F_AT + HEADS, :] for part in range(2)]
        wf_raw = sb("wf_raw", [P, C * HEADS], F32)
        wf_hi, wf_lo = (t[:, 0:C * HEADS].rearrange("p (c h) -> p c h", c=C) for t in (pt_hi, pt_lo))

        ps = [ctx.enter_context(nc.psum_tensor(f"ps{i}", [P, T], F32)) for i in range(8)]
        S_BANK = [[ps[0], ps[1]], [ps[2], ps[3]]]
        T_BANK = [ps[4], ps[5]]
        PQ, PK = ps[6], ps[7]

        ident = cc[:, CC_ID:CC_ID + P]
        sc = v_raw
        prob = [[probs[:, 2 * r + s, :] for s in range(2)] for r in range(2)]
        rope_ab = ((adab[:, 2, :], adab[:, 3, :]), (prob[0][0], prob[0][1]))
        cos_t, sin_t = adab[:, 0, :], adab[:, 1, :]
        ada_slots = [t.rearrange("p a t -> p (a t)") for t in (
            adab[:, :, :], v_raw[:, 0:4, :], probs[:, :, :],
            *(ada_space[:, n:n + 1, :] for n in range(4)))]
        v_tok = v_raw[:, :, :].rearrange("p a t -> p (a t)").rearrange("p (b n) -> p b n", b=TB)

        def mcols(layer, what):
            at = C * ADA_ORDER.index((layer, what))
            return mod[:, at:at + C]

        s_cin, s_xin, s_posin, s_fin = sem("const_in"), sem("x_in"), sem("pos_in"), sem("wf_in")
        s_ast = [sem(f"ada_start_in{i}") for i in range(7)]
        s_ain = [sem(f"ada_in{i}") for i in range(2)]
        s_win = [sem(f"w_in{i}") for i in range(2)]
        s_whi, s_wlo = sem("w_hi_done"), sem("w_lo_done")
        s_astep = [sem("ada_step_vector"), sem("ada_step_gpsimd")]
        s_adamm, s_mod, s_warm = sem("ada_mm"), sem("mod_done"), sem("table_warm")
        s_ones, s_bf, s_csil, s_cact = sem("ones_set"), sem("bf_consts"), sem("silu_act"), sem("silu_dve")
        s_tile = sem("tile_done")
        s_tact, s_tdve = sem("tile_read_act"), sem("tile_read_dve")
        s_sq, s_acc = sem("square_done"), sem("square_summed")
        s_ss, s_ln, s_rstd = sem("sumsq_mm"), sem("ln_done"), sem("rstd_done")
        s_acol, s_tm, s_hhi, s_hlo = sem("acol_done"), sem("xhat_done"), sem("h_hi_done"), sem("h_lo_done")
        s_sqr, s_ahi, s_alo = sem("relu_squared"), sem("a_hi_done"), sem("a_lo_done")
        s_wf, s_fmm, s_fa, s_fd, s_fr = sem("wf_split"), sem("f_mm"), sem("f_act"), sem("f_dve"), sem("f_rows")
        s_score, s_max, s_exp, s_rinv, s_norm = sem("scores"), sem("rowmax"), sem("exp"), sem("rinv"), sem("normed")
        s_tr, s_pthi, s_ptlo = sem("transposed"), sem("pt_hi_done"), sem("pt_lo_done")
        s_pq, s_pk, s_qhi, s_qlo, s_khi, s_klo = (sem(n) for n in ("q_mm", "k_mm", "q_hi_done", "q_lo_done", "k_hi_done", "k_lo_done"))
        s_qx, s_kx, s_fx = ([sem(f"{n}{s}") for s in range(2)] for n in ("q_rows_in", "k_rows_in", "f_rows_in"))
        s_vhi, s_vlo, s_pv, s_ohi, s_olo = sem("v_hi_done"), sem("v_lo_done"), sem("pv_mm"), sem("o_hi_done"), sem("o_lo_done")
        s_rope, s_rpa, s_kr = sem("latent_dve"), sem("latent_act"), sem("krope_rows")
        s_trig, s_triga = sem("trig_dve"), sem("trig_act")
        s_qrd, s_qra, s_qsin, s_qadd = sem("qrope_done"), sem("qrope_swapped"), sem("qrope_sin"), sem("qrope_added")
        s_out = [sem(f"y_out{i}") for i in range(C)]
        s_fdram = sem("f_stored")
        s_orow, s_passed = sem("ones_rows"), sem("pool_waits_passed")
        s_yn = sem("y_done")

        block = ctx.enter_context(nc.Block())

        def pt(s, buf, i, n):
            at = s * PTH + P * i
            return buf[:, at:at + PTS * n].rearrange("p (j c) -> p j c", c=PTS)[:, :, 0:P]


        def after(i, r):
            return (i, 1) if r == 0 else (i + 1, 0)

        @block.sync
        def _(sp):
            def load_w(u, src, n=UNIT, narrow=False):
                for hf in range(2):
                    split = 2 * u if narrow else 2 * u + hf - 1
                    if not (isinstance(u, int) and u == 0):
                        sp.wait_ge(s_whi, split)
                        sp.wait_ge(s_wlo, split)
                    a, b = hf * (n // 2), (hf + 1) * (n // 2)
                    sp.dma_start(w_raw[:, a:b], src[:, a:b]).then_inc(s_win[hf], 16)

            def load_ada_early(a):
                slot = ADA_SLOT[a]
                before = [b for b in range(a) if ADA_SLOT[b] == slot]
                if before:
                    own, idx = ada_own(before[-1])
                    if own == 2:
                        sp.wait_ge(s_adamm, ADA_MM.index(before[-1]) + 1)
                    else:
                        sp.wait_ge(s_astep[own], ADA_STEPS[own] * (idx + 1))
                sp.dma_start(ada_slots[slot], ada[a, :, :]).then_inc(s_ast[slot], 16)

            def load_ada(a, own, idx):
                for hf in range(2):
                    sp.wait_ge(s_astep[own], ADA_STEPS[own] * (idx - 1) + (4, 3)[own] * (hf + 1) + own * hf)
                    a0, b0 = hf * HALF, (hf + 1) * HALF
                    sp.dma_start(ada_slots[0][:, a0:b0], ada[a, :, a0:b0]).then_inc(s_ain[hf], 16)

            def operand_rows(layer, i, r):
                gp = PAIRS * layer + 2 * i + r
                if not (isinstance(gp, int) and gp == 0):
                    sp.wait_ge(s_score, 8 * gp)
                for s in range(2):
                    if layer == 0:
                        for rows in (kb[s][HD:HD + 2, :], qb[s][HD + 2:HD + 4, :]):
                            sp.dma_start(rows.bitcast(F32), f_dram[bass.ds(4 * i + (2 * r + s), 1), :, :]).then_inc(s_fx[s], 16)
                    else:
                        at = ROPE * (2 * r + s)
                        for dst, src in ((qa, h_hi), (qb, h_lo)):
                            sp.dma_start(dst[s][HD:MLA_K, :].bitcast(F32), src[at:at + ROPE, bass.ds(2 + i, 1), :].bitcast(F32)).then_inc(s_qx[s], 16)
                if layer == 0:
                    for s in range(2):
                        sp.wait_ge(s_qhi, 2 * gp + s + 1)
                        sp.dma_start(qb[s][0:HD, :].bitcast(F32), qa[s][0:HD, :].bitcast(F32)).then_inc(s_qx[s], 16)
                    for s in range(2):
                        sp.wait_ge(s_khi, 2 * gp + s + 1)
                        sp.dma_start(ka[s][HD:P, :].bitcast(F32), ka[s][0:HD, :].bitcast(F32)).then_inc(s_kx[s], 16)

            sp.dma_start(cv[:], cvec).then_inc(s_cin, 16)
            sp.dma_start(cc[:], cconst).then_inc(s_cin, 16)
            for a in range(ADA_START):
                if a == 4:
                    sp.dma_start(x[:, :, :], xt).then_inc(s_xin, 16)
                if a == ADA_START - 1:
                    load_w(0, w_v[0])
                    sp.dma_start(wf_raw[:], w_f).then_inc(s_fin, 16)
                load_ada_early(a)
            for n in range(4):
                load_w(U_V + n + 1, w_v[n + 1] if n < 3 else w_qk[0])
                load_ada_early(ADA_START + 2 * n)
                load_ada_early(ADA_START + 2 * n + 1)
            load_w(U_QK + 1, w_qk[1])
            for part in range(2):
                sp.wait_ge(s_fr, part + 1)
                sp.dma_start(f_dram[:, part, :], f_rows[part].bitcast(F32)).then_inc(s_fdram, 16)
            sp.wait_ge(s_fdram, 32)
            operand_rows(0, 0, 0)
            with sp.Fori(0, 3) as i:
                for r in range(2):
                    load_w(U_QK + 2 * i + r + 2, w_qk[2 * i + (r + 2)])
                    load_ada(ADA_EARLY + 2 * i + r, 0, 8 + 2 * i + r)
                    operand_rows(0, *after(i, r))
            load_w(U_FOUT, w_fout[0])
            load_ada(22, 0, 14)
            operand_rows(0, 3, 1)
            load_ada(23, 0, 15)
            for n in range(1, 4):
                load_w(U_FOUT + n, w_fout[n])
            load_w(U_MLP[0], w_mlp[0])
            sp.wait_ge(s_astep[0], 8 * 16)

            def mlp_loads(layer, g, last):
                for n in range(8):
                    if not (last and n == 7):
                        load_w(U_MLP[layer] + 8 * g + n + 1, w_mlp[32 * layer + 8 * g + (n + 1)])
                    elif layer == 0:
                        load_w(U_DKV, w_dkv[0], C * 160)
                    if layer == 0 and n < 6:
                        load_ada(24 + 6 * g + n, 1, 6 + 6 * g + n)
                    if layer == 0 and last and n == 5:
                        sp.wait_ge(s_astep[1], 7 * (6 + 24))
                        sp.dma_start(adab[:, 2, :].bitcast(I32), pos.partition_broadcast(P)).then_inc(s_posin, 16)

            with sp.Fori(0, GROUPS - 1) as g:
                mlp_loads(0, g, False)
            mlp_loads(0, GROUPS - 1, True)
            load_w(U_DQ, w_dq[0], narrow=True)
            load_w(U_MV, w_mv[0], D)
            load_w(U_QROPE, w_qrope[0], 2 * T)
            load_w(U_MQK, w_mqk[0], MQK_W)
            load_w(U_MQK + 1, w_mqk[1], MQK_W)
            sp.wait_ge(s_qrd, TB)
            operand_rows(1, 0, 0)
            with sp.Fori(0, 3) as i:
                for r in range(2):
                    load_w(U_MQK + 2 * i + r + 2, w_mqk[2 * i + (r + 2)], MQK_W)
                    operand_rows(1, *after(i, r))
            load_w(U_MOUT, w_mout[0], narrow=True)
            operand_rows(1, 3, 1)
            for n in range(1, 4):
                load_w(U_MOUT + n, w_mout[n])
            load_w(U_MLP[1], w_mlp[32])
            with sp.Fori(0, GROUPS - 1) as g:
                mlp_loads(1, g, False)
            mlp_loads(1, GROUPS - 1, True)
            for c in range(C):
                sp.wait_ge(s_yn, c + 1)
                sp.dma_start(yt[:, c, :], sc[:, c, :]).then_inc(s_out[c], 16)
            for c in range(C):
                sp.wait_ge(s_out[c], 16)


        @block.gpsimd
        def _(pool):
            nc.gpsimd.memset(ones[:], 1.0).then_inc(s_ones, 1)
            for s in range(2):
                for n, (rows, value) in enumerate(((qb[s], 1.0), (kb[s], -1.0))):
                    pool.wait_ge(s_ones, 1)
                    if 2 * s + n:
                        pool.wait_ge(s_orow, 2 * s + n)
                    nc.gpsimd.memset(rows[HD:HD + 4, :].bitcast(F32), value).then_inc(s_orow, 1)

            def waits(*pairs):
                for sem, count in pairs:
                    pool.wait_ge(sem, count)
                pool.sem_inc(s_passed, 1)

            def ada_sum(a, idx, par, buf, arrived):
                acc = adaacc[:, 2 + par, :]
                step = 7 * idx
                free = ada_acc_free(a) if isinstance(a, int) else a - 1
                if free is not None:
                    waits((s_adamm, free))
                for hf in range(2):
                    if isinstance(step, int) and step == 0:
                        waits(arrived(hf))
                    else:
                        waits(arrived(hf), (s_astep[1], step))
                    w = buf[:, hf * HALF:(hf + 1) * HALF]
                    wk = w.rearrange("p (k n) -> p k n", k=C // 2)
                    c = cact[:, hf * C // 2:(hf + 1) * C // 2].unsqueeze(2).to_broadcast([P, C // 2, UW])
                    nc.gpsimd.tensor_tensor(wk, wk, c, ALU.mult).then_inc(s_astep[1], 1)
                    waits((s_astep[1], step + 1))
                    nc.gpsimd.tensor_tensor(w[:, 0:HALF // 2], w[:, 0:HALF // 2], w[:, HALF // 2:HALF], ALU.add).then_inc(s_astep[1], 1)
                    waits((s_astep[1], step + 2))
                    out = w[:, 0:UW] if hf else acc
                    nc.gpsimd.tensor_tensor(out, w[:, 0:UW], w[:, UW:2 * UW], ALU.add).then_inc(s_astep[1], 1)
                    step = step + 3
                waits((s_astep[1], step))
                nc.gpsimd.tensor_tensor(acc, acc, w[:, 0:UW], ALU.add).then_inc(s_astep[1], 1)

            def pair_rows(layer, i, r, more, u, n):
                gp = PAIRS * layer + 2 * i + r

                def norm(st):
                    for s in range(2):
                        pr = prob[st % 2][s][:, 0:P * (st + 1)]
                        k = 2 * st + s
                        if st == 0 and s == 0:
                            before = (s_vlo, gp + 1)
                        elif st == 2 and s == 0 and more:
                            before = (s_wlo, 2 * u + 2)
                        else:
                            before = (s_norm, 8 * gp + k)
                        waits((s_rinv, 4 * gp + st + 1), before)
                        nc.gpsimd.tensor_scalar(pr, pr, rinv[:, st % 2, s:s + 1], 1.0, ALU.mult, ALU.mult).then_inc(s_norm, 1)

                if layer == 0:
                    waits((s_vhi, gp + 1))
                else:
                    waits((s_vhi, gp + 1), (s_wlo, 2 * u))
                nc.gpsimd.tensor_tensor(vs_lo[:], v_tok[:, :, bass.ds(P * (2 * i + r), P)], vs_hi[:].bitcast(F32), ALU.subtract).then_inc(s_vlo, 1)
                if layer == 0:
                    norm(0)
                    norm(1)
                if more:
                    slot = r
                    for hf in range(2):
                        a, b = hf * (n // 2), (hf + 1) * (n // 2)
                        waits((s_whi, 2 * u + hf + 1), (s_wlo, 2 * u + 1) if hf else (s_norm, 8 * gp + 4) if layer == 0 else (s_vlo, gp + 1))
                        nc.gpsimd.tensor_tensor(w_lo[:, slot, a:b], w_raw[:, a:b], w_hi[:, slot, a:b].bitcast(F32), ALU.subtract).then_inc(s_wlo, 1)
                if layer == 0:
                    norm(2)
                    norm(3)
                    waits((s_norm, 8 * gp + 8))

            pool.wait_ge(s_orow, 4)
            pool.wait_ge(s_cact, 3)
            for a in ADA_GP:
                idx, slot = ada_own(a)[1], ADA_SLOT[a]
                uses = 16 * sum(ADA_SLOT[b] == slot for b in range(a + 1))
                ada_sum(a, idx, idx % 2, ada_slots[slot], lambda hf: (s_ast[slot], uses))
            for layer, u0, n, then in ((0, U_QK, UNIT, U_FOUT), (1, U_MQK, MQK_W, U_MOUT)):
                waits((s_astep[1], 7 * (6 + 24 * layer)))
                if layer == 1:
                    pool.wait_ge(s_trig, 13)
                    for k in range(TB):
                        b = rope_ab[k % 2][1]
                        if k:
                            pool.wait_ge(s_qsin, k)
                        pool.wait_ge(s_qra, k + 1)
                        nc.gpsimd.tensor_tensor(b, b, sin_t, ALU.mult).then_inc(s_qsin, 1)
                    pool.wait_ge(s_qsin, TB)
                with pool.Fori(0, 3) as i:
                    for r in range(2):
                        pair_rows(layer, i, r, True, u0 + 2 * i + r + 2, n)
                pair_rows(layer, 3, 0, True, then, UNIT)
                pair_rows(layer, 3, 1, False, then + 1, None)
                if layer == 0:
                    with pool.Fori(0, GROUPS) as g:
                        for k in range(6):
                            a = 24 + 6 * g + k
                            ada_sum(a, 6 + 6 * g + k, k % 2, ada_slots[0], lambda hf: (s_ain[hf], 16 * (a - ADA_EARLY + 1)))

        @block.scalar
        def _(act):
            def split_hi(u, n=UNIT, used=None):
                if used is not None:
                    act.wait_ge(*used)
                for hf in range(2):
                    a, b = hf * (n // 2), (hf + 1) * (n // 2)
                    act.wait_ge(s_win[hf], 16 * u + 16)
                    nc.scalar.activation(w_hi[:, slot_of[0], a:b], w_raw[:, a:b], ACT.Copy).then_inc(s_whi, 1)
                slot_of[0] ^= 1

            slot_of = [0]

            def rstd(out, width, k):
                if k:
                    act.wait_ge(s_warm, k)
                nc.scalar.activation(warm[:], ones[:, 0:1], ACT.Ln).then_inc(s_warm, 1)
                act.wait_ge(s_ss, k + 1)
                nc.scalar.activation(out, T_BANK[1][:], ACT.Ln, bias=cc[:, CC_EPS:CC_EPS + 1], scale=1.0 / width).then_inc(s_ln, 1)
                act.wait_ge(s_ln, k + 1)
                nc.scalar.activation(out, out, ACT.Exp, scale=-0.5).then_inc(s_rstd, 1)

            def squares(n, c):
                if c >= 2:
                    act.wait_ge(s_acc, 6 * n + max(1, c - 2))
                nc.scalar.activation(sc[:, 4 + c % 2, :], x[:, c, :], ACT.Square).then_inc(s_sq, 1)

            def h_chunks(n, layer, what):
                sh = mcols(layer, what)
                for c in range(C):
                    act.wait_ge(s_tm, C * n + c + 1)
                    nc.scalar.activation(h_hi[:, c, :], sc[:, 4 + c % 2, :], ACT.Identity, bias=sh[:, c:c + 1]).then_inc(s_hhi, 1)

            act.wait_ge(s_cin, 32)
            act.wait_ge(s_ones, 1)
            nc.scalar.activation(ctmp[:, 0, :], cv[:, CV_C:CV_C + C], ACT.Exp, scale=-1.0).then_inc(s_csil, 1)
            nc.scalar.activation(id_b[:], ident, ACT.Copy).then_inc(s_bf, 1)
            nc.scalar.activation(mask_b[:], cc[:, CC_MASK:CC_MASK + P], ACT.Copy).then_inc(s_bf, 1)
            act.wait_ge(s_xin, 16)
            for c in range(C):
                squares(0, c)
            act.wait_ge(s_fin, 16)
            nc.scalar.activation(wf_hi[:, :, :].rearrange("p c h -> p (c h)"), wf_raw[:], ACT.Copy).then_inc(s_wf, 1)
            split_hi(0)
            rstd(sc[:, 7, :], D, 0)
            h_chunks(0, 0, "sh_m")
            for n in range(4):
                split_hi(n + 1, used=(s_tile, D_V + 4 * n) if n else None)

            z, za, ze, zl = (probs[F_AT:F_AT + HEADS, k, :] for k in range(4))
            act.wait_ge(s_fmm, 1)
            nc.scalar.activation(z, T_BANK[0][0:HEADS, :], ACT.Identity, bias=cv[0:HEADS, CV_BF:CV_BF + 1]).then_inc(s_fa, 1)
            act.wait_ge(s_fa, 1)
            nc.scalar.activation(za, z, ACT.Abs).then_inc(s_fa, 1)
            act.wait_ge(s_fa, 2)
            nc.scalar.activation(ze, za, ACT.Exp, scale=-1.0).then_inc(s_fa, 1)
            act.wait_ge(s_fa, 3)
            nc.scalar.activation(zl, ze, ACT.Ln, bias=ones[F_AT:F_AT + HEADS, 0:1]).then_inc(s_fa, 1)
            act.wait_ge(s_fd, 3)
            nc.scalar.activation(f_rows[0], za, ACT.Copy, scale=-1.0).then_inc(s_fr, 1)

            def q_hi(layer, gp, first=False):
                scale = FOX_SCALE if layer == 0 else MLA_SCALE
                act.wait_ge(s_pq, gp + 1)
                if not first:
                    act.wait_ge(s_score, 8 * gp)
                for s in range(2):
                    nc.scalar.activation(qa[s][0:HD, :], PQ[s * HD:(s + 1) * HD, :], ACT.Copy, scale=scale).then_inc(s_qhi, 1)

            def k_hi(layer, gp):
                act.wait_ge(s_pk, gp + 1)
                for s in range(2):
                    nc.scalar.activation(ka[s][0:HD, :], PK[s * HD:(s + 1) * HD, :], ACT.Copy).then_inc(s_khi, 1)

            def exps(gp, st):
                for s in range(2):
                    n = P * (st + 1)
                    act.wait_ge(s_max, 2 * (4 * gp + st) + s + 1)
                    if st >= 2:
                        act.wait_ge(s_tr, 2 * (4 * gp + st) + s - 3)
                    nc.scalar.activation(prob[st % 2][s][:, 0:n], S_BANK[st % 2][s][:, 0:n], ACT.Exp,
                                         bias=nmax[:, st % 2, s:s + 1], accum_out=rsum[:, st % 2, s:s + 1]).then_inc(s_exp, 1)

            def pt_his(gp, st):
                for s in range(2):
                    act.wait_ge(s_tr, 2 * (4 * gp + st) + s + 1)
                    nc.scalar.activation(pt(s, pt_hi, st, st + 1), T_BANK[s][:, 0:P * (st + 1)].rearrange("p (j c) -> p j c", c=P),
                                         ACT.Copy).then_inc(s_pthi, 1)

            def o_his(gp, p, banks):
                for s in range(2):
                    act.wait_ge(s_pv, 2 * gp + s + 1)
                    rows = slice(s * HD, (s + 1) * HD)
                    nc.scalar.activation(o_hi[rows, bass.ds(p, 1), :].rearrange("p a t -> p (a t)"), banks[s][rows, :], ACT.Copy).then_inc(s_ohi, 1)

            def latent_attn(p, first, more, unit):
                gp = PAIRS + p
                exps(gp, 0)
                exps(gp, 1)
                if not first:
                    o_his(gp - 1, p - 1, T_BANK)
                nc.scalar.activation(vs_hi[:], v_tok[:, :, bass.ds(P * p, P)], ACT.Copy).then_inc(s_vhi, 1)
                if more:
                    split_hi(*unit, used=(s_pq, gp + 1))
                pt_his(gp, 0)
                exps(gp, 2)
                pt_his(gp, 1)
                exps(gp, 3)
                pt_his(gp, 2)
                if more:
                    q_hi(1, gp + 1)
                    k_hi(1, gp + 1)
                pt_his(gp, 3)

            def latent_layer():
                split_hi(U_MQK + 1, MQK_W, used=(s_tile, D_MOUT))
                q_hi(1, PAIRS)
                k_hi(1, PAIRS)
                latent_attn(0, True, True, (U_MQK + 2, MQK_W))
                with act.Fori(0, 2) as i:
                    for r in range(2):
                        latent_attn(2 * i + (r + 1), False, True, (U_MQK + 2 * i + r + 3, MQK_W))
                latent_attn(5, False, True, (U_MQK + 7, MQK_W))
                latent_attn(6, False, True, (U_MOUT, UNIT))
                latent_attn(PAIRS - 1, False, False, None)
                o_his(2 * PAIRS - 1, PAIRS - 1, T_BANK)

            def attn(layer, i, r, more, unit):
                gp = PAIRS * layer + 2 * i + r
                nc.scalar.activation(vs_hi[:], v_tok[:, :, bass.ds(P * (2 * i + r), P)], ACT.Copy).then_inc(s_vhi, 1)
                exps(gp, 0)
                exps(gp, 1)
                if more:
                    split_hi(*unit, used=(s_pk, gp + 1))
                pt_his(gp, 0)
                exps(gp, 2)
                pt_his(gp, 1)
                exps(gp, 3)
                if more:
                    q_hi(layer, gp + 1)
                pt_his(gp, 2)
                pt_his(gp, 3)
                if more:
                    k_hi(layer, gp + 1)
                o_his(gp, 2 * i + r, S_BANK[1])

            def attn_layer(layer, u0, n, then):
                split_hi(u0 + 1, n, used=(s_tile, D_MOUT if layer else D_FOUT))
                q_hi(layer, PAIRS * layer, first=(layer == 0))
                k_hi(layer, PAIRS * layer)
                with act.Fori(0, 3) as i:
                    for r in range(2):
                        attn(layer, i, r, True, (u0 + 2 * i + r + 2, n))
                attn(layer, 3, 0, True, (then, UNIT))
                attn(layer, 3, 1, False, None)

            def out_proj(layer, u0, d, td):
                n = 2 * layer + 1
                for k in range(4):
                    split_hi(u0 + k + 1, used=(s_tile, d + 2 * k) if k else (s_pq if layer else s_pk, PAIRS * (layer + 1)))
                    for c in (2 * k, 2 * k + 1):
                        act.wait_ge(s_tdve, td + c + 1)
                        squares(n, c)
                rstd(sc[:, 7, :], D, n + 2 * (n > 2))
                h_chunks(n, layer, "sh_f")

            def mlp_group(layer, g, last, after_u):
                base = 32 * layer + 8 * g
                for k in range(8):
                    used = (s_tile, D_MLP[layer] + 16 * g + 2 * k)
                    if not (last and k == 7):
                        split_hi(U_MLP[layer] + 8 * g + k + 1, used=used)
                    elif after_u:
                        split_hi(*after_u, used=used)
                    if layer == 0 and last and k == 7:
                        act.wait_ge(s_trig, 8)
                        nc.scalar.activation(sin_t, adab[:, 2, :], ACT.Sin).then_inc(s_triga, 1)
                        act.wait_ge(s_trig, 12)
                        nc.scalar.activation(cos_t, adab[:, 3, :], ACT.Sin).then_inc(s_triga, 1)
                    for j in (2 * k, 2 * k + 1):
                        if k < 4:
                            act.wait_ge(s_tile, D_MLP[layer] + 16 * g + j + 1)
                            nc.scalar.activation(sc[:, j % 2, :], ps[j % RING][:], ACT.Relu).then_inc(s_tact, 1)
                            act.wait_ge(s_sqr, base + j + 1)
                            nc.scalar.activation(o_hi[:, j, :], sc[:, 2 + j % 2, :], ACT.Copy).then_inc(s_ahi, 1)
                        elif last:
                            c = j - 8
                            act.wait_ge(s_tdve, TD_MLP[layer] + 8 * g + c + 1)
                            squares(2 * layer + 2, c)

            def mlp(layer, after_u):
                with act.Fori(0, GROUPS - 1) as g:
                    mlp_group(layer, g, False, None)
                mlp_group(layer, GROUPS - 1, True, after_u)

            attn_layer(0, U_QK, UNIT, U_FOUT)
            out_proj(0, U_FOUT, D_FOUT, TD_FOUT)
            mlp(0, (U_DKV, C * 160))
            rstd(sc[:, 7, :], D, 2)
            h_chunks(2, 1, "sh_m")
            split_hi(U_DQ, used=(s_tile, D_DKV))
            ckv_raw, cq_raw, cq_n = prob[0][0], (prob[0][1], prob[1][0]), (prob[0][0], prob[1][1])
            act.wait_ge(s_tdve, TD_DKV + 1)
            nc.scalar.activation(sc[:, 4, :], ckv_raw, ACT.Square).then_inc(s_rpa, 1)
            act.wait_ge(s_kr, 3)
            nc.scalar.activation(qa[0][0:ROPE, :], sc[0:ROPE, 1, :], ACT.Copy).then_inc(s_rpa, 1)
            rstd(sc[:, 6, :], KVR, 3)
            split_hi(U_MV, D, used=(s_tile, D_DQ))
            act.wait_ge(s_rope, 1)
            nc.scalar.activation(o_hi[:, 7, :], sc[:, 5, :], ACT.Copy).then_inc(s_rpa, 1)
            act.wait_ge(s_kr, 4)
            for s in range(2):
                nc.scalar.activation(ka[s][HD:MLA_K, :], qa[0][0:ROPE, :].bitcast(F32), ACT.Copy).then_inc(s_rpa, 1)
                nc.scalar.activation(kb[s][HD:MLA_K, :], qa[1][0:ROPE, :].bitcast(F32), ACT.Copy).then_inc(s_rpa, 1)
            for k in range(2):
                act.wait_ge(s_tdve, TD_DKV + 3 + k)
                nc.scalar.activation(adab[:, 2 + k, :], cq_raw[k], ACT.Square).then_inc(s_rpa, 1)

            def v_tile(n):
                act.wait_ge(s_tile, D_MV + n + 1)
                nc.scalar.activation(v_tok[:, n // 2, (n % 2) * T:(n % 2 + 1) * T], ps[n % RING][:], ACT.Copy).then_inc(s_tdve, 1)

            v_tile(0)
            v_tile(1)
            split_hi(U_QROPE, 2 * T, used=(s_tile, D_MV))
            rstd(adab[:, 3, :], QR, 4)
            v_tile(2)
            v_tile(3)
            for k in range(2):
                act.wait_ge(s_rope, 4 + k)
                nc.scalar.activation(h_hi[:, k, :], cq_n[k], ACT.Copy).then_inc(s_rpa, 1)
            for n in range(4, 8):
                v_tile(n)
            split_hi(U_MQK, MQK_W, used=(s_tile, D_QROPE))
            for k in range(TB):
                act.wait_ge(s_qadd, k + 1)
                nc.scalar.activation(h_hi[:, 2 + k, :], rope_ab[k % 2][0], ACT.Copy, scale=MLA_SCALE).then_inc(s_rpa, 1)
            latent_layer()
            out_proj(1, U_MOUT, D_MOUT, TD_MOUT)
            mlp(1, None)
            rstd(prob[0][0], D, 6)

        @block.vector
        def _(dve):
            slot_of = [0]

            def split_lo(u, n=UNIT):
                for hf in range(2):
                    a, b = hf * (n // 2), (hf + 1) * (n // 2)
                    dve.wait_ge(s_whi, 2 * u + hf + 1)
                    nc.vector.tensor_tensor(w_lo[:, slot_of[0], a:b], w_raw[:, a:b], w_hi[:, slot_of[0], a:b].bitcast(F32),
                                            ALU.subtract).then_inc(s_wlo, 1)
                slot_of[0] ^= 1

            def ada_sum(a, idx, par, k0=0, k1=C):
                early = isinstance(a, int) and a < ADA_EARLY
                slot = ADA_SLOT[a] if early else 0
                free = ada_acc_free(a) if early else a - 1
                if k0 == 0 and free is not None:
                    dve.wait_ge(s_adamm, free)
                for k in range(k0, k1):
                    if early and k == 0:
                        dve.wait_ge(s_ast[slot], 16 * sum(ADA_SLOT[b] == slot for b in range(a + 1)))
                    elif not early and k % 4 == 0:
                        dve.wait_ge(s_ain[k // 4], 16 * (a - ADA_EARLY + 1))
                    w = ada_slots[slot][:, k * UW:(k + 1) * UW]
                    acc = adaacc[:, par, :]
                    if k == 0:
                        nc.vector.tensor_scalar(acc, w, cact[:, 0:1], None, ALU.mult).then_inc(s_astep[0], 1)
                    else:
                        dve.wait_ge(s_astep[0], 8 * idx + k)
                        nc.vector.scalar_tensor_tensor(out=acc, in0=w, scalar=cact[:, k:k + 1], in1=acc,
                                                       op0=ALU.mult, op1=ALU.add).then_inc(s_astep[0], 1)

            def ada_early(a):
                idx = ada_own(a)[1]
                ada_sum(a, idx, idx % 2)

            def ada_add(a, n=1, bank=ps[7]):
                dve.wait_ge(s_adamm, a + n)
                nc.vector.tensor_tensor(mod[:, bass.ds(2 * a, 2 * n)], bank[:, 0:2 * n], cv[:, bass.ds(CV_ADAB + 2 * a, 2 * n)],
                                        ALU.add).then_inc(s_mod, n)

            def sum_square(n, c):
                if c in (0, C - 1):
                    return
                dve.wait_ge(s_sq, C * n + c + 1)
                if c > 1:
                    dve.wait_ge(s_acc, 6 * n + c - 1)
                a = sc[:, 4, :] if c == 1 else sc[:, 6, :]
                nc.vector.tensor_tensor(sc[:, 6, :], a, sc[:, 4 + c % 2, :], ALU.add).then_inc(s_acc, 1)

            def gain_col(n, gain, layer, what, mods):
                dve.wait_ge(s_mod, mods)
                nc.vector.scalar_tensor_tensor(out=acol[:], in0=mcols(layer, what), scalar=1.0, in1=cv[:, gain:gain + C],
                                               op0=ALU.add, op1=ALU.mult).then_inc(s_acol, 1)

            def h_chunks(n, layer, what, rk):
                sh = mcols(layer, what)

                def lo(c):
                    dve.wait_ge(s_hhi, C * n + c + 1)
                    nc.vector.scalar_tensor_tensor(out=h_lo[:, c, :], in0=sc[:, 4 + c % 2, :], scalar=sh[:, c:c + 1],
                                                   in1=h_hi[:, c, :].bitcast(F32), op0=ALU.add, op1=ALU.subtract).then_inc(s_hlo, 1)

                dve.wait_ge(s_rstd, rk + 1)
                dve.wait_ge(s_acol, n + 1)
                for c in range(C):
                    if c >= 2:
                        dve.wait_ge(s_hlo, C * n + c - 1)
                    nc.vector.scalar_tensor_tensor(out=sc[:, 4 + c % 2, :], in0=x[:, c, :], scalar=acol[:, c:c + 1], in1=sc[:, 7, :],
                                                   op0=ALU.mult, op1=ALU.mult).then_inc(s_tm, 1)
                    if c >= 1:
                        lo(c - 1)
                lo(C - 1)

            dve.wait_ge(s_csil, 1)
            nc.vector.tensor_scalar(ctmp[:, 1, :], ctmp[:, 0, :], 1.0, None, ALU.add).then_inc(s_cact, 1)
            dve.wait_ge(s_cact, 1)
            nc.vector.reciprocal(ctmp[:, 2, :], ctmp[:, 1, :]).then_inc(s_cact, 1)
            dve.wait_ge(s_cact, 2)
            nc.vector.tensor_tensor(cact[:], ctmp[:, 2, :], cv[:, CV_C:CV_C + C], ALU.mult).then_inc(s_cact, 1)
            dve.wait_ge(s_cact, 3)
            for a in (0, 3):
                ada_early(a)
            for c in range(C):
                sum_square(0, c)
            ada_early(5)
            ada_add(0, 4)
            gain_col(0, CV_GMIX, 0, "sc_m", 4)
            split_lo(0)
            ada_early(7)
            dve.wait_ge(s_wf, 1)
            nc.vector.tensor_tensor(wf_lo[:, :, :].rearrange("p c h -> p (c h)"), wf_raw[:],
                                    wf_hi[:, :, :].rearrange("p c h -> p (c h)").bitcast(F32), ALU.subtract).then_inc(s_wf, 1)
            ada_add(4, 4, ps[6])
            h_chunks(0, 0, "sh_m", 0)

            for n in range(4):
                split_lo(n + 1)
                for tk in range(TB):
                    dve.wait_ge(s_tile, D_V + 4 * n + tk + 1)
                    nc.vector.tensor_copy(v_tok[:, tk, n * UW:(n + 1) * UW], ps[tk][:, 0:UW]).then_inc(s_tdve, 1)
                    a = ADA_START + 2 * n
                    if tk == 0:
                        ada_early(a + 1)
                    if tk == 2 and n:
                        ada_add(a - 2, 2)
            ada_add(ADA_EARLY - 2)

            z, za, ze, zl = (probs[F_AT:F_AT + HEADS, k, :] for k in range(4))
            dve.wait_ge(s_fa, 4)
            nc.vector.tensor_scalar(ze, z, 0.0, None, ALU.min).then_inc(s_fd, 1)
            dve.wait_ge(s_fd, 1)
            nc.vector.tensor_tensor(ze, ze, zl, ALU.subtract).then_inc(s_fd, 1)
            dve.wait_ge(s_fd, 2)
            nc.vector.tensor_tensor_scan(za, ze, ze, 0.0, ALU.add, ALU.bypass).then_inc(s_fd, 1)
            dve.wait_ge(s_fr, 1)
            nc.vector.scalar_tensor_tensor(out=f_rows[1], in0=za, scalar=-1.0, in1=f_rows[0].bitcast(F32),
                                           op0=ALU.mult, op1=ALU.subtract).then_inc(s_fr, 1)

            def q_lo(layer, gp):
                scale = FOX_SCALE if layer == 0 else MLA_SCALE
                for s in range(2):
                    dve.wait_ge(s_qhi, 2 * gp + s + 1)
                    out = qa[s][HD:P, :] if layer == 0 else qb[s][0:HD, :]
                    nc.vector.scalar_tensor_tensor(out=out, in0=PQ[s * HD:(s + 1) * HD, :], scalar=scale, in1=qa[s][0:HD, :].bitcast(F32),
                                                   op0=ALU.mult, op1=ALU.subtract).then_inc(s_qlo, 1)

            def k_lo(layer, gp):
                for s in range(2):
                    dve.wait_ge(s_khi, 2 * gp + s + 1)
                    nc.vector.tensor_tensor(kb[s][0:HD, :], PK[s * HD:(s + 1) * HD, :], ka[s][0:HD, :].bitcast(F32), ALU.subtract).then_inc(s_klo, 1)

            def maxes(gp, st):
                for s in range(2):
                    dve.wait_ge(s_score, 2 * (4 * gp + st) + s + 1)
                    nc.vector.tensor_reduce(nmax[:, st % 2, s:s + 1], S_BANK[st % 2][s][:, 0:P * (st + 1)], AXX, ALU.max,
                                            negate=True).then_inc(s_max, 1)

            def rinvs(gp, st):
                dve.wait_ge(s_exp, 2 * (4 * gp + st) + 2)
                nc.vector.reciprocal(rinv[:, st % 2, :], rsum[:, st % 2, :]).then_inc(s_rinv, 1)

            def pt_los(gp, st):
                for s in range(2):
                    dve.wait_ge(s_pthi, 2 * (4 * gp + st) + s + 1)
                    nc.vector.tensor_tensor(pt(s, pt_lo, st, st + 1), T_BANK[s][:, 0:P * (st + 1)].rearrange("p (j c) -> p j c", c=P),
                                            pt(s, pt_hi, st, st + 1).bitcast(F32), ALU.subtract).then_inc(s_ptlo, 1)

            def attn(layer, i, r, more, a):
                gp = PAIRS * layer + 2 * i + r
                maxes(gp, 0)
                maxes(gp, 1)
                rinvs(gp, 0)
                if a is not None:
                    ada_add(a - 1)
                rinvs(gp, 1)
                if a is not None:
                    ada_sum(a, a - 8, r, 0, 4)
                maxes(gp, 2)
                maxes(gp, 3)
                pt_los(gp, 0)
                rinvs(gp, 2)
                pt_los(gp, 1)
                rinvs(gp, 3)
                if more:
                    q_lo(layer, gp + 1)
                pt_los(gp, 2)
                pt_los(gp, 3)
                if a is not None:
                    ada_sum(a, a - 8, r, 4, 8)
                if more:
                    k_lo(layer, gp + 1)
                o_los(gp, 2 * i + r, S_BANK[1])

            def o_los(gp, p, banks):
                for s in range(2):
                    dve.wait_ge(s_ohi, 2 * gp + s + 1)
                    rows = slice(s * HD, (s + 1) * HD)
                    hi = o_hi[rows, bass.ds(p, 1), :].rearrange("p a t -> p (a t)").bitcast(F32)
                    lo = o_lo[rows, bass.ds(p, 1), :].rearrange("p a t -> p (a t)")
                    nc.vector.tensor_tensor(lo, banks[s][rows, :], hi, ALU.subtract).then_inc(s_olo, 1)

            def latent_attn(p, first, more):
                gp = PAIRS + p
                def norm(st):
                    rinvs(gp, st)
                    dve.wait_ge(s_rinv, 4 * gp + st + 1)
                    for s in range(2):
                        pr = prob[st % 2][s][:, 0:P * (st + 1)]
                        nc.vector.tensor_scalar(pr, pr, rinv[:, st % 2, s:s + 1], None, ALU.mult).then_inc(s_norm, 1)

                maxes(gp, 0)
                maxes(gp, 1)
                norm(0)
                norm(1)
                if not first:
                    o_los(gp - 1, p - 1, T_BANK)
                maxes(gp, 2)
                pt_los(gp, 0)
                maxes(gp, 3)
                norm(2)
                pt_los(gp, 1)
                norm(3)
                pt_los(gp, 2)
                if more:
                    q_lo(1, gp + 1)
                    k_lo(1, gp + 1)
                pt_los(gp, 3)

            def latent_layer():
                split_lo(U_MQK + 1, MQK_W)
                q_lo(1, PAIRS)
                k_lo(1, PAIRS)
                latent_attn(0, True, True)
                with dve.Fori(0, 3) as i:
                    for r in range(2):
                        latent_attn(2 * i + (r + 1), False, True)
                latent_attn(PAIRS - 1, False, False)
                o_los(2 * PAIRS - 1, PAIRS - 1, T_BANK)

            def attn_layer(layer, u0, n):
                split_lo(u0 + 1, n)
                q_lo(layer, PAIRS * layer)
                k_lo(layer, PAIRS * layer)
                a0 = ADA_START + 8 if layer == 0 else None
                with dve.Fori(0, 3) as i:
                    for r in range(2):
                        attn(layer, i, r, True, None if a0 is None else a0 + 2 * i + r)
                attn(layer, 3, 0, True, None if a0 is None else a0 + 6)
                attn(layer, 3, 1, False, None if a0 is None else a0 + 7)
                if layer == 0:
                    ada_add(a0 + 7)

            def gated_add(layer, what, j, c):
                g = mcols(layer, what)
                nc.vector.scalar_tensor_tensor(out=x[:, c, :], in0=ps[j % RING][:], scalar=g[:, c:c + 1], in1=x[:, c, :],
                                               op0=ALU.mult, op1=ALU.add).then_inc(s_tdve, 1)

            def out_proj(layer, u0, d):
                slot_of[0] = (u0 + 1) % 2
                n = 2 * layer + 1
                for k in range(4):
                    split_lo(u0 + k + 1)
                    for c in (2 * k, 2 * k + 1):
                        dve.wait_ge(s_tile, d + c + 1)
                        gated_add(layer, "g_m", c, c)
                        if c:
                            sum_square(n, c - 1)
                sum_square(n, C - 1)
                gain_col(n, CV_GMLP + C * layer, layer, "sc_f", 24 if layer == 0 else ADA_UNITS)
                h_chunks(n, layer, "sh_f", n + 2 * (n > 2))

            def mlp_group(layer, g, last, after_u):
                base = 32 * layer + 8 * g
                a = 24 + 6 * g
                for k in range(8):
                    if not (last and k == 7):
                        split_lo(U_MLP[layer] + 8 * g + k + 1)
                    elif after_u:
                        split_lo(*after_u)
                    if layer == 0 and last and k == 7:
                        trig_tables()
                    for j in (2 * k, 2 * k + 1):
                        dve.wait_ge(s_tile, D_MLP[layer] + 16 * g + j + 1) if k >= 4 else dve.wait_ge(s_tact, base + j + 1)
                        if k < 4:
                            nc.vector.tensor_tensor(sc[:, 2 + j % 2, :], sc[:, j % 2, :], sc[:, j % 2, :], ALU.mult).then_inc(s_sqr, 1)
                            dve.wait_ge(s_ahi, base + j + 1)
                            nc.vector.tensor_tensor(o_lo[:, j, :], sc[:, 2 + j % 2, :], o_hi[:, j, :].bitcast(F32), ALU.subtract).then_inc(s_alo, 1)
                        else:
                            c = j - 8
                            gated_add(layer, "g_f", j, c)
                            if last and c:
                                sum_square(2 * layer + 2, c - 1)
                        if layer == 0 and 0 < k < 7 and j % 2 == 0:
                            ada_add(a + k - 1)
                if last:
                    sum_square(2 * layer + 2, C - 1)

            def trig_tables():
                k, r = adab[:, 3, :], adab[:, 2, :]
                pi = 3.1415925
                dve.wait_ge(s_posin, 16)
                nc.vector.tensor_copy(k, adab[:, 2, :].bitcast(I32)).then_inc(s_trig, 1)
                dve.wait_ge(s_trig, 1)
                nc.vector.tensor_scalar(r, k, cc[:, CC_FREQ:CC_FREQ + 1], None, ALU.mult).then_inc(s_trig, 1)
                dve.wait_ge(s_trig, 2)
                nc.vector.tensor_scalar(k, r, INV_2PI, ROUND, ALU.mult, ALU.add).then_inc(s_trig, 1)
                dve.wait_ge(s_trig, 3)
                nc.vector.tensor_scalar(k, k, ROUND, None, ALU.subtract).then_inc(s_trig, 1)
                for n, part in enumerate(TWO_PI_PARTS):
                    dve.wait_ge(s_trig, 4 + n)
                    nc.vector.scalar_tensor_tensor(out=r, in0=k, scalar=-part, in1=r, op0=ALU.mult, op1=ALU.add).then_inc(s_trig, 1)
                dve.wait_ge(s_trig, 7)
                nc.vector.tensor_scalar(r, r, pi, -pi, ALU.min, ALU.max).then_inc(s_trig, 1)
                dve.wait_ge(s_trig, 8)
                nc.vector.tensor_scalar(k, r, 0.5 * math.pi, None, ALU.add).then_inc(s_trig, 1)
                dve.wait_ge(s_trig, 9)
                nc.vector.tensor_scalar(cos_t, k, math.pi, -2 * math.pi, ALU.is_gt, ALU.mult).then_inc(s_trig, 1)
                dve.wait_ge(s_trig, 10)
                nc.vector.tensor_tensor(k, k, cos_t, ALU.add).then_inc(s_trig, 1)
                dve.wait_ge(s_trig, 11)
                nc.vector.tensor_scalar(k, k, pi, -pi, ALU.min, ALU.max).then_inc(s_trig, 1)
                dve.wait_ge(s_triga, 1)
                nc.vector.tensor_scalar(sin_t, sin_t, cc[:, CC_SIGN:CC_SIGN + 1], None, ALU.mult).then_inc(s_trig, 1)

            def mlp(layer, after_u):
                with dve.Fori(0, GROUPS - 1) as g:
                    mlp_group(layer, g, False, None)
                mlp_group(layer, GROUPS - 1, True, after_u)

            attn_layer(0, U_QK, UNIT)
            out_proj(0, U_FOUT, D_FOUT)
            mlp(0, (U_DKV, C * 160))
            gain_col(2, CV_GMIX + C, 1, "sc_m", ADA_UNITS)
            h_chunks(2, 1, "sh_m", 2)
            split_lo(U_DQ)

            ckv_raw, cq_raw, cq_n = prob[0][0], (prob[0][1], prob[1][0]), (prob[0][0], prob[1][1])
            swap = [(m + ROPE // 2) % ROPE for m in range(ROPE)]
            krot, ksum = sc[0:ROPE, 0, :], sc[0:ROPE, 1, :]
            dve.wait_ge(s_tile, D_DKV + 1)
            nc.vector.tensor_copy(ckv_raw, ps[0][:]).then_inc(s_tdve, 1)
            dve.wait_ge(s_tile, D_DKV + 2)
            nc.vector.stream_shuffle(krot, ps[1][0:ROPE, :], swap).then_inc(s_kr, 1)
            dve.wait_ge(s_triga, 2)
            nc.vector.tensor_tensor(ksum, ps[1][0:ROPE, :], cos_t[0:ROPE, :], ALU.mult).then_inc(s_tdve, 1)
            dve.wait_ge(s_kr, 1)
            dve.wait_ge(s_trig, 13)
            nc.vector.tensor_tensor(krot, krot, sin_t[0:ROPE, :], ALU.mult).then_inc(s_kr, 1)
            dve.wait_ge(s_kr, 2)
            dve.wait_ge(s_tdve, TD_DKV + 2)
            nc.vector.tensor_tensor(ksum, ksum, krot, ALU.add).then_inc(s_kr, 1)
            dve.wait_ge(s_rstd, 4)
            nc.vector.scalar_tensor_tensor(out=sc[:, 5, :], in0=ckv_raw, scalar=cv[:, CV_GKV:CV_GKV + 1], in1=sc[:, 6, :],
                                           op0=ALU.mult, op1=ALU.mult).then_inc(s_rope, 1)
            dve.wait_ge(s_rpa, 2)
            nc.vector.tensor_tensor(qa[1][0:ROPE, :], ksum, qa[0][0:ROPE, :].bitcast(F32), ALU.subtract).then_inc(s_kr, 1)
            split_lo(U_MV, D)
            dve.wait_ge(s_rpa, 3)
            nc.vector.tensor_tensor(o_lo[:, 7, :], sc[:, 5, :], o_hi[:, 7, :].bitcast(F32), ALU.subtract).then_inc(s_rope, 1)
            for k in range(2):
                dve.wait_ge(s_tile, D_DQ + 1 + k)
                nc.vector.tensor_copy(cq_raw[k], ps[2 + k][:]).then_inc(s_tdve, 1)

            dve.wait_ge(s_rpa, 9)
            nc.vector.tensor_tensor(adab[:, 2, :], adab[:, 2, :], adab[:, 3, :], ALU.add).then_inc(s_rope, 1)
            split_lo(U_QROPE, 2 * T)
            dve.wait_ge(s_rstd, 5)
            for k in range(2):
                nc.vector.scalar_tensor_tensor(out=cq_n[k], in0=cq_raw[k], scalar=cv[:, CV_GQ + k:CV_GQ + k + 1], in1=adab[:, 3, :],
                                               op0=ALU.mult, op1=ALU.mult).then_inc(s_rope, 1)
            for k in range(2):
                dve.wait_ge(s_rpa, 10 + k)
                nc.vector.tensor_tensor(h_lo[:, k, :], cq_n[k], h_hi[:, k, :].bitcast(F32), ALU.subtract).then_inc(s_rope, 1)
            split_lo(U_MQK, MQK_W)

            def rope_lo(k):
                dve.wait_ge(s_rpa, 12 + k)
                nc.vector.scalar_tensor_tensor(out=h_lo[:, 2 + k, :], in0=rope_ab[k % 2][0], scalar=MLA_SCALE,
                                               in1=h_hi[:, 2 + k, :].bitcast(F32), op0=ALU.mult, op1=ALU.subtract).then_inc(s_qrd, 1)

            dve.wait_ge(s_tdve, TD_DKV + 12)
            for k in range(TB + 1):
                if k < TB:
                    a, b = rope_ab[k % 2]
                    if k >= 2:
                        dve.wait_ge(s_qadd, k - 1)
                    dve.wait_ge(s_tile, D_QROPE + k + 1)
                    nc.vector.stream_shuffle(b, ps[k][:], swap).then_inc(s_qra, 1)
                    if k >= 2:
                        rope_lo(k - 2)
                        dve.wait_ge(s_qrd, k - 1)
                    nc.vector.tensor_tensor(a, ps[k][:], cos_t, ALU.mult).then_inc(s_tdve, 1)
                if k:
                    a, b = rope_ab[(k - 1) % 2]
                    dve.wait_ge(s_tdve, TD_DKV + 12 + k)
                    dve.wait_ge(s_qsin, k)
                    nc.vector.tensor_tensor(a, a, b, ALU.add).then_inc(s_qadd, 1)
            rope_lo(TB - 2)
            rope_lo(TB - 1)

            latent_layer()
            out_proj(1, U_MOUT, D_MOUT)
            mlp(1, None)
            dve.wait_ge(s_rstd, 7)
            for c in range(C):
                nc.vector.scalar_tensor_tensor(out=sc[:, c, :], in0=x[:, c, :], scalar=cv[:, CV_GFIN + c:CV_GFIN + c + 1], in1=prob[0][0],
                                               op0=ALU.mult, op1=ALU.mult).then_inc(s_yn, 1)

        @block.tensor
        def _(pe):
            def product(out, lhs, rhs, start, stop):
                nc.tensor.matmul(out, lhs[0], rhs[0], start=start, stop=False)
                nc.tensor.matmul(out, lhs[1], rhs[0], start=False, stop=False)
                return nc.tensor.matmul(out, lhs[0], rhs[1], start=False, stop=stop)

            def w_view(slot, kc, n):
                return [w[:, slot, 0:kc * n].rearrange("p (k n) -> p k n", k=kc) for w in (w_hi, w_lo)]

            def w_ready(u):
                pe.wait_ge(s_wlo, 2 * u + 2)

            def bank_free(first, n, td):
                pe.wait_ge(s_tdve, td + n - 3)

            def ada_mm(a, own, idx, par, col=0, bank=ps[7]):
                pe.wait_ge(s_astep[own], ADA_STEPS[own] * (idx + 1))
                if col == 0 and not (isinstance(a, int) and a < ADA_START):
                    pe.wait_ge(s_mod, a)
                for j in range(2):
                    mm = nc.tensor.matmul(bank[:, col + j:col + j + 1], adaacc[:, 2 * own + par, j * P:(j + 1) * P], ones[:, 0:1],
                                          start=True, stop=True)
                mm.then_inc(s_adamm, 1)

            def ada_early(a, col, bank=ps[7]):
                own, idx = ada_own(a)
                ada_mm(a, own, idx, idx % 2, col, bank)

            def column_sums(src):
                nc.tensor.matmul(T_BANK[1][:], ones[:], src, start=True, stop=True).then_inc(s_ss, 1)

            def sum_over_features(n):
                pe.wait_ge(s_acc, 6 * (n + 1))
                nc.tensor.matmul(T_BANK[1][:], ones[:], sc[:, 6, :], start=True, stop=False)
                pe.wait_ge(s_sq, C * (n + 1))
                nc.tensor.matmul(T_BANK[1][:], ones[:], sc[:, 5, :], start=False, stop=True).then_inc(s_ss, 1)

            pe.wait_ge(s_ones, 1)
            for a in ADA_MM[:ADA_START]:
                col, bank = 2 * (a % 4), ps[7 - a // 4]
                if a in ADA_PE:
                    slot = ADA_SLOT[a]
                    pe.wait_ge(s_cact, 3)
                    pe.wait_ge(s_ast[slot], 16)
                    for j in range(2):
                        for k in range(C):
                            mm = nc.tensor.matmul(bank[:, col + j:col + j + 1], ada_slots[slot][:, k * UW + j * P:k * UW + (j + 1) * P],
                                                  cact[:, k:k + 1], start=k == 0, stop=k == C - 1)
                    mm.then_inc(s_adamm, 1)
                else:
                    ada_early(a, col, bank)
                if a == 3:
                    sum_over_features(0)

            for n in range(4):
                w = w_view(n % 2, C, UW)
                w_ready(U_V + n)

                def part(tk, k):
                    return product(ps[tk][:, 0:UW], [h[:, k, tk * P:(tk + 1) * P] for h in (h_hi, h_lo)],
                                   [v[:, k, :] for v in w], k == 0, k == C - 1)

                if n == 0:
                    for k in range(C):
                        pe.wait_ge(s_hlo, k + 1)
                        for tk in range(TB):
                            mm = part(tk, k)
                            if k == C - 1:
                                mm.then_inc(s_tile, 1)
                for tk in range(TB):
                    if n:
                        pe.wait_ge(s_tdve, 4 * n + tk - RING + 1)
                        for k in range(C):
                            mm = part(tk, k)
                        mm.then_inc(s_tile, 1)
                    if tk == 1 and n:
                        ada_early(ADA_START + 2 * n - 2, 0)
                        ada_early(ADA_START + 2 * n - 1, 2)
            ada_early(ADA_EARLY - 2, 0)
            pe.wait_ge(s_wf, 2)
            for k in range(C):
                mm = product(T_BANK[0][0:HEADS, :], [w[:, k, :] for w in (wf_hi, wf_lo)], [h[:, k, :] for h in (h_hi, h_lo)],
                             k == 0, k == C - 1)
            mm.then_inc(s_fmm, 1)

            def q_part(layer, slot, k0, k1):
                if layer == 0:
                    w, n, at = w_view(slot, C, UW), C, 0
                else:
                    w, n, at = w_view(slot, 3, P), 2, 0
                for k in range(k0, min(k1, n)):
                    mm = product(PQ[:], [v[:, k, at:at + P] for v in w], [h[:, k, :] for h in (h_hi, h_lo)], k == 0, k == n - 1)
                    if k == n - 1:
                        mm.then_inc(s_pq, 1)

            def k_part(layer, slot, k0, k1):
                if layer == 0:
                    for k in range(k0, k1):
                        mm = product(PK[:], [v[:, k, P:2 * P] for v in w_view(slot, C, UW)], [h[:, k, :] for h in (h_hi, h_lo)],
                                     k == 0, k == C - 1)
                        if k == C - 1:
                            mm.then_inc(s_pk, 1)
                elif k0 == 0:
                    product(PK[:], [v[:, 2, :] for v in w_view(slot, 3, P)], [o[:, 7, :] for o in (o_hi, o_lo)],
                            True, True).then_inc(s_pk, 1)

            def scores(layer, gp, st, r=0):
                rows = (P, HD + 4) if layer == 0 else (MLA_K, MLA_K)
                n = P * (st + 1)
                for s in range(2):
                    out = S_BANK[st % 2][s]
                    if st == 0:
                        pe.wait_ge(s_qlo, 2 * gp + s + 1)
                        pe.wait_ge(s_klo, 2 * gp + s + 1)
                        if layer == 0:
                            pe.wait_ge(s_qx[s], 16 * gp + 16)
                            pe.wait_ge(s_kx[s], 16 * gp + 16)
                            pe.wait_ge(s_fx[s], 32 * gp + 32)
                        else:
                            pe.wait_ge(s_qx[s], 32 * gp + (32 - 16 * PAIRS))
                    if st == 1 and layer == 0:
                        if r == 0:
                            pe.wait_ge(s_max, 8 * gp + 1)
                        else:
                            pe.wait_ge(s_olo, 2 * gp)
                    if st >= 2:
                        pe.wait_ge(s_exp, 2 * (4 * gp + st - 2) + s + 1)
                    q = [t[s][0:m, P * st:n] for t, m in zip((qa, qb), rows)]
                    k = [t[s][0:m, 0:n] for t, m in zip((ka, kb), rows)]
                    nc.tensor.matmul(out[:, 0:n], q[0], k[0], start=True, stop=False)
                    if layer == 0:
                        nc.tensor.matmul(out[:, 0:n], q[1], k[1], start=False, stop=False)
                    else:
                        nc.tensor.matmul(out[:, 0:n], q[1], k[0], start=False, stop=False)
                        nc.tensor.matmul(out[:, 0:n], q[0], k[1], start=False, stop=False)
                    nc.tensor.matmul(out[:, P * st:n], id_b[:], mask_b[:], start=False, stop=True).then_inc(s_score, 1)

            def transposes(gp, st, latent=False):
                for s in range(2):
                    pe.wait_ge(s_norm, 2 * (4 * gp + st) + s + 1)
                    if st == 0:
                        if latent:
                            pe.wait_ge(s_olo, 2 * gp + s - 1)
                    else:
                        pe.wait_ge(s_ptlo, 2 * (4 * gp + st - 1) + s + 1)
                    for j in range(st + 1):
                        mm = nc.tensor.transpose(T_BANK[s][:, P * j:P * (j + 1)], prob[st % 2][s][:, P * j:P * (j + 1)], ident)
                    mm.then_inc(s_tr, 1)

            def attend(gp, banks=S_BANK[1]):
                pe.wait_ge(s_vlo, gp + 1)
                for s in range(2):
                    pe.wait_ge(s_ptlo, 2 * (4 * gp + 3) + s + 1)
                    for j in range(TB):
                        at = s * PTH + (PTS + P) * j
                        mm = product(banks[s][:, P * j:T], [v[:, j, :] for v in (vs_hi, vs_lo)],
                                     [b[:, at:at + T - P * j] for b in (pt_hi, pt_lo)], j == 0, j == TB - 1)
                    mm.then_inc(s_pv, 1)

            def attn(layer, i, r, more, u, a):
                gp = PAIRS * layer + 2 * i + r
                slot = (r + 1) % 2
                if more:
                    w_ready(u)
                    pe.wait_ge(s_qlo, 2 * gp + 2)
                    q_part(layer, slot, 0, 4)
                scores(layer, gp, 0)
                if a is not None:
                    ada_mm(a - 1, 0, a - 9, (r + 1) % 2)
                scores(layer, gp, 1, r)
                if more:
                    q_part(layer, slot, 4, 8)
                scores(layer, gp, 2)
                scores(layer, gp, 3)
                transposes(gp, 0)
                if more:
                    if a is not None:
                        pe.wait_ge(s_mod, a)
                    pe.wait_ge(s_klo, 2 * gp + 2)
                    k_part(layer, slot, 0, 2)
                transposes(gp, 1)
                if more:
                    k_part(layer, slot, 2, 4)
                transposes(gp, 2)
                if more:
                    k_part(layer, slot, 4, 6)
                transposes(gp, 3)
                if more:
                    k_part(layer, slot, 6, 8)
                attend(gp)

            def latent_attn(p, par, first, more, u):
                gp = PAIRS + p
                scores(1, gp, 0)
                scores(1, gp, 1)
                if not first:
                    attend(gp - 1, T_BANK)
                scores(1, gp, 2)
                transposes(gp, 0, True)
                scores(1, gp, 3)
                if more:
                    w_ready(u)
                    k_part(1, (par + 1) % 2, 0, 2)
                transposes(gp, 1)
                if more:
                    q_part(1, (par + 1) % 2, 0, 2)
                transposes(gp, 2)
                transposes(gp, 3)

            def latent_layer():
                w_ready(U_MQK)
                q_part(1, 0, 0, 2)
                k_part(1, 0, 0, 2)
                pe.wait_ge(s_tdve, TD_MOUT)
                pe.wait_ge(s_rpa, 7)
                latent_attn(0, 0, True, True, U_MQK + 1)
                with pe.Fori(0, 3) as i:
                    for r in range(2):
                        latent_attn(2 * i + (r + 1), (r + 1) % 2, False, True, U_MQK + 2 * i + (r + 2))
                latent_attn(PAIRS - 1, 1, False, False, None)
                attend(2 * PAIRS - 1, T_BANK)

            def attn_layer(layer, u0):
                w_ready(u0)
                q_part(layer, 0, 0, 8)
                if layer == 0:
                    pe.wait_ge(s_mod, ADA_START + 7)
                k_part(layer, 0, 0, 8)
                if layer == 0:
                    pe.wait_ge(s_tdve, TD_FOUT)
                    pe.wait_ge(s_orow, 4)
                else:
                    pe.wait_ge(s_tdve, TD_MOUT)
                    pe.wait_ge(s_rpa, 7)
                a0 = ADA_START + 8 if layer == 0 else None
                with pe.Fori(0, 3) as i:
                    for r in range(2):
                        attn(layer, i, r, True, u0 + 2 * i + r + 1, None if a0 is None else a0 + 2 * i + r)
                attn(layer, 3, 0, True, u0 + 7, None if a0 is None else a0 + 6)
                attn(layer, 3, 1, False, None, None if a0 is None else a0 + 7)
                if layer == 0:
                    ada_mm(a0 + 7, 0, 15, 1)

            def dense_tile(bank, w, at, rhs):
                for k in range(C):
                    mm = product(bank[:], [v[:, k, at:at + P] for v in w], [t[:, k, :] for t in rhs], k == 0, k == C - 1)
                mm.then_inc(s_tile, 1)

            def dense_pair(banks, w, rhs, ready, widths=(P, P)):
                for k in range(C):
                    if ready(k) is not None:
                        pe.wait_ge(*ready(k))
                    for t, m in enumerate(widths):
                        mm = product(banks[t][0:m, :], [v[:, k, t * P:t * P + m] for v in w], [b[:, k, :] for b in rhs], k == 0, k == C - 1)
                        if k == C - 1:
                            mm.then_inc(s_tile, 1)

            def out_proj(layer, u0, td):
                for n in range(4):
                    w_ready(u0 + n)
                    if n == 0:
                        olo = HEADS * (layer + 1)
                        dense_pair(ps[0:2], w_view(0, C, UW), (o_hi, o_lo),
                                   lambda k: (s_olo, olo - 2) if k == 0 else (s_olo, olo) if k == C - 1 else None)
                        continue
                    for t in range(2):
                        c = 2 * n + t
                        if c >= RING:
                            pe.wait_ge(s_tdve, td + c - 3)
                        dense_tile(ps[c % RING], w_view(n % 2, C, UW), t * P, (o_hi, o_lo))
                sum_over_features(2 * layer + 1)

            def mlp_group(layer, g, first):
                base = 32 * layer + 8 * g
                norm = 2 * layer + 1

                def bank_free(j):
                    if j < 4:
                        pe.wait_ge(s_tdve, TD_MLP[layer] + 8 * g + j - 3)
                    elif j < 12:
                        pe.wait_ge(s_tact, base + j - 3)
                    else:
                        pe.wait_ge(s_tdve, TD_MLP[layer] + 8 * g + j - 11)

                for n in range(8):
                    w_ready(U_MLP[layer] + 8 * g + n)
                    rhs = (h_hi, h_lo) if n < 4 else (o_hi, o_lo)
                    if (n == 0 and first) or n == 4:
                        sem_, count = (s_hlo, C * norm + 1) if n == 0 else (s_alo, base + 1)
                        bank_free(2 * n)
                        bank_free(2 * n + 1)
                        dense_pair(ps[0:2], w_view(0, C, UW), rhs, lambda k: (sem_, count + k))
                    for t in range(2):
                        j = 2 * n + t
                        if not ((n == 0 and first) or n == 4):
                            bank_free(j)
                            dense_tile(ps[j % RING], w_view(n % 2, C, UW), t * P, rhs)
                        if layer == 0 and 0 < n < 7 and t == 0:
                            ada_mm(24 + 6 * g + n - 1, 1, 5 + 6 * g + n, (n + 1) % 2)

            def mlp(layer):
                mlp_group(layer, 0, True)
                with pe.Fori(1, GROUPS) as g:
                    mlp_group(layer, g, False)
                sum_over_features(2 * layer + 2)

            attn_layer(0, U_QK)
            out_proj(0, U_FOUT, TD_FOUT)
            mlp(0)

            w = w_view(0, C, KVR + ROPE)
            w_ready(U_DKV)
            pe.wait_ge(s_tdve, TD_DKV - 2)
            dense_pair(ps[0:2], w, (h_hi, h_lo), lambda k: (s_hlo, 2 * C + 1 + k), (KVR, ROPE))
            w_ready(U_DQ)
            for t in range(2):
                pe.wait_ge(s_tdve, TD_DKV - 1 + t)
                dense_tile(ps[2 + t], w_view(1, C, UW), t * P, (h_hi, h_lo))
                if t == 0:
                    pe.wait_ge(s_rpa, 1)
                    column_sums(sc[:, 4, :])
            w_ready(U_MV)
            pe.wait_ge(s_rope, 2)
            for n in range(2 * TB):
                tk, half = n // 2, n % 2
                pe.wait_ge(s_tdve, TD_DKV + n + 1)
                product(ps[n % RING][:], [o[:, 7, tk * P:(tk + 1) * P] for o in (o_hi, o_lo)],
                        [v[:, 0, half * T:(half + 1) * T] for v in w_view(0, 1, D)], True, True).then_inc(s_tile, 1)
                if n == 3:
                    pe.wait_ge(s_rope, 3)
                    column_sums(adab[:, 2, :])
            w_ready(U_QROPE)
            pe.wait_ge(s_rope, 7)
            for t in range(TB):
                pe.wait_ge(s_tdve, TD_DKV + t + 9)
                for k in range(2):
                    mm = product(ps[t][:], [v[:, k, t * P:(t + 1) * P] for v in w_view(1, 2, T)], [h[:, k, :] for h in (h_hi, h_lo)],
                                 k == 0, k == 1)
                mm.then_inc(s_tile, 1)

            latent_layer()
            out_proj(1, U_MOUT, TD_MOUT)
            mlp(1)


def columns(v):
    import numpy as np
    return np.ascontiguousarray(np.asarray(v).reshape(-1, P).T)


def units(w, n):
    import numpy as np
    k, m = w.shape
    return np.ascontiguousarray(w.reshape(k // P, P, m // n, n).transpose(2, 1, 0, 3)).reshape(m // n, P, -1)


def kernel(**inputs):
    import numpy as np
    import concourse.bacc as bacc
    from concourse.bass_utils import run_bass_kernel_spmd as run

    a = {k: np.asarray(v) for k, v in inputs.items()}
    cat = np.concatenate

    which = ("sh_m", "sc_m", "g_m", "sh_f", "sc_f", "g_f")
    spans = [(layer, which.index(w) * D) for layer, w in ADA_ORDER]
    ada = cat([units(a["ada_w"][layer][:, at:at + D], UW) for layer, at in spans])
    ada_b = cat([a["ada_b"][layer][at:at + D] for layer, at in spans])
    bf = np.zeros(P, np.float32)
    bf[:HEADS] = a["fox_b_f"][0]
    cvec = cat([columns(v) for v in (
        a["c"][0], ada_b, a["norm_mix_g"][0], a["norm_mix_g"][1], a["norm_mlp_g"][0], a["norm_mlp_g"][1],
        a["final_norm_g"], a["mla_q_norm_g"][0], a["mla_kv_norm_g"][0], bf)], axis=1)

    row = np.arange(P)
    cconst = np.zeros((P, CC_N), np.float32)
    cconst[:, CC_ID:CC_ID + P] = np.eye(P)
    cconst[:, CC_MASK:CC_MASK + P] = np.where(row[None, :] > row[:, None], NEG, 0.0)
    cconst[:, CC_FREQ] = 10000.0 ** (-(2 * (row % (ROPE // 2))).astype(np.float64) / ROPE)
    cconst[:, CC_EPS] = EPS
    cconst[:, CC_SIGN] = np.where(row % ROPE < ROPE // 2, -1.0, 1.0)

    w_in = a["fox_w_in"][0]
    q, k, v, f = (w_in[:, n * D:(n + 1) * D] for n in range(4))
    w_qk = np.concatenate([units(q, P).reshape(PAIRS, P, C, P), units(k, P).reshape(PAIRS, P, C, P)], axis=3).reshape(PAIRS, P, UNIT)
    uq = a["mla_w_uq"][0].reshape(QR, HEADS, HD + ROPE)
    ukv = a["mla_w_ukv"][0].reshape(KVR, HEADS, 2 * HD)
    uq_nope, uq_rope = uq[:, :, :HD].reshape(QR, D), uq[:, :, HD:].reshape(QR, HEADS * ROPE)
    uk, uv = ukv[:, :, :HD].reshape(KVR, D), ukv[:, :, HD:].reshape(KVR, D)
    w_mlp = []
    for layer in range(2):
        w1, w2 = a["mlp_w1"][layer], a["mlp_w2"][layer]
        for g in range(GROUPS):
            w_mlp += [units(w1[:, g * D:(g + 1) * D], UW), units(w2[g * D:(g + 1) * D], UW)]
    feeds = dict(
        xt=np.ascontiguousarray(a["x"][0].reshape(T, C, P).transpose(2, 1, 0)),
        pos=a["positions"].reshape(T),
        cvec=cvec, cconst=cconst, ada=ada,
        w_v=units(v, UW), w_qk=w_qk, w_f=units(f, HEADS)[0],
        w_fout=units(a["fox_w_out"][0], UW),
        w_dkv=units(a["mla_w_dkv"][0], KVR + ROPE), w_dq=units(a["mla_w_dq"][0], UW),
        w_mv=units(uv, D), w_qrope=units(uq_rope, T),
        w_mqk=cat([units(uq_nope, P), units(uk, P)], axis=2),
        w_mout=units(a["mla_w_out"][0], UW), w_mlp=cat(w_mlp))

    nc = bacc.Bacc("TRN2", target_bir_lowering=False, num_devices=1)
    args, arrays = {}, {}
    for name, arr in feeds.items():
        arr = np.ascontiguousarray(arr)
        arrays[name + "_dram"] = arr
        args[name] = nc.dram_tensor(name + "_dram", arr.shape, mybir.dt.from_np(arr.dtype), kind="ExternalInput").ap()
    args["yt"] = nc.dram_tensor("yt_dram", (P, C, T), F32, kind="ExternalOutput").ap()
    args["f_dram"] = nc.dram_tensor("f_rows_dram", (HEADS, 2, T), F32, kind="Internal").ap()
    trunk(nc, **args)
    r = run(nc, [arrays], core_ids=[0])
    y = r.results[0]["yt_dram"]
    return np.ascontiguousarray(y.transpose(2, 1, 0)).reshape(1, T, D)
```
